# Optimizing a Trainium2 kernel written in Bass

```python
import math
import jax, jax.numpy as jnp
from jax import lax
import numpy as np

D_MODEL = 1024
BATCH = 1
SEQ = 512
DEPTH = 1
DEC_BATCH = 1
DEC_SEQ = 1024
PAST_LEN = 128

MIX_DIM = D_MODEL
POOL_WINDOWS = (2, 4, 8, 16)
N_POOL_GROUPS = len(POOL_WINDOWS)
POOL_DIM = MIX_DIM // 2
POOL_GROUP_DIM = POOL_DIM // N_POOL_GROUPS
N_HEADS = 8
QK_NOPE_DIM = 64
QK_ROPE_DIM = 32
V_HEAD_DIM = 64
ATTN_DIM = N_HEADS * V_HEAD_DIM
Q_LORA_RANK = 384
KV_LORA_RANK = 256
ROPE_THETA = 10000.0
Q_BLOCK = 128
IN_PROJ_DIM = POOL_DIM + Q_LORA_RANK + KV_LORA_RANK + QK_ROPE_DIM
N_EXPERTS = 16
CAPACITY_FACTOR = 2
FFN_HIDDEN = 512
LN_EPS = 1e-5
RMS_EPS = 1e-6
DEEPNORM_ALPHA = (2.0 * DEPTH) ** 0.25
DEEPNORM_BETA = (8.0 * DEPTH) ** -0.25

kernel_name = "hybrid_pool_mla_expert_choice_encoder"

def _layer_norm(x, g, b):
    xf = x.astype(jnp.float32)
    mu = jnp.mean(xf, axis=-1, keepdims=True)
    var = jnp.mean(jnp.square(xf - mu), axis=-1, keepdims=True)
    y = (xf - mu) * lax.rsqrt(var + LN_EPS) * g.astype(jnp.float32) + b.astype(jnp.float32)
    return y.astype(x.dtype)

def _rms_norm(x, g):
    xf = x.astype(jnp.float32)
    y = xf * lax.rsqrt(jnp.mean(jnp.square(xf), axis=-1, keepdims=True) + RMS_EPS) * g.astype(jnp.float32)
    return y.astype(x.dtype)

def _rope(x):
    s = x.shape[1]
    inv = 1.0 / (ROPE_THETA ** (jnp.arange(0, QK_ROPE_DIM, 2, dtype=jnp.float32) / QK_ROPE_DIM))
    ang = jnp.arange(s, dtype=jnp.float32)[:, None] * inv[None, :]
    cos = jnp.cos(ang)[None, :, None, :]
    sin = jnp.sin(ang)[None, :, None, :]
    x1, x2 = jnp.split(x.astype(jnp.float32), 2, axis=-1)
    return jnp.concatenate([x1 * cos - x2 * sin, x1 * sin + x2 * cos], axis=-1).astype(x.dtype)

def _pool_mixer(u, w_pool, pool_scale):
    b, s, _ = u.shape
    ug = u.reshape(b, s, N_POOL_GROUPS, POOL_GROUP_DIM).astype(jnp.float32)
    cs = jnp.concatenate([jnp.zeros((b, 1, N_POOL_GROUPS, POOL_GROUP_DIM), jnp.float32),
                          lax.cumsum(ug, axis=1)], axis=1)
    pos = jnp.arange(s)
    outs = []
    for g, w in enumerate(POOL_WINDOWS):
        lo = jnp.clip(pos - w // 2, 0, s - 1)
        hi = jnp.clip(pos + w // 2 - 1, 0, s - 1)
        win_sum = cs[:, hi + 1, g] - cs[:, lo, g]
        cnt = (hi - lo + 1).astype(jnp.float32)[None, :, None]
        outs.append(win_sum / cnt - ug[:, :, g])
    d = jnp.stack(outs, axis=2).astype(u.dtype)
    y = jnp.einsum('bsgc,gcd->bsgd', d, w_pool)
    return y.reshape(b, s, POOL_DIM) * pool_scale

def _mla(q_lat, kv_lat, k_rope_raw, q_norm_g, w_uq, kv_norm_g, w_ukv):
    b, s, _ = q_lat.shape
    q = jnp.einsum('bsr,rf->bsf', _rms_norm(q_lat, q_norm_g), w_uq).reshape(b, s, N_HEADS, QK_NOPE_DIM + QK_ROPE_DIM)
    q_nope = q[..., :QK_NOPE_DIM]
    q_rope = _rope(q[..., QK_NOPE_DIM:])
    kv = jnp.einsum('bsr,rf->bsf', _rms_norm(kv_lat, kv_norm_g), w_ukv).reshape(b, s, N_HEADS, QK_NOPE_DIM + V_HEAD_DIM)
    k_nope = kv[..., :QK_NOPE_DIM]
    v = kv[..., QK_NOPE_DIM:]
    k_rope = _rope(k_rope_raw[:, :, None, :])[:, :, 0, :]
    scale = 1.0 / math.sqrt(QK_NOPE_DIM + QK_ROPE_DIM)
    nq = s // Q_BLOCK
    qn_blk = q_nope.reshape(b, nq, Q_BLOCK, N_HEADS, QK_NOPE_DIM).swapaxes(0, 1)
    qr_blk = q_rope.reshape(b, nq, Q_BLOCK, N_HEADS, QK_ROPE_DIM).swapaxes(0, 1)

    def block(args):
        qn, qr = args
        sc = (jnp.einsum('bqhd,bkhd->bhqk', qn, k_nope, preferred_element_type=jnp.float32)
              + jnp.einsum('bqhd,bkd->bhqk', qr, k_rope, preferred_element_type=jnp.float32)) * scale
        p = jax.nn.softmax(sc, axis=-1)
        return jnp.einsum('bhqk,bkhd->bqhd', p.astype(v.dtype), v)

    o = lax.map(block, (qn_blk, qr_blk))
    return o.swapaxes(0, 1).reshape(b, s, ATTN_DIM)

def _expert_choice_ffn(x, w_router, w_gate, w_up, w_down):
    b, s, d = x.shape
    t = b * s
    cap = max(1, (CAPACITY_FACTOR * t) // N_EXPERTS)
    xt = x.reshape(t, d)
    aff = jax.nn.softmax(jnp.einsum('td,de->te', xt, w_router, preferred_element_type=jnp.float32), axis=-1)
    gate, idx = lax.top_k(aff.T, cap)
    xe = xt[idx]
    h = jax.nn.silu(jnp.einsum('ecd,edf->ecf', xe, w_gate)) * jnp.einsum('ecd,edf->ecf', xe, w_up)
    ye = jnp.einsum('ecf,efd->ecd', h, w_down) * gate[..., None].astype(x.dtype)
    out = jnp.zeros((t, d), x.dtype).at[idx.reshape(-1)].add(ye.reshape(-1, d))
    return out.reshape(b, s, d)

def _encoder_layer(x, w_in, w_pool, pool_scale, q_norm_g, w_uq, kv_norm_g, w_ukv, w_o,
                   ln1_g, ln1_b, w_router, w_gate, w_up, w_down, ln2_g, ln2_b):
    proj = jnp.einsum('bsd,df->bsf', x, w_in)
    o1 = POOL_DIM
    o2 = o1 + Q_LORA_RANK
    o3 = o2 + KV_LORA_RANK
    pool_out = _pool_mixer(proj[..., :o1], w_pool, pool_scale)
    attn_out = _mla(proj[..., o1:o2], proj[..., o2:o3], proj[..., o3:], q_norm_g, w_uq, kv_norm_g, w_ukv)
    mix = jnp.einsum('bsm,md->bsd', jnp.concatenate([pool_out, attn_out], axis=-1), w_o)
    x = _layer_norm(DEEPNORM_ALPHA * x + mix, ln1_g, ln1_b)
    x = _layer_norm(DEEPNORM_ALPHA * x + _expert_choice_ffn(x, w_router, w_gate, w_up, w_down), ln2_g, ln2_b)
    return x

def setup_inputs(seed: int = 0) -> dict:
    key = jax.random.key(seed)
    ks = jax.random.split(key, 24)
    f32 = jnp.float32
    L = DEPTH

    def nrm(k, shape, scale):
        return jax.random.normal(k, shape, f32) * scale

    return {
        "x_prompt": jax.random.normal(ks[0], (BATCH, SEQ, D_MODEL), f32),
        "x_sample": jax.random.normal(ks[1], (DEC_BATCH, DEC_SEQ, D_MODEL), f32),
        "ln_in_g": 1.0 + nrm(ks[2], (D_MODEL,), 0.02),
        "ln_in_b": nrm(ks[3], (D_MODEL,), 0.02),
        "w_in": nrm(ks[4], (L, D_MODEL, IN_PROJ_DIM), D_MODEL ** -0.5),
        "w_pool": nrm(ks[5], (L, N_POOL_GROUPS, POOL_GROUP_DIM, POOL_GROUP_DIM), POOL_GROUP_DIM ** -0.5),
        "pool_scale": 1.0 + nrm(ks[6], (L, POOL_DIM), 0.1),
        "q_norm_g": 1.0 + nrm(ks[7], (L, Q_LORA_RANK), 0.02),
        "w_uq": nrm(ks[8], (L, Q_LORA_RANK, N_HEADS * (QK_NOPE_DIM + QK_ROPE_DIM)), Q_LORA_RANK ** -0.5),
        "kv_norm_g": 1.0 + nrm(ks[9], (L, KV_LORA_RANK), 0.02),
        "w_ukv": nrm(ks[10], (L, KV_LORA_RANK, N_HEADS * (QK_NOPE_DIM + V_HEAD_DIM)), KV_LORA_RANK ** -0.5),
        "w_o": nrm(ks[11], (L, MIX_DIM, D_MODEL), MIX_DIM ** -0.5 * DEEPNORM_BETA),
        "ln1_g": 1.0 + nrm(ks[12], (L, D_MODEL), 0.02),
        "ln1_b": nrm(ks[13], (L, D_MODEL), 0.02),
        "w_router": nrm(ks[14], (L, D_MODEL, N_EXPERTS), D_MODEL ** -0.5),
        "w_gate": nrm(ks[15], (L, N_EXPERTS, D_MODEL, FFN_HIDDEN), D_MODEL ** -0.5),
        "w_up": nrm(ks[16], (L, N_EXPERTS, D_MODEL, FFN_HIDDEN), D_MODEL ** -0.5),
        "w_down": nrm(ks[17], (L, N_EXPERTS, FFN_HIDDEN, D_MODEL), FFN_HIDDEN ** -0.5 * DEEPNORM_BETA),
        "ln2_g": 1.0 + nrm(ks[18], (L, D_MODEL), 0.02),
        "ln2_b": nrm(ks[19], (L, D_MODEL), 0.02),
    }

def _trunk(x, ln_in_g, ln_in_b, w_in, w_pool, pool_scale, q_norm_g, w_uq, kv_norm_g, w_ukv, w_o,
           ln1_g, ln1_b, w_router, w_gate, w_up, w_down, ln2_g, ln2_b):
    x = _layer_norm(x, ln_in_g, ln_in_b)
    for l in range(DEPTH):
        x = _encoder_layer(x, w_in[l], w_pool[l], pool_scale[l], q_norm_g[l], w_uq[l], kv_norm_g[l], w_ukv[l],
                           w_o[l], ln1_g[l], ln1_b[l], w_router[l], w_gate[l], w_up[l], w_down[l],
                           ln2_g[l], ln2_b[l])
    return x

def reference(x_prompt, x_sample, ln_in_g, ln_in_b, w_in, w_pool, pool_scale, q_norm_g, w_uq, kv_norm_g,
              w_ukv, w_o, ln1_g, ln1_b, w_router, w_gate, w_up, w_down, ln2_g, ln2_b):
    y_prompt = _trunk(x_prompt, ln_in_g, ln_in_b, w_in, w_pool, pool_scale, q_norm_g, w_uq, kv_norm_g, w_ukv,
                      w_o, ln1_g, ln1_b, w_router, w_gate, w_up, w_down, ln2_g, ln2_b)
    y_sample = _trunk(x_sample, ln_in_g, ln_in_b, w_in, w_pool, pool_scale, q_norm_g, w_uq, kv_norm_g, w_ukv,
                      w_o, ln1_g, ln1_b, w_router, w_gate, w_up, w_down, ln2_g, ln2_b)
    return (y_prompt, y_sample)


_drawn_inputs = setup_inputs


def setup_inputs(seed=0):
    import zlib

    import numpy as np

    out = dict(_drawn_inputs(seed))
    spreads = {}
    factors = {'ln_in_b': 2.879,
     'q_norm_g': 8.0,
     'kv_norm_g': 8.0,
     'ln2_g': 24.351,
     'ln2_b': 23.88,
     'pool_scale': 4.472,
     'ln1_g': 2.677,
     'ln1_b': 3.73}
    for name, (base, spread) in spreads.items():
        noise = np.random.default_rng([zlib.crc32(name.encode()), seed]).standard_normal(out[name].shape)
        drawn = base * np.exp(spread * noise) if base else spread * noise
        out[name] = __import__('jax').numpy.asarray(drawn.astype(out[name].dtype))
    for name, factor in factors.items():
        out[name] = (out[name] * factor).astype(out[name].dtype)
    return out
```

```python
from contextlib import ExitStack

import concourse.bass as bass
from concourse import mybir
import numpy as np

F32, F32R, U32, I32 = mybir.dt.float32, mybir.dt.float32r, mybir.dt.uint32, mybir.dt.int32
ALU, ACT, AX = mybir.AluOpType, mybir.ActivationFunctionType, mybir.AxisListType

P = 128
D = 1024
S_SAMPLE, S_PROMPT = 1024, 512
T = S_SAMPLE + S_PROMPT
N_TILES = T // P
SAMPLE_TILES = S_SAMPLE // P
POOL_WINDOWS = (2, 4, 8, 16)
POOL_DIM, GROUP = 512, 128
N_HEADS, NOPE, ROPE, V_DIM = 8, 64, 32, 64
QK = NOPE + ROPE
Q_RANK, KV_RANK = 384, 256
IN_DIM = POOL_DIM + Q_RANK + KV_RANK + ROPE
N_EXPERTS, FFN = 16, 512
CAP_SAMPLE, CAP_PROMPT = 2 * S_SAMPLE // N_EXPERTS, 2 * S_PROMPT // N_EXPERTS
LN_EPS, RMS_EPS = 1e-5, 1e-6
ALPHA = 2.0 ** 0.25
SCALE = 1.0 / float(np.sqrt(QK))
KD = D // P
QT_, KVT_ = Q_RANK // P, KV_RANK // P



class Scope:

    def __init__(self, nc, ctx):
        self.nc, self.ctx, self.sems = nc, ctx, []

    def sb(self, name, shape, dt=F32):
        return self.ctx.enter_context(self.nc.sbuf_tensor(name, shape, dt))

    def ps(self, name, shape=(P, 512)):
        return self.ctx.enter_context(self.nc.psum_tensor(name, list(shape), F32))

    def sem(self, name):
        self.sems.append(self.ctx.enter_context(self.nc.semaphore(name)))
        return self.sems[-1]

    def clear_semaphores(self):
        numbers = sorted(s.num for s in self.sems)
        with self.nc.Block() as block:
            @block.gpsimd
            def _(pool):
                start = numbers[0]
                for n, after in zip(numbers, numbers[1:] + [None]):
                    if after != n + 1:
                        pool.sem_clear(range(start, n + 1))
                        start = after


def three_passes(nc, out, a_hi, a_lo, b_hi, b_lo, first, last):
    nc.tensor.matmul(out, a_hi, b_hi, start=first, stop=False)
    nc.tensor.matmul(out, a_hi, b_lo, start=False, stop=False)
    return nc.tensor.matmul(out, a_lo, b_hi, start=False, stop=last)


def wait_carrier(nc, cell):
    nc.vector.memset(cell[:, :], 0.0)


def f32(ap):
    return ap.bitcast(F32)


def phase_project(nc, ident, dram):
    with ExitStack() as ctx:
        m = Scope(nc, ctx)
        x_in = m.sb("x_in", [P, 2, D])
        x0 = m.sb("x0", [P, 2, D])
        ln_g, ln_b = m.sb("ln_in_g_all", [P, D]), m.sb("ln_in_b_all", [P, D])
        x0T_hi = [m.sb(f"x0T_hi{s}", [P, KD, 2 * P], F32R) for s in range(2)]
        x0T_lo = [m.sb(f"x0T_lo{s}", [P, KD, 2 * P], F32R) for s in range(2)]
        RING = 5
        w_raw = m.sb("w_in_raw", [P, RING, IN_DIM])
        w_hi, w_lo = m.sb("w_in_hi", [P, KD, IN_DIM], F32R), m.sb("w_in_lo", [P, KD, IN_DIM], F32R)
        wv_hi, wv_lo = m.sb("w_v_hi", [P, KVT_, 512], F32R), m.sb("w_v_lo", [P, KVT_, 512], F32R)
        stats, moments = m.sb("ln_stats", [P, 2, 2, 6]), m.sb("ln_moments", [P, 2, 2])
        rstd = m.sb("ln_rstd", [P, 2])
        half_neg = m.sb("minus_half", [P, 2])
        eps = m.sb("eps_ln_rms_rms", [P, 3])
        carrier = m.sb("wait_carrier", [P, 1])
        squares = m.sb("squares_unused", [P, Q_RANK])
        mean_sq, rms = m.sb("lat_mean_sq", [P, 2, 2]), m.sb("lat_rms", [P, 2, 2])
        lat = m.sb("lat_scaled", [P, 2, Q_RANK + KV_RANK])
        rope_cos, rope_sin = m.sb("rope_cos", [P, SAMPLE_TILES, ROPE]), m.sb("rope_sin", [P, SAMPLE_TILES, ROPE])
        kr_cos, kr_sin = m.sb("kr_cos", [P, 2, ROPE]), m.sb("kr_sin", [P, 2, ROPE])
        k_rope = m.sb("k_rope_twice", [P, 2, P])
        q_g, kv_g = m.sb("q_norm_gain", [P, QT_]), m.sb("kv_norm_gain", [P, KVT_])
        qT, kvT = m.sb("qT", [P, QT_, 2 * P]), m.sb("kvT", [P, KVT_, 2 * P])
        kvT_hi, kvT_lo = m.sb("kvT_hi", [P, 2, KVT_, P], F32R), m.sb("kvT_lo", [P, 2, KVT_, P], F32R)
        krT = m.sb("krT", [P, 2 * P])
        uT = m.sb("uT", [P, 4, 2 * P])
        v_out = m.sb("v_out", [P, 2, 512])

        ps_tr = [m.ps(f"ps_transpose{b}") for b in range(2)]
        ps_lat = [m.ps(f"ps_lat{b}") for b in range(2)]
        ps_u = [m.ps(f"ps_u{b}") for b in range(2)]
        ps_qr, ps_kv = m.ps("ps_latT_q_rope"), m.ps("ps_latT_kv")

        x_loaded = [m.sem(f"a_x_loaded{s}") for s in range(2)]
        consts_loaded, ln_loaded = m.sem("a_consts_loaded"), m.sem("a_ln_loaded")
        w_loaded = [m.sem(f"a_w_loaded{s}") for s in range(RING)]
        w_hi_done, w_lo_done = m.sem("a_w_hi_done"), m.sem("a_w_lo_done")
        stats_part, stats_done = m.sem("a_stats_part"), m.sem("a_stats_done")
        eps_added, rstd_done = m.sem("a_eps_added"), m.sem("a_rstd_done")
        x_centred, x_scaled, x0_done = m.sem("a_x_centred"), m.sem("a_x_scaled"), m.sem("a_x0_done")
        x0_stored = [m.sem(f"a_x0_stored{s}") for s in range(2)]
        tr_done, tr_hi_done, tr_lo_done = m.sem("a_tr_done"), m.sem("a_tr_hi_done"), m.sem("a_tr_lo_done")
        lat_done, sq_done, rms_eps, rms_done = m.sem("a_lat_done"), m.sem("a_sq_done"), m.sem("a_rms_eps"), m.sem("a_rms_done")
        lat_scaled, kr_products = m.sem("a_lat_scaled"), m.sem("a_kr_products")
        u_done, u_copied, u_stored = m.sem("a_u_done"), m.sem("a_u_copied"), m.sem("a_u_stored")
        latT_done, latT_scaled = m.sem("a_latT_done"), m.sem("a_latT_scaled")
        kr_copied, kv_hi_done, kv_lo_done = m.sem("a_kr_copied"), m.sem("a_kv_hi_done"), m.sem("a_kv_lo_done")
        v_done, v_copied = m.sem("a_v_done"), m.sem("a_v_copied")
        v_stored = [m.sem(f"a_v_stored{s}") for s in range(2)]
        q_stored, kv_stored, kr_stored = m.sem("a_q_stored"), m.sem("a_kv_stored"), m.sem("a_kr_stored")
        filled = m.sem("a_filled")

        N_BLOCKS = N_TILES // 2
        PAIRS = N_BLOCKS // 2
        X0T_AFTER = (3, 6)
        SPLIT = Q_RANK

        ctx.callback(m.clear_semaphores)
        block = ctx.enter_context(nc.Block())

        @block.sync
        def _(sp):
            def load_x(rows, s):
                sp.dma_start(x_in[:, s, :], rows).then_inc(x_loaded[s], 16)

            for s in range(2):
                load_x(dram["x_sample"][s * P:(s + 1) * P, :], s)
            w_ukv_v = dram["w_ukv"].rearrange("(t p) (h c) -> t p h c", p=P, c=NOPE + V_DIM)

            def load_w(c):
                if c >= RING:
                    sp.wait_ge(w_lo_done, c - RING + 1)
                if c < KD:
                    sp.dma_start(w_raw[:, c % RING, :], dram["w_in"][c * P:(c + 1) * P, :]).then_inc(w_loaded[c % RING], 16)
                else:
                    dst = w_raw[:, c % RING, 0:512].rearrange("p (h v) -> p h v", v=V_DIM)
                    sp.dma_start(dst, w_ukv_v[c - KD][:, :, NOPE:]).then_inc(w_loaded[c % RING], 16)

            for dst, name in ((ln_g, "ln_in_g"), (ln_b, "ln_in_b")):
                sp.dma_start(dst[:, :], dram[name].partition_broadcast(P)).then_inc(ln_loaded, 16)
            for c in range(RING):
                load_w(c)
            sp.dma_start(rope_cos[:, :, :], dram["rope_cos"]).then_inc(consts_loaded, 16)
            sp.dma_start(rope_sin[:, :, :], dram["rope_sin"]).then_inc(consts_loaded, 16)
            with nc.allow_non_contiguous_dma("a gain per partition, once"):
                sp.dma_start(q_g[:, :], dram["q_norm_g"].rearrange("(t p) -> p t", p=P)).then_inc(consts_loaded, 16)
                sp.dma_start(kv_g[:, :], dram["kv_norm_g"].rearrange("(t p) -> p t", p=P)).then_inc(consts_loaded, 16)
            for c in range(RING, KD + KVT_):
                load_w(c)

            def step(i, last=False):
                for b in range(2):
                    j = 2 * i + b
                    if not (last and b == 1):
                        for s in range(2):
                            sp.wait_ge(x_centred, 2 * j + s + 1)
                            if last:
                                rows = dram["x_prompt"][(2 + s) * P:(3 + s) * P, :]
                            else:
                                rows = None
                            yield ("x", j, s, rows, b)
                    for s in range(2):
                        sp.wait_ge(x0_done, 2 * j + s + 1)
                        sp.dma_start(dram["x0"][bass.ds((2 * j + s) * P, P), :], x0[:, s, :]).then_inc(x0_stored[s], 16)
                    cols = bass.ds(j * 2 * P, 2 * P)
                    sp.wait_ge(u_copied, 2 * j + 2)
                    sp.dma_start(dram["uT"].rearrange("(g p) t -> p g t", p=P)[:, :, cols], uT[:, :, :]).then_inc(u_stored, 16)
                    sp.wait_ge(latT_scaled, 4 * j + 4)
                    sp.dma_start(dram["qT"].rearrange("(g p) t -> p g t", p=P)[:, :, cols], qT[:, :, :]).then_inc(q_stored, 16)
                    sp.dma_start(dram["kvT"].rearrange("(g p) t -> p g t", p=P)[:, :, cols], kvT[:, :, :]).then_inc(kv_stored, 16)
                    sp.wait_ge(kr_copied, 2 * j + 2)
                    sp.dma_start(dram["krT"][:, cols], krT[:, :]).then_inc(kr_stored, 16)
                    for s in range(2):
                        sp.wait_ge(v_copied, 2 * j + s + 1)
                        sp.dma_start(dram["v"][bass.ds((2 * j + s) * P, P), :], v_out[:, s, :]).then_inc(v_stored[s], 16)

            with sp.Fori(0, PAIRS - 2) as i:
                for _, j, s, _, _ in step(i):
                    load_x(dram["x_sample"][bass.ds((2 * j + 2 + s) * P, P), :], s)
            for i in range(PAIRS - 2, PAIRS):
                for _, j, s, rows, b in step(i, last=(i == PAIRS - 1)):
                    t = 2 * j + 2 + s
                    src = dram["x_sample"][t * P:(t + 1) * P, :] if t < SAMPLE_TILES else \
                        dram["x_prompt"][(t - SAMPLE_TILES) * P:(t - SAMPLE_TILES + 1) * P, :]
                    load_x(src, s)
            for s in range(2):
                sp.wait_ge(x0_stored[s], 16 * N_BLOCKS)
                sp.wait_ge(v_stored[s], 16 * N_BLOCKS)
            for sem in (u_stored, q_stored, kv_stored, kr_stored):
                sp.wait_ge(sem, 16 * N_BLOCKS)

        @block.gpsimd
        def _(pool):
            pool.memset(half_neg[:, :], -0.5).then_inc(filled, 1)
            pool.memset(eps[:, 0:1], LN_EPS).then_inc(filled, 1)
            pool.memset(eps[:, 1:3], RMS_EPS).then_inc(filled, 1)
            pool.memset(k_rope[:, :, :], 0.0).then_inc(filled, 1)

            def reciprocal_std(j, s):
                pool.wait_ge(stats_done, 2 * j + s + 1)
                pool.tensor_tensor(rstd[:, s:s + 1], moments[:, s, 1:2], eps[:, 0:1], ALU.add).then_inc(eps_added, 1)
                pool.wait_ge(eps_added, 2 * j + s + 1)
                pool.tensor_tensor(rstd[:, s:s + 1], rstd[:, s:s + 1], half_neg[:, 0:1], ALU.pow).then_inc(rstd_done, 1)

            def add_bias(j, s):
                pool.wait_ge(x_scaled, 2 * j + s + 1)
                pool.tensor_tensor(x0[:, s, :], x0[:, s, :], ln_b[:, :], ALU.add).then_inc(x0_done, 1)

            def latent_rms(j, s):
                pool.wait_ge(sq_done, 2 * (2 * j + s + 1))
                pool.tensor_tensor(rms[:, s, :], mean_sq[:, s, :], eps[:, 1:3], ALU.add).then_inc(rms_eps, 1)
                pool.wait_ge(rms_eps, 2 * j + s + 1)
                pool.tensor_tensor(rms[:, s, :], rms[:, s, :], half_neg[:, :], ALU.pow).then_inc(rms_done, 1)

            pool.wait_ge(filled, 4)
            for s in range(2):
                reciprocal_std(0, s)
            pool.wait_ge(ln_loaded, 32)
            for s in range(2):
                add_bias(0, s)

            def step(i, last=False):
                for b in range(2):
                    j = 2 * i + b
                    more = not (last and b == 1)
                    if more:
                        reciprocal_std(j + 1, 0)
                        reciprocal_std(j + 1, 1)
                    latent_rms(j, 0)
                    if more:
                        add_bias(j + 1, 0)
                        add_bias(j + 1, 1)
                    latent_rms(j, 1)

            with pool.Fori(0, PAIRS - 1) as i:
                step(i)
            step(PAIRS - 1, last=True)

        @block.scalar
        def _(act):
            def round_x0T(j, s, slot):
                for h in range(2):
                    act.wait_ge(tr_done, 2 * (2 * j + s) + h + 1)
                    act.activation(x0T_hi[slot][:, 4 * h:4 * h + 4, s * P:(s + 1) * P],
                                   ps_tr[h][:, :].rearrange("p (k t) -> p k t", t=P), ACT.Copy).then_inc(tr_hi_done, 1)

            for c in range(KD + KVT_):
                act.wait_ge(w_loaded[c % RING], 16 * (c // RING + 1))
                if c < KD:
                    act.activation(w_hi[:, c, :], w_raw[:, c % RING, :], ACT.Copy).then_inc(w_hi_done, 1)
                else:
                    act.activation(wv_hi[:, c - KD, :], w_raw[:, c % RING, 0:512], ACT.Copy).then_inc(w_hi_done, 1)
                if c in X0T_AFTER:
                    round_x0T(0, X0T_AFTER.index(c), 0)

            def square(j, s):
                act.wait_ge(lat_done, 2 * (2 * j + s) + 1)
                act.wait_ge(sq_done, 2 * (2 * j + s))
                act.activation(squares[:, :], ps_lat[0][:, 0:Q_RANK], ACT.Square, scale=Q_RANK ** -0.5,
                               accum_out=mean_sq[:, s, 0:1]).then_inc(sq_done, 1)
                act.wait_ge(lat_done, 2 * (2 * j + s) + 2)
                act.wait_ge(sq_done, 2 * (2 * j + s) + 1)
                act.activation(squares[:, 0:KV_RANK], ps_lat[1][:, 0:KV_RANK], ACT.Square, scale=KV_RANK ** -0.5,
                               accum_out=mean_sq[:, s, 1:2]).then_inc(sq_done, 1)

            def copy_u(j, h):
                act.wait_ge(u_done, 2 * j + h + 1)
                act.wait_ge(u_stored, 16 * j)
                act.activation(uT[:, 2 * h:2 * h + 2, :], ps_u[h][:, :].rearrange("p (g t) -> p g t", g=2),
                               ACT.Copy).then_inc(u_copied, 1)

            def copy_latT(j, s):
                act.wait_ge(latT_scaled, 2 * (2 * j + s) + 2)
                act.activation(kvT_hi[:, s, :, :], kvT[:, :, s * P:(s + 1) * P], ACT.Copy).then_inc(kv_hi_done, 1)
                act.wait_ge(kr_stored, 16 * j)
                act.activation(krT[:, s * P:(s + 1) * P], ps_qr[:, Q_RANK:Q_RANK + P], ACT.Copy).then_inc(kr_copied, 1)

            def copy_v(j, s):
                act.wait_ge(v_done, 2 * j + s + 1)
                act.wait_ge(v_stored[s], 16 * j)
                act.activation(v_out[:, s, :], ps_lat[s][:, :], ACT.Copy).then_inc(v_copied, 1)

            def step(i, last=False):
                for b in range(2):
                    j = 2 * i + b
                    for s in range(2):
                        square(j, s)
                        copy_u(j, s)
                        copy_latT(j, s)
                        if not (last and b == 1):
                            round_x0T(j + 1, s, 1 - b)
                    for s in range(2):
                        copy_v(j, s)

            with act.Fori(0, PAIRS - 1) as i:
                step(i)
            step(PAIRS - 1, last=True)

        @block.vector
        def _(dve):
            def statistics(j, s):
                dve.wait_ge(x_loaded[s], 16 * (j + 1))
                if not (isinstance(j, int) and j == 0):
                    dve.wait_ge(eps_added, 2 * j + s - 1)
                    dve.wait_ge(x_centred, 2 * j + s - 1)
                for h in range(2):
                    nc.vector.bn_stats(stats[:, s, h, :], x_in[:, s, h * 512:(h + 1) * 512]).then_inc(stats_part, 1)
                dve.wait_ge(stats_part, 2 * (2 * j + s) + 2)
                wait_carrier(nc, carrier)
                nc.vector.bn_aggr(moments[:, s, :], stats[:, s, :, :].rearrange("p h c -> p (h c)")).then_inc(stats_done, 1)

            def normalise(j, s):
                dve.wait_ge(rstd_done, 2 * j + s + 1)
                if not (isinstance(j, int) and j == 0):
                    dve.wait_ge(tr_done, 2 * (2 * j + s - 1))
                    dve.wait_ge(x0_stored[s], 16 * j)
                nc.vector.tensor_scalar(x0[:, s, :], x_in[:, s, :], moments[:, s, 0:1], rstd[:, s:s + 1],
                                        ALU.subtract, ALU.mult).then_inc(x_centred, 1)
                dve.wait_ge(x_centred, 2 * j + s + 1)
                nc.vector.tensor_tensor(x0[:, s, :], x0[:, s, :], ln_g[:, :], ALU.mult).then_inc(x_scaled, 1)

            def rest_x0T(j, s, slot):
                for h in range(2):
                    dve.wait_ge(tr_hi_done, 2 * (2 * j + s) + h + 1)
                    hi = x0T_hi[slot][:, 4 * h:4 * h + 4, s * P:(s + 1) * P]
                    nc.vector.tensor_tensor(x0T_lo[slot][:, 4 * h:4 * h + 4, s * P:(s + 1) * P],
                                            ps_tr[h][:, :].rearrange("p (k t) -> p k t", t=P), f32(hi),
                                            ALU.subtract).then_inc(tr_lo_done, 1)

            def scale_latents(j, s, position):
                dve.wait_ge(rms_done, 2 * j + s + 1)
                t = 2 * j + s
                nc.vector.tensor_scalar(lat[:, s, 0:Q_RANK], ps_lat[0][:, 0:Q_RANK], rms[:, s, 0:1], None,
                                        ALU.mult).then_inc(lat_scaled, 1)
                nc.vector.tensor_scalar(lat[:, s, Q_RANK:], ps_lat[1][:, 0:KV_RANK], rms[:, s, 1:2], None,
                                        ALU.mult).then_inc(lat_scaled, 1)
                raw = ps_lat[1][:, KV_RANK:KV_RANK + ROPE]
                cos = rope_cos[:, bass.ds(position, 1), :].rearrange("p a c -> p (a c)")
                sin = rope_sin[:, bass.ds(position, 1), :].rearrange("p a c -> p (a c)")
                nc.vector.tensor_tensor(kr_cos[:, s, :], raw, cos, ALU.mult).then_inc(kr_products, 1)
                nc.vector.tensor_tensor(kr_sin[:, s, :], raw, sin, ALU.mult).then_inc(kr_products, 1)
                dve.wait_ge(kr_products, 2 * t + 2)
                half = ROPE // 2
                both = k_rope[:, s, :].rearrange("p (d c) -> p d c", d=2)
                for h in range(2):
                    a = kr_cos[:, s:s + 1, h * half:(h + 1) * half].to_broadcast([P, 2, half])
                    b = kr_sin[:, s:s + 1, (1 - h) * half:(2 - h) * half].to_broadcast([P, 2, half])
                    nc.vector.tensor_tensor(both[:, :, h * half:(h + 1) * half], a, b, ALU.add).then_inc(lat_scaled, 1)

            def scale_latT(j, s):
                t = 2 * j + s
                dve.wait_ge(latT_done, t + 1)
                dve.wait_ge(q_stored, 16 * j)
                dve.wait_ge(kv_stored, 16 * j)
                nc.vector.tensor_tensor(qT[:, :, s * P:(s + 1) * P], ps_qr[:, 0:Q_RANK].rearrange("p (k t) -> p k t", t=P),
                                        q_g[:, :].unsqueeze(2).to_broadcast([P, QT_, P]), ALU.mult).then_inc(latT_scaled, 1)
                nc.vector.tensor_tensor(kvT[:, :, s * P:(s + 1) * P], ps_kv[:, 0:KV_RANK].rearrange("p (k t) -> p k t", t=P),
                                        kv_g[:, :].unsqueeze(2).to_broadcast([P, KVT_, P]), ALU.mult).then_inc(latT_scaled, 1)
                dve.wait_ge(kv_hi_done, t + 1)
                nc.vector.tensor_tensor(kvT_lo[:, s, :, :], kvT[:, :, s * P:(s + 1) * P], f32(kvT_hi[:, s, :, :]),
                                        ALU.subtract).then_inc(kv_lo_done, 1)

            for s in range(2):
                statistics(0, s)
            dve.wait_ge(filled, 4)
            dve.wait_ge(ln_loaded, 32)
            for s in range(2):
                normalise(0, s)
            for c in range(KD + KVT_):
                dve.wait_ge(w_hi_done, c + 1)
                if c < KD:
                    nc.vector.tensor_tensor(w_lo[:, c, :], w_raw[:, c % RING, :], f32(w_hi[:, c, :]),
                                            ALU.subtract).then_inc(w_lo_done, 1)
                else:
                    nc.vector.tensor_tensor(wv_lo[:, c - KD, :], w_raw[:, c % RING, 0:512], f32(wv_hi[:, c - KD, :]),
                                            ALU.subtract).then_inc(w_lo_done, 1)
                if c in X0T_AFTER:
                    rest_x0T(0, X0T_AFTER.index(c), 0)
            dve.wait_ge(consts_loaded, 64)

            def step(i, positions, last=False):
                for b in range(2):
                    j = 2 * i + b
                    more = not (last and b == 1)
                    if more:
                        statistics(j + 1, 0)
                        statistics(j + 1, 1)
                        normalise(j + 1, 0)
                    scale_latents(j, 0, positions + 2 * b)
                    if more:
                        normalise(j + 1, 1)
                    for s in range(2):
                        if s:
                            scale_latents(j, 1, positions + 2 * b + 1)
                        scale_latT(j, s)
                        if more:
                            rest_x0T(j + 1, s, 1 - b)

            with dve.Fori(0, PAIRS - 1) as i:
                step(i, 4 * i)
            step(PAIRS - 1, 0, last=True)

        @block.tensor
        def _(pe):
            def transpose_x0(j, s):
                pe.wait_ge(x0_done, 2 * j + s + 1)
                for h in range(2):
                    t = 2 * j + s
                    if not (isinstance(t, int) and t == 0):
                        pe.wait_ge(tr_lo_done, 2 * t + h - 1)
                    for k in range(4):
                        last = nc.tensor.transpose(ps_tr[h][:, k * P:(k + 1) * P],
                                                   x0[:, s, (4 * h + k) * P:(4 * h + k + 1) * P], ident[:, :])
                    last.then_inc(tr_done, 1)

            def latents(j, s, slot):
                t = 2 * j + s
                pe.wait_ge(tr_lo_done, 4 * j + 2 * s + 2)
                pe.wait_ge(lat_scaled, 4 * t)
                pe.wait_ge(kr_products, 2 * t)
                for h, (c0, c1) in enumerate(((POOL_DIM, POOL_DIM + SPLIT), (POOL_DIM + SPLIT, IN_DIM))):
                    if s == 0 and not (isinstance(j, int) and j == 0):
                        pe.wait_ge(v_copied, 2 * j - 1 + h)
                    for k in range(KD):
                        if isinstance(t, int) and t == 0 and h == 0:
                            pe.wait_ge(w_lo_done, k + 1)
                        a_hi, a_lo = (x[slot][:, k, s * P:(s + 1) * P] for x in (x0T_hi, x0T_lo))
                        last = three_passes(nc, ps_lat[h][:, 0:c1 - c0], a_hi, a_lo,
                                            w_hi[:, k, c0:c1], w_lo[:, k, c0:c1], k == 0, k == KD - 1)
                    last.then_inc(lat_done, 1)

            def pool_inputs(j, h, slot):
                pe.wait_ge(u_copied, 2 * j)
                for g in range(2):
                    c0 = (2 * h + g) * P
                    for k in range(KD):
                        last = three_passes(nc, ps_u[h][:, g * 2 * P:(g + 1) * 2 * P],
                                            w_hi[:, k, c0:c0 + P], w_lo[:, k, c0:c0 + P],
                                            x0T_hi[slot][:, k, :], x0T_lo[slot][:, k, :], k == 0, k == KD - 1)
                last.then_inc(u_done, 1)

            def transpose_latents(j, s):
                t = 2 * j + s
                pe.wait_ge(lat_scaled, 4 * t + 4)
                if not (isinstance(t, int) and t == 0):
                    pe.wait_ge(kr_copied, t)
                    pe.wait_ge(latT_scaled, 2 * t)
                for k in range(QT_):
                    nc.tensor.transpose(ps_qr[:, k * P:(k + 1) * P], lat[:, s, k * P:(k + 1) * P], ident[:, :])
                nc.tensor.transpose(ps_qr[:, Q_RANK:Q_RANK + P], k_rope[:, s, :], ident[:, :])
                for k in range(KVT_):
                    last = nc.tensor.transpose(ps_kv[:, k * P:(k + 1) * P],
                                               lat[:, s, Q_RANK + k * P:Q_RANK + (k + 1) * P], ident[:, :])
                last.then_inc(latT_done, 1)

            def values(j, s):
                if isinstance(j, int) or s == 0:
                    pe.wait_ge(w_lo_done, KD + KVT_)
                pe.wait_ge(kv_lo_done, 2 * j + s + 1)
                for k in range(KVT_):
                    last = three_passes(nc, ps_lat[s][:, :], kvT_hi[:, s, k, :], kvT_lo[:, s, k, :],
                                        wv_hi[:, k, :], wv_lo[:, k, :], k == 0, k == KVT_ - 1)
                last.then_inc(v_done, 1)

            for s in range(2):
                transpose_x0(0, s)
            latents(0, 0, 0)

            def step(i, last=False):
                for b in range(2):
                    j = 2 * i + b
                    more = not (last and b == 1)
                    pe.wait_ge(tr_lo_done, 4 * j + 4)
                    pool_inputs(j, 0, b)
                    transpose_latents(j, 0)
                    if more:
                        transpose_x0(j + 1, 0)
                    latents(j, 1, b)
                    pool_inputs(j, 1, b)
                    transpose_latents(j, 1)
                    if more:
                        transpose_x0(j + 1, 1)
                    for s in range(2):
                        values(j, s)
                    if more:
                        latents(j + 1, 0, 1 - b)

            with pe.Fori(0, PAIRS - 1) as i:
                step(i)
            step(PAIRS - 1, last=True)


def phase_attention(nc, ident, dram):
    with ExitStack() as ctx:
        m = Scope(nc, ctx)
        BLK = 512
        PAIRS, BLOCKS, TILES, UNITS = N_HEADS // 2, 6, 24, 12
        halves = []
        for n in range(TILES):
            halves += [(n, h) for h in range(2 if (n // 4) % 3 < 2 else 1)]
        HALVES = len(halves)
        first_half = [halves.index((n, 0)) for n in range(TILES)] + [HALVES]

        def keys(n):
            return (0, S_SAMPLE // P) if (n // 4) % 3 < 2 else (S_SAMPLE, S_PROMPT // P)

        qn_hi, qn_lo = m.sb("qn_hi", [P, QT_, T], F32R), m.sb("qn_lo", [P, QT_, T], F32R)
        kvn_hi, kvn_lo = m.sb("kvn_hi", [P, KVT_, T], F32R), m.sb("kvn_lo", [P, KVT_, T], F32R)
        k_hi, k_lo = m.sb("k_hi", [P, 2, T], F32R), m.sb("k_lo", [P, 2, T], F32R)
        q_hi, q_lo = m.sb("q_hi", [P, 2, BLK], F32R), m.sb("q_lo", [P, 2, BLK], F32R)
        q_table, q_work, q_moved = m.sb("q_table", [P, S_SAMPLE]), m.sb("q_work", [P, BLK]), m.sb("q_moved", [ROPE, BLK])
        v_parts = m.sb("v_hi_lo", [P, N_TILES, 2, 2, V_DIM], F32R)
        v_raw = m.sb("v_raw", [P, N_TILES, 2, V_DIM])
        probs = m.sb("probs", [P, 2, S_SAMPLE])
        pT_hi = [m.sb(f"pT_hi{s}", [P, 8, 2 * P], F32R) for s in range(2)]
        pT_lo = [m.sb(f"pT_lo{s}", [P, 8, 2 * P], F32R) for s in range(2)]
        neg_max = m.sb("neg_max", [P, 2])
        row_sum, inv_sum = m.sb("row_sum", [P, 4]), m.sb("inv_sum", [P, 4])
        wq_raw, wq_wide = m.sb("wq_raw", [P, QT_, 2, QK]), m.sb("wq_wide", [P, QT_, 2, P])
        wq_hi, wq_lo = m.sb("wq_hi", [P, QT_, 2, P], F32R), m.sb("wq_lo", [P, QT_, 2, P], F32R)
        wk_raw = m.sb("wk_raw", [P, KVT_, 2, NOPE])
        wk_hi, wk_lo = m.sb("wk_hi", [P, KVT_, P], F32R), m.sb("wk_lo", [P, KVT_, P], F32R)
        o_low, o_sum = m.sb("o_low", [V_DIM, 2 * P]), m.sb("o_sum", [V_DIM, 2 * P])
        o_out = m.sb("o_out", [V_DIM, 2, BLK])
        PAD = max(POOL_WINDOWS) // 2
        W_MAX = S_SAMPLE + 2 * PAD
        u_in, sum_a, sum_b = m.sb("u_in", [P, W_MAX]), m.sb("window_a", [P, W_MAX]), m.sb("window_b", [P, W_MAX])
        inv_count = m.sb("inv_count", [P, S_SAMPLE])

        ps_s = [m.ps(f"ps_scores{s}", (P, 1024)) for s in range(2)]
        ps_t = [m.ps(f"ps_probsT{s}") for s in range(2)]
        ps_k = [ps_s[0][:, 0:BLK], ps_s[0][:, BLK:2 * BLK], ps_s[1][:, 0:BLK]]
        ps_q, ps_o = m.ps("ps_q"), m.ps("ps_o")

        RING = 6
        lat_loaded = [m.sem(f"b_lat_loaded{s}") for s in range(RING)]
        lat_hi_done, lat_lo_done = m.sem("b_lat_hi_done"), m.sem("b_lat_lo_done")
        table_loaded = m.sem("b_table_loaded")
        wq_loaded, wk_loaded, v_loaded = m.sem("b_wq_loaded"), m.sem("b_wk_loaded"), m.sem("b_v_loaded")
        wq_widened, w_hi_done, w_lo_done = m.sem("b_wq_widened"), m.sem("b_w_hi_done"), m.sem("b_w_lo_done")
        v_hi_done, v_lo_done = m.sem("b_v_hi_done"), m.sem("b_v_lo_done")
        k_done, k_hi_done, k_lo_done = m.sem("b_k_done"), m.sem("b_k_hi_done"), m.sem("b_k_lo_done")
        q_done, q_rotated, q_shifted = m.sem("b_q_done"), m.sem("b_q_rotated"), m.sem("b_q_shifted")
        q_added, q_hi_done, q_lo_done = m.sem("b_q_added"), m.sem("b_q_hi_done"), m.sem("b_q_lo_done")
        s_done, max_done, exp_done = m.sem("b_s_done"), m.sem("b_max_done"), m.sem("b_exp_done")
        t_done, t_hi_done, t_lo_done = m.sem("b_t_done"), m.sem("b_t_hi_done"), m.sem("b_t_lo_done")
        o_done, inv_done, o_low_copied, o_added, o_scaled = (
            m.sem("b_" + x) for x in ("o_done", "inv_done", "o_low_copied", "o_added", "o_scaled"))
        o_stored = [m.sem(f"b_o_stored{s}") for s in range(2)]
        u_loaded, count_loaded = m.sem("b_u_loaded"), m.sem("b_count_loaded")
        window_step, d_stored = m.sem("b_window_step"), m.sem("b_d_stored")

        PIECE = T // 2
        piece_raw = m.sb("piece_raw", [P, RING - 2, PIECE])
        pieces = [("kvT", kvn_hi, kvn_lo, k, c) for k in range(KVT_) for c in range(2)] \
            + [("krT", k_hi, k_lo, None, c) for c in range(2)] \
            + [("qT", qn_hi, qn_lo, k, c) for c in range(2) for k in range(QT_)]
        KEY_PIECES, FIRST_QUERY_PIECES = 2 * KVT_ + 2, 2 * KVT_ + 2 + QT_

        def raw_piece(n, rows=P):
            slot = n % RING
            return probs[0:rows, slot, 0:PIECE] if slot < 2 else piece_raw[0:rows, slot - 2, :]

        def piece_views(n, part):
            _, hi, lo, k, c = pieces[n]
            buf = hi if part == "hi" else lo
            cols = slice(c * PIECE, (c + 1) * PIECE)
            if k is not None:
                return [(buf[:, k, cols], raw_piece(n), f32(hi[:, k, cols]))]
            return [(buf[0:2 * ROPE, h, cols], raw_piece(n, 2 * ROPE), f32(hi[0:2 * ROPE, h, cols])) for h in range(2)]

        splits_before = [sum(2 if pieces[x][3] is None else 1 for x in range(n)) for n in range(len(pieces) + 1)]

        def next_block(i, n, last):
            b = n // 4 + 1
            return (i, b) if b < BLOCKS else None if last else (i + 1, 0)

        block = ctx.enter_context(nc.Block())

        @block.sync
        def _(sp):
            w_q = dram["w_uq"].rearrange("(t p) (h c) -> p t (h c)", p=P, c=QK)
            w_k = dram["w_ukv"].rearrange("(t p) (h c) -> t p h c", p=P, c=NOPE + V_DIM)
            v_rows = dram["v"].rearrange("(t p) c -> p t c", p=P)

            def load_weights(q_column, head, v_column):
                sp.dma_start(wq_raw[:, :, :, :].rearrange("p t h c -> p t (h c)"),
                             w_q[:, :, bass.ds(q_column, 2 * QK)]).then_inc(wq_loaded, 16)
                for k in range(KVT_):
                    sp.dma_start(wk_raw[:, k, :, :], w_k[k][:, bass.ds(head, 2), 0:NOPE]).then_inc(wk_loaded, 16)
                sp.dma_start(v_raw[:, :, :, :].rearrange("p t h v -> p t (h v)"), v_rows[:, :, bass.ds(v_column, 2 * V_DIM)]).then_inc(v_loaded, 16)

            load_weights(0, 0, 0)
            for n, (name, _, _, k, c) in enumerate(pieces):
                if n >= RING:
                    sp.wait_ge(lat_lo_done, splits_before[n - RING + 1])
                cols = slice(c * PIECE, (c + 1) * PIECE)
                rows, n_rows = (slice(k * P, (k + 1) * P), P) if k is not None else (slice(0, 2 * ROPE), 2 * ROPE)
                sp.dma_start(raw_piece(n, n_rows), dram[name][rows, cols]).then_inc(lat_loaded[n % RING], 16)
                if n == KEY_PIECES - 1:
                    sp.dma_start(q_table[:, :], dram["q_table"]).then_inc(table_loaded, 16)

            def step(i, last=False):
                if not last:
                    at = [sp.snap((i + 1) * 2 * size) for size in (QK, 1, V_DIM)]
                    sp.wait_ge(v_lo_done, i + 1)
                    sp.wait_ge(w_lo_done, 2 * i + 2)
                    load_weights(*at)
                for b in range(BLOCKS):
                    head, blk = b // 3, b % 3
                    first = POOL_DIM + (2 * i + head) * V_DIM
                    rows = bass.ds(first if last else sp.snap(first), V_DIM)
                    sp.wait_ge(o_scaled, UNITS * i + 2 * b + 2)
                    sp.dma_start(dram["mixT"][rows, blk * BLK:(blk + 1) * BLK], o_out[:, b % 2, :]).then_inc(o_stored[b % 2], 16)

            with sp.Fori(0, PAIRS - 1) as i:
                step(i)
            step(PAIRS - 1, last=True)
            for s in range(2):
                sp.wait_ge(o_stored[s], 16 * 3 * PAIRS)

        @block.gpsimd
        def _(pool):
            pool.memset(u_in[:, :], 0.0).then_inc(window_step, 1)
            steps, loads = 1, 0
            for start, n in ((0, S_SAMPLE), (S_SAMPLE, S_PROMPT)):
                width = n + 2 * PAD
                if start:
                    pool.wait_ge(window_step, steps)
                    pool.memset(u_in[:, PAD + n:width], 0.0).then_inc(window_step, 1)
                    steps += 1
                for g, window in enumerate(POOL_WINDOWS):
                    pool.wait_ge(window_step, steps)
                    pool.wait_ge(d_stored, 16 * loads)
                    pool.dma_start(u_in[:, PAD:PAD + n], dram["uT"][g * GROUP:(g + 1) * GROUP, start:start + n]).then_inc(u_loaded, 16)
                    pool.dma_start(inv_count[:, 0:n], dram["inv_count"][g, start:start + n].partition_broadcast(P)).then_inc(count_loaded, 16)
                    loads += 1
                    pool.wait_ge(u_loaded, 16 * loads)
                    pool.wait_ge(count_loaded, 16 * loads)
                    src, dst, other = u_in, sum_a, sum_b
                    pool.tensor_tensor(dst[:, 1:width], u_in[:, 0:width - 1], u_in[:, 1:width], ALU.add).then_inc(window_step, 1)
                    steps += 1
                    reach, size = 1, 2
                    while size < window:
                        src, dst, other = dst, other, dst
                        half = size // 2
                        lo, hi = reach + half, width - (reach - 1) - half
                        pool.wait_ge(window_step, steps)
                        pool.tensor_tensor(dst[:, lo:hi], src[:, lo - half:hi - half], src[:, lo + half:hi + half], ALU.add).then_inc(window_step, 1)
                        steps += 1
                        reach, size = lo, 2 * size
                    body = slice(PAD, PAD + n)
                    pool.wait_ge(window_step, steps)
                    pool.tensor_tensor(dst[:, body], dst[:, body], inv_count[:, 0:n], ALU.mult).then_inc(window_step, 1)
                    pool.wait_ge(window_step, steps + 1)
                    pool.tensor_tensor(dst[:, body], dst[:, body], u_in[:, body], ALU.subtract).then_inc(window_step, 1)
                    steps += 2
                    pool.wait_ge(window_step, steps)
                    pool.dma_start(dram["dT"][g * GROUP:(g + 1) * GROUP, start:start + n], dst[:, body]).then_inc(d_stored, 16)
            pool.wait_ge(d_stored, 16 * loads)

        @block.scalar
        def _(act):
            def round_weights(i):
                act.wait_ge(wk_loaded, 32 * (i + 1))
                act.wait_ge(k_done, 3 * i)
                act.activation(wk_hi[:, :, :], wk_raw[:, :, :, :].rearrange("p t h c -> p t (h c)"), ACT.Copy).then_inc(w_hi_done, 1)
                act.wait_ge(wq_widened, 4 * (i + 1))
                act.wait_ge(q_done, BLOCKS * i)
                act.activation(wq_hi[:, :, :, :], wq_wide[:, :, :, :], ACT.Copy).then_inc(w_hi_done, 1)

            round_weights(0)

            def round_pieces(first, after):
                for n in range(first, after):
                    act.wait_ge(lat_loaded[n % RING], 16 * (n // RING + 1))
                    for out, src, _ in piece_views(n, "hi"):
                        act.activation(out, src, ACT.Copy).then_inc(lat_hi_done, 1)

            def shift_rope(i, b):
                act.wait_ge(q_rotated, BLOCKS * i + b + 1)
                act.wait_ge(q_added, BLOCKS * i + b)
                act.activation(q_moved[:, :], q_work[ROPE:2 * ROPE, :], ACT.Copy).then_inc(q_shifted, 1)

            def round_q(i, b):
                act.wait_ge(q_added, BLOCKS * i + b + 1)
                if b != 0 or not isinstance(i, int) or i > 0:
                    act.wait_ge(s_done, TILES * i + (4 * (b - 1) if b else -4))
                act.activation(q_hi[:, b % 2, :], q_work[:, :], ACT.Copy).then_inc(q_hi_done, 1)

            def round_probsT(i, n):
                unit = n // 2
                for h in range(first_half[n + 1] - first_half[n]):
                    at = first_half[n] + h
                    act.wait_ge(o_done, UNITS * i + max(unit - 1, 0))
                    act.wait_ge(t_done, HALVES * i + at + 1)
                    act.activation(pT_hi[unit % 2][:, 4 * h:4 * h + 4, (n % 2) * P:(n % 2 + 1) * P],
                                   ps_t[at % 2][:, :].rearrange("p (k t) -> p k t", t=P), ACT.Copy).then_inc(t_hi_done, 1)

            def exponent(i, n):
                _, nk = keys(n)
                act.wait_ge(t_done, HALVES * i + (first_half[n - 1] if n >= 2 else 0))
                act.wait_ge(max_done, TILES * i + n + 1)
                act.activation(probs[:, n % 2, 0:nk * P], ps_s[n % 2][:, 0:nk * P], ACT.Exp,
                               bias=neg_max[:, n % 2:n % 2 + 1], accum_out=row_sum[:, n % 4:n % 4 + 1]).then_inc(exp_done, 1)

            def copy_low(i, unit):
                act.wait_ge(o_done, UNITS * i + unit + 1)
                act.wait_ge(o_added, UNITS * i + unit)
                act.activation(o_low[:, :], ps_o[V_DIM:P, 0:2 * P], ACT.Copy).then_inc(o_low_copied, 1)

            def round_keys(i):
                for blk in range(3):
                    act.wait_ge(k_done, 3 * i + blk + 1)
                    for head in range(2):
                        act.activation(k_hi[NOPE:P, head, blk * BLK:(blk + 1) * BLK],
                                       ps_k[blk][head * NOPE:(head + 1) * NOPE, :], ACT.Copy).then_inc(k_hi_done, 1)

            def round_v(i):
                act.wait_ge(v_loaded, 16 * (i + 1))
                act.wait_ge(o_done, UNITS * i)
                act.activation(v_parts[:, :, :, 0, :], v_raw[:, :, :, :], ACT.Copy).then_inc(v_hi_done, 1)

            def step(i, last=False):
                for n in range(TILES):
                    if n >= 4 and n % 2 == 0:
                        copy_low(i, n // 2 - 2)
                    if n:
                        round_probsT(i, n - 1)
                    exponent(i, n)
                    ahead = next_block(i, n, last)
                    if ahead and n % 4 == 0:
                        shift_rope(*ahead)
                    if ahead and n % 4 == 1:
                        round_q(*ahead)
                    if n == 0:
                        round_v(i)
                    if n == 17 and not last:
                        round_weights(i + 1)
                copy_low(i, UNITS - 2)
                round_probsT(i, TILES - 1)
                if not last:
                    round_keys(i + 1)
                copy_low(i, UNITS - 1)

            round_pieces(0, KEY_PIECES)
            round_keys(0)
            round_pieces(KEY_PIECES, FIRST_QUERY_PIECES)
            shift_rope(0, 0)
            round_q(0, 0)
            round_pieces(FIRST_QUERY_PIECES, len(pieces))
            with act.Fori(0, PAIRS - 1) as i:
                step(i)
            step(PAIRS - 1, last=True)

        @block.vector
        def _(dve):
            def widen_weights(i):
                dve.wait_ge(wq_loaded, 16 * (i + 1))
                dve.wait_ge(w_lo_done, 2 * i)
                half = ROPE // 2
                for dst, src, size in ((0, NOPE, ROPE), (ROPE, NOPE + half, half), (ROPE + half, NOPE, half), (2 * ROPE, 0, NOPE)):
                    nc.vector.tensor_copy(wq_wide[:, :, :, dst:dst + size], wq_raw[:, :, :, src:src + size]).then_inc(wq_widened, 1)

            def rest_weights(i):
                dve.wait_ge(w_hi_done, 2 * i + 1)
                nc.vector.tensor_tensor(wk_lo[:, :, :], wk_raw[:, :, :, :].rearrange("p t h c -> p t (h c)"),
                                        f32(wk_hi[:, :, :]), ALU.subtract).then_inc(w_lo_done, 1)
                dve.wait_ge(w_hi_done, 2 * i + 2)
                nc.vector.tensor_tensor(wq_lo[:, :, :, :], wq_wide[:, :, :, :], f32(wq_hi[:, :, :, :]),
                                        ALU.subtract).then_inc(w_lo_done, 1)

            widen_weights(0)
            rest_weights(0)

            def rest_pieces(first, after):
                for n in range(first, after):
                    for x, (out, src, hi) in enumerate(piece_views(n, "lo")):
                        dve.wait_ge(lat_hi_done, splits_before[n] + x + 1)
                        nc.vector.tensor_tensor(out, src, hi, ALU.subtract).then_inc(lat_lo_done, 1)

            def rotate(i, b):
                blk = b % 3
                dve.wait_ge(q_done, BLOCKS * i + b + 1)
                dve.wait_ge(q_lo_done, BLOCKS * i + b)
                position = 0 if blk == 2 else blk * BLK
                nc.vector.tensor_tensor(q_work[:, :], ps_q[:, :], q_table[:, position:position + BLK], ALU.mult).then_inc(q_rotated, 1)

            def add_rope(i, b):
                dve.wait_ge(q_shifted, BLOCKS * i + b + 1)
                nc.vector.tensor_tensor(q_work[0:ROPE, :], q_work[0:ROPE, :], q_moved[:, :], ALU.add).then_inc(q_added, 1)

            def rest_q(i, b):
                dve.wait_ge(q_hi_done, BLOCKS * i + b + 1)
                nc.vector.tensor_tensor(q_lo[:, b % 2, :], q_work[:, :], f32(q_hi[:, b % 2, :]), ALU.subtract).then_inc(q_lo_done, 1)

            def maximum(i, n):
                _, nk = keys(n)
                dve.wait_ge(exp_done, TILES * i + max(n - 1, 0))
                dve.wait_ge(s_done, TILES * i + n + 1)
                nc.vector.tensor_reduce(neg_max[:, n % 2:n % 2 + 1], ps_s[n % 2][:, 0:nk * P], op=ALU.max, axis=AX.X,
                                        negate=True).then_inc(max_done, 1)

            def rest_probsT(i, n):
                unit = n // 2
                dve.wait_ge(exp_done, TILES * i + n + 1)
                nc.vector.reciprocal(inv_sum[:, n % 4:n % 4 + 1], row_sum[:, n % 4:n % 4 + 1]).then_inc(inv_done, 1)
                for h in range(first_half[n + 1] - first_half[n]):
                    at = first_half[n] + h
                    dve.wait_ge(t_hi_done, HALVES * i + at + 1)
                    dst = (slice(None), slice(4 * h, 4 * h + 4), slice((n % 2) * P, (n % 2 + 1) * P))
                    nc.vector.tensor_tensor(pT_lo[unit % 2][dst], ps_t[at % 2][:, :].rearrange("p (k t) -> p k t", t=P),
                                            f32(pT_hi[unit % 2][dst]), ALU.subtract).then_inc(t_lo_done, 1)

            def divide(i, unit):
                b = unit // 2
                dve.wait_ge(o_low_copied, UNITS * i + unit + 1)
                nc.vector.tensor_tensor(o_sum[:, :], ps_o[0:V_DIM, 0:2 * P], o_low[:, :], ALU.add).then_inc(o_added, 1)
                dve.wait_ge(o_stored[b % 2], 16 * (3 * i + b // 2))
                dve.wait_ge(o_added, UNITS * i + unit + 1)
                nc.vector.tensor_tensor(o_out[:, b % 2, (unit % 2) * 2 * P:(unit % 2 + 1) * 2 * P], o_sum[:, :],
                                        ps_o[0:V_DIM, 2 * P:4 * P], ALU.mult).then_inc(o_scaled, 1)

            def rest_keys(i):
                for blk in range(3):
                    for head in range(2):
                        dve.wait_ge(k_hi_done, 6 * i + 2 * blk + 2)
                        keep = (slice(NOPE, P), head, slice(blk * BLK, (blk + 1) * BLK))
                        nc.vector.tensor_tensor(k_lo[keep], ps_k[blk][head * NOPE:(head + 1) * NOPE, :], f32(k_hi[keep]),
                                                ALU.subtract).then_inc(k_lo_done, 1)

            def rest_v(i):
                dve.wait_ge(v_hi_done, i + 1)
                nc.vector.tensor_tensor(v_parts[:, :, :, 1, :], v_raw[:, :, :, :], f32(v_parts[:, :, :, 0, :]),
                                        ALU.subtract).then_inc(v_lo_done, 1)

            rest_pieces(0, KEY_PIECES)
            rest_keys(0)
            rest_pieces(KEY_PIECES, FIRST_QUERY_PIECES)
            dve.wait_ge(table_loaded, 16)
            rotate(0, 0)
            add_rope(0, 0)
            rest_q(0, 0)
            rest_pieces(FIRST_QUERY_PIECES, len(pieces))

            def step(i, last=False):
                for n in range(TILES):
                    maximum(i, n)
                    if n:
                        rest_probsT(i, n - 1)
                    ahead = next_block(i, n, last)
                    if ahead and n % 4 < 3:
                        (rotate, add_rope, rest_q)[n % 4](*ahead)
                    if n == 0:
                        rest_v(i)
                    if n >= 4 and n % 2 == 0:
                        divide(i, n // 2 - 2)
                    if n == 16 and not last:
                        widen_weights(i + 1)
                    if n == 18 and not last:
                        rest_weights(i + 1)
                rest_probsT(i, TILES - 1)
                divide(i, UNITS - 2)
                if not last:
                    rest_keys(i + 1)
                divide(i, UNITS - 1)

            with dve.Fori(0, PAIRS - 1) as i:
                step(i)
            step(PAIRS - 1, last=True)

        @block.tensor
        def _(pe):
            def key_block(i, blk):
                if blk == 0:
                    pe.wait_ge(w_lo_done, 2 * i + 2)
                for k in range(KVT_):
                    cols = slice(blk * BLK, (blk + 1) * BLK)
                    last = three_passes(nc, ps_k[blk], wk_hi[:, k, :], wk_lo[:, k, :], kvn_hi[:, k, cols], kvn_lo[:, k, cols],
                                        k == 0, k == KVT_ - 1)
                last.then_inc(k_done, 1)

            def query_block(i, b):
                head, blk = b // 3, b % 3
                if b == 0:
                    pe.wait_ge(w_lo_done, 2 * i + 2)
                if b or not isinstance(i, int) or i:
                    pe.wait_ge(q_rotated, BLOCKS * i + b)
                for k in range(QT_):
                    cols = slice(blk * BLK, (blk + 1) * BLK)
                    last = three_passes(nc, ps_q[:, :], wq_hi[:, k, head, :], wq_lo[:, k, head, :],
                                        qn_hi[:, k, cols], qn_lo[:, k, cols], k == 0, k == QT_ - 1)
                last.then_inc(q_done, 1)

            def scores(i, n):
                b, (start, nk) = n // 4, keys(n)
                if n == 0:
                    pe.wait_ge(k_lo_done, 6 * i + 6)
                pe.wait_ge(q_lo_done, BLOCKS * i + b + 1)
                pe.wait_ge(exp_done, TILES * i + max(n - 1, 0))
                rows = slice((n % 4) * P, (n % 4 + 1) * P)
                for c in range(nk // 4):
                    cols = slice(start + c * BLK, start + (c + 1) * BLK)
                    last = three_passes(nc, ps_s[n % 2][:, c * BLK:(c + 1) * BLK], q_hi[:, b % 2, rows], q_lo[:, b % 2, rows],
                                        k_hi[:, b // 3, cols], k_lo[:, b // 3, cols], True, True)
                last.then_inc(s_done, 1)

            def transpose_probs(i, n):
                for h in range(first_half[n + 1] - first_half[n]):
                    at = first_half[n] + h
                    pe.wait_ge(exp_done, TILES * i + n + 1)
                    pe.wait_ge(t_lo_done, HALVES * i + max(at - 1, 0))
                    for k in range(4):
                        last = nc.tensor.transpose(ps_t[at % 2][:, k * P:(k + 1) * P],
                                                   probs[:, n % 2, (4 * h + k) * P:(4 * h + k + 1) * P], ident[:, :])
                    last.then_inc(t_done, 1)

            def outputs(i, unit):
                start, nk = keys(2 * unit)
                head = unit // 6
                if unit == 0:
                    pe.wait_ge(v_lo_done, i + 1)
                pe.wait_ge(t_lo_done, HALVES * i + first_half[2 * unit + 2])
                pe.wait_ge(o_scaled, UNITS * i + unit)
                for k in range(nk):
                    both = v_parts[:, start // P + k, head, :, :].rearrange("p a v -> p (a v)")
                    nc.tensor.matmul(ps_o[:, 0:2 * P], both, pT_hi[unit % 2][:, k, :], start=k == 0, stop=False)
                    nc.tensor.matmul(ps_o[:, 0:2 * P], both, pT_lo[unit % 2][:, k, :], start=False, stop=k == nk - 1)
                pe.wait_ge(inv_done, TILES * i + 2 * unit + 2)
                for x in range(2):
                    at = (2 * unit + x) % 4
                    last = nc.tensor.matmul(ps_o[0:V_DIM, (2 + x) * P:(3 + x) * P], inv_sum[:, at:at + 1].to_broadcast([P, V_DIM]),
                                            ident[:, :], start=True, stop=True)
                last.then_inc(o_done, 1)

            pe.wait_ge(lat_lo_done, splits_before[KEY_PIECES])
            for blk in range(3):
                key_block(0, blk)
            pe.wait_ge(lat_lo_done, splits_before[FIRST_QUERY_PIECES])
            query_block(0, 0)

            def step(i, last=False):
                for n in range(TILES):
                    ahead = next_block(i, n, last)
                    scores(i, n)
                    if n:
                        transpose_probs(i, n - 1)
                    else:
                        pe.wait_ge(lat_lo_done, splits_before[-1])
                    if ahead and n % 4 == 0:
                        query_block(*ahead)
                    if n >= 3 and n % 2:
                        outputs(i, (n - 3) // 2)
                transpose_probs(i, TILES - 1)
                if not last:
                    for blk in range(3):
                        key_block(i + 1, blk)
                outputs(i, UNITS - 1)

            with pe.Fori(0, PAIRS - 1) as i:
                step(i)
            step(PAIRS - 1, last=True)


class ExpertWeights:
    CHUNK, HALF, N_CHUNKS = 2048, FFN // 2, 6
    EARLY = 4
    GATE, UP, DOWN = (0, 2), (1, 3), (4, 5)

    def __init__(self, m, dram):
        self.dram = dram
        self.raw = m.sb("w_raw", [P, self.N_CHUNKS, self.CHUNK])
        self.hi = [m.sb(f"w_hi{c}", [P, self.CHUNK], F32R) for c in range(self.EARLY)]
        self.lo = [m.sb(f"w_lo{c}", [P, self.CHUNK], F32R) for c in range(self.EARLY)]
        self.loaded = [m.sem(f"expert_loaded{c}") for c in range(self.N_CHUNKS)]
        self.hi_done, self.lo_done = m.sem("expert_hi_done"), m.sem("expert_lo_done")

    def load(self, sp, e, c):
        if c in self.DOWN:
            rows = slice((c - 4) * 2 * P, (c - 3) * 2 * P)
            src = self.dram["w_down"][bass.ds(e, 1), rows, :].rearrange("e (k p) d -> p (e k) d", p=P)
            dst = self.raw[:, c, :].rearrange("p (k d) -> p k d", d=D)
        else:
            w = self.dram["w_gate" if c in self.GATE else "w_up"]
            cols = slice(c // 2 * self.HALF, (c // 2 + 1) * self.HALF)
            src = w[bass.ds(e, 1), :, cols].rearrange("e (k p) f -> p (e k) f", p=P)
            dst = self.raw[:, c, :].rearrange("p (k f) -> p k f", f=self.HALF)
        sp.dma_start(dst, src).then_inc(self.loaded[c], 16)


def phase_mix(nc, ident, dram, route, experts):
    with ExitStack() as ctx:
        m = Scope(nc, ctx)
        w_raw = experts.raw[:, :, :].rearrange("p c (h d) -> p (c h) d", d=D)
        w_hi = [experts.hi[k // 2][:, k % 2 * D:(k % 2 + 1) * D] for k in range(KD)]
        w_lo = [experts.lo[k // 2][:, k % 2 * D:(k % 2 + 1) * D] for k in range(KD)]
        w_pool, pool_scale = m.sb("w_pool", [P, 4, P]), m.sb("pool_scale_all", [P, 4, P])
        d = m.sb("d", [P, 2, 4, P])
        mix_raw = m.sb("mix_raw", [P, 2, 4, P])
        mix_hi, mix_lo = m.sb("mix_hi", [P, 2, KD, P], F32R), m.sb("mix_lo", [P, 2, KD, P], F32R)
        x0, x1, acc = m.sb("x0_again", [P, 2, D]), m.sb("x1", [P, 2, D]), m.sb("acc_out", [P, 2, D])
        ln_g, ln_b = m.sb("ln1_g_all", [P, D]), m.sb("ln1_b_all", [P, D])
        stats, moments, rstd = m.sb("ln1_stats", [P, 2, 2, 6]), m.sb("ln1_moments", [P, 2, 2]), m.sb("ln1_rstd", [P, 2])
        half_neg, eps, carrier = m.sb("c_minus_half", [P, 1]), m.sb("c_eps", [P, 1]), m.sb("c_wait_carrier", [P, 1])
        x1T = m.sb("x1T", [P, KD, P])
        w_router = m.sb("w_router", [P, KD, N_EXPERTS])
        logitsT, neg_max, e_logits = m.sb("logitsT", [N_EXPERTS, P]), m.sb("router_neg_max", [P, 1]), m.sb("e_logits", [P, N_EXPERTS])
        e_sum, e_inv, affinity = m.sb("e_sum", [P, 1]), m.sb("e_inv", [P, 1]), m.sb("affinity", [P, N_EXPERTS])
        affT = m.sb("affT", [N_EXPERTS, T])
        left = [m.sb(f"topk_left{s}", [N_EXPERTS, S_SAMPLE]) for s in range(2)]
        value = [m.sb(f"topk_value{q}", [N_EXPERTS, P]) for q in range(2)]
        index = [m.sb(f"topk_index{q}", [N_EXPERTS, P], U32) for q in range(2)]
        index_f = [m.sb(f"topk_index_f{q}", [N_EXPERTS, P]) for q in range(2)]

        ps_mix = [m.ps(f"ps_mix{s}", (P, D)) for s in range(2)]
        ps_t = [m.ps(f"ps_x1T{s}") for s in range(2)]
        ps_r, ps_a = m.ps("ps_router"), m.ps("ps_affinity")

        consts_loaded, ln_loaded, filled = m.sem("c_consts_loaded"), m.sem("c_ln_loaded"), m.sem("c_filled")
        wp_scaled = m.sem("c_wp_scaled")
        d_loaded = [m.sem(f"c_d_loaded{s}") for s in range(2)]
        pool_done = m.sem("c_pool_done")
        w_loaded = [m.sem(f"c_w_loaded{k}") for k in range(KD)]
        w_hi_done, w_lo_done = m.sem("c_w_hi_done"), m.sem("c_w_lo_done")
        mix_loaded = [m.sem(f"c_mix_loaded{s}") for s in range(2)]
        mix_hi_done, mix_lo_done = m.sem("c_mix_hi_done"), m.sem("c_mix_lo_done")
        pool_hi_done, pool_lo_done = m.sem("c_pool_hi_done"), m.sem("c_pool_lo_done")
        x0_loaded = [m.sem(f"c_x0_loaded{s}") for s in range(2)]
        wo_done, summed, stats_part, stats_done = m.sem("c_wo_done"), m.sem("c_summed"), m.sem("c_stats_part"), m.sem("c_stats_done")
        eps_added, rstd_done, centred, scaled, x1_done = (m.sem("c_" + x) for x in ("eps_added", "rstd_done", "centred", "scaled", "x1_done"))
        acc_done = m.sem("c_acc_done")
        x1_stored, acc_stored = [m.sem(f"c_x1_stored{s}") for s in range(2)], [m.sem(f"c_acc_stored{s}") for s in range(2)]
        t_done, t_copied, logits_done, logits_copied, logits_turned = (m.sem("c_" + x) for x in ("t_done", "t_copied", "logits_done", "logits_copied", "logits_turned"))
        r_max_done, r_exp_done, r_inv_done, r_aff_done, aff_turned, aff_copied = (
            m.sem("c_" + x) for x in ("r_max_done", "r_exp_done", "r_inv_done", "r_aff_done", "aff_turned", "aff_copied"))
        topk_step, lists_turned, lists_copied = m.sem("c_topk_step"), m.sem("c_lists_turned"), m.sem("c_lists_copied")

        TOPK_STEPS = 3 * (CAP_SAMPLE // 8) + 1 + 3 * (CAP_PROMPT // 8) + 4
        K_ORDER = (4, 5, 6, 7, 0, 1, 2, 3)
        EARLY_TOPK = {N_TILES - 2: (1, 2), N_TILES - 1: (1, 2), N_TILES: (0, 2), N_TILES + 1: (2, 6)}
        block = ctx.enter_context(nc.Block())

        def steps(eng, step):
            for s in range(2):
                step(s)
            with eng.Fori(1, N_TILES // 2 - 1) as i:
                for b in range(2):
                    step(2 * i + b, b)
            for s in range(N_TILES - 2, N_TILES + 2):
                step(s)

        def has(s, lag):
            return not isinstance(s, int) or lag <= s < N_TILES + lag

        @block.sync
        def _(sp):
            def load_mix(s, slot):
                cols = bass.ds(s * P, P)
                by_slice = lambda name: dram[name].rearrange("(k p) t -> p k t", p=P)
                sp.dma_start(d[:, slot, :, :], by_slice("dT")[:, :, cols]).then_inc(d_loaded[slot], 16)
                sp.dma_start(mix_raw[:, slot, :, :], by_slice("mixT")[:, 4:8, cols]).then_inc(mix_loaded[slot], 16)

            def load_x0(s, slot):
                sp.dma_start(x0[:, slot, :], dram["x0"][bass.ds(s * P, P), :]).then_inc(x0_loaded[slot], 16)

            sp.dma_start(w_pool[:, :, :], dram["w_pool"].rearrange("g c d -> c g d")).then_inc(consts_loaded, 16)
            sp.dma_start(pool_scale[:, :, :].rearrange("p g d -> p (g d)"),
                         dram["pool_scale"].partition_broadcast(P)).then_inc(consts_loaded, 16)
            load_mix(0, 0)
            for n, k in enumerate(K_ORDER):
                sp.dma_start(w_raw[:, n, :], dram["w_o"][k * P:(k + 1) * P, :]).then_inc(w_loaded[n], 16)
                if n == 3:
                    load_x0(0, 0)
                    load_mix(1, 1)
            sp.dma_start(ln_g[:, :], dram["ln1_g"].partition_broadcast(P)).then_inc(ln_loaded, 16)
            sp.dma_start(ln_b[:, :], dram["ln1_b"].partition_broadcast(P)).then_inc(ln_loaded, 16)
            sp.dma_start(w_router[:, :, :], dram["w_router"].rearrange("(k p) e -> p k e", p=P)).then_inc(ln_loaded, 16)
            load_x0(1, 1)

            def step(s, slot=None):
                slot = s % 2 if slot is None else slot
                if not isinstance(s, int) or s + 2 < N_TILES:
                    sp.wait_ge(mix_lo_done, s + 1)
                    sp.wait_ge(pool_done, s + 1)
                    load_mix(s + 2, slot)
                if not isinstance(s, int) or 0 < s < N_TILES - 1:
                    sp.wait_ge(summed, s)
                    load_x0(s + 1, 1 - slot)
                if isinstance(s, int) and s == N_TILES - 1:
                    sp.wait_ge(w_lo_done, KD)
                    for c in range(experts.N_CHUNKS):
                        experts.load(sp, 0, c)
                if has(s, 1):
                    t = s - 1
                    sp.wait_ge(x1_done, s)
                    sp.dma_start(dram["x1"][bass.ds(t * P, P), :], x1[:, 1 - slot, :]).then_inc(x1_stored[1 - slot], 16)
                    sp.wait_ge(acc_done, s)
                    sp.dma_start(dram["acc"][bass.ds(t * P, P), :], acc[:, 1 - slot, :]).then_inc(acc_stored[1 - slot], 16)

            steps(sp, step)
            for s in range(2):
                sp.wait_ge(x1_stored[s], 16 * N_TILES // 2)
                sp.wait_ge(acc_stored[s], 16 * N_TILES // 2)

        @block.gpsimd
        def _(pool):
            pool.memset(half_neg[:, :], -0.5).then_inc(filled, 1)
            pool.memset(eps[:, :], LN_EPS).then_inc(filled, 1)
            pool.wait_ge(filled, 2)
            pool.wait_ge(ln_loaded, 48)

            def step(s, slot=None):
                slot = s % 2 if slot is None else slot
                if not has(s, 0):
                    return
                pool.wait_ge(stats_done, s + 1)
                pool.tensor_tensor(rstd[:, slot:slot + 1], moments[:, slot, 1:2], eps[:, :], ALU.add).then_inc(eps_added, 1)
                pool.wait_ge(eps_added, s + 1)
                pool.tensor_tensor(rstd[:, slot:slot + 1], rstd[:, slot:slot + 1], half_neg[:, :], ALU.pow).then_inc(rstd_done, 1)
                pool.wait_ge(scaled, s + 1)
                pool.tensor_tensor(x1[:, slot, :], x1[:, slot, :], ln_b[:, :], ALU.add).then_inc(x1_done, 1)

            steps(pool, step)
            for c in range(experts.EARLY):
                pool.wait_ge(experts.hi_done, c + 1)
                pool.tensor_tensor(experts.lo[c][:, :], experts.raw[:, c, :], f32(experts.hi[c][:, :]), ALU.subtract).then_inc(experts.lo_done, 1)

        @block.scalar
        def _(act):
            def round_attention(s, slot):
                act.wait_ge(mix_loaded[slot], 16 * ((s - slot) // 2 + 1) if isinstance(s, int) else 8 * (s - slot) + 16)
                if not isinstance(s, int) or s >= 2:
                    act.wait_ge(wo_done, s - 1)
                act.activation(mix_hi[:, slot, 4:8, :], mix_raw[:, slot, :, :], ACT.Copy).then_inc(mix_hi_done, 1)

            def round_pool(s, slot):
                act.wait_ge(pool_done, s + 1)
                act.activation(mix_hi[:, slot, 0:4, :], ps_t[0][:, :].rearrange("p (k t) -> p k t", t=P), ACT.Copy).then_inc(pool_hi_done, 1)

            round_attention(0, 0)
            for n, k in enumerate(K_ORDER):
                act.wait_ge(w_loaded[n], 16)
                act.activation(w_hi[k], w_raw[:, n, :], ACT.Copy).then_inc(w_hi_done, 1)
                if n == 1:
                    round_pool(0, 0)

            def step(s, slot=None):
                slot = s % 2 if slot is None else slot
                if has(s, 2):
                    act.wait_ge(logits_done, s - 1)
                    act.activation(logitsT[:, :], ps_r[0:N_EXPERTS, 0:P], ACT.Copy).then_inc(logits_copied, 1)
                if has(s, -1) and not (isinstance(s, int) and s + 1 >= N_TILES):
                    round_attention(s + 1, 1 - slot)
                    round_pool(s + 1, 1 - slot)
                if has(s, 1):
                    if not isinstance(s, int) or s >= 3:
                        act.wait_ge(acc_stored[1 - slot], 16 * ((s - 1) // 2) if isinstance(s, int) else 8 * (s - 1 - (1 - slot)))
                    act.wait_ge(x1_done, s)
                    act.activation(acc[:, 1 - slot, :], x1[:, 1 - slot, :], ACT.Copy, scale=ALPHA).then_inc(acc_done, 1)
                if has(s, 2):
                    act.wait_ge(r_max_done, s - 1)
                    act.activation(e_logits[:, :], ps_a[:, 0:N_EXPERTS], ACT.Exp, bias=neg_max[:, :],
                                   accum_out=e_sum[:, :]).then_inc(r_exp_done, 1)
                if has(s, 1):
                    for h in range(2):
                        if has(s, 2):
                            act.wait_ge(logits_done, s - 1)
                        act.wait_ge(t_done, 2 * (s - 1) + h + 1)
                        act.activation(x1T[:, 4 * h:4 * h + 4, :], ps_t[h][:, :].rearrange("p (k t) -> p k t", t=P),
                                       ACT.Copy).then_inc(t_copied, 1)

            steps(act, step)
            act.wait_ge(wo_done, N_TILES)
            for c in range(experts.EARLY):
                act.wait_ge(experts.loaded[c], 16)
                act.activation(experts.hi[c][:, :], experts.raw[:, c, :], ACT.Copy).then_inc(experts.hi_done, 1)

        @block.vector
        def _(dve):
            def rest_attention(s, slot):
                dve.wait_ge(mix_hi_done, s + 1)
                nc.vector.tensor_tensor(mix_lo[:, slot, 4:8, :], mix_raw[:, slot, :, :], f32(mix_hi[:, slot, 4:8, :]),
                                        ALU.subtract).then_inc(mix_lo_done, 1)

            def rest_pool(s, slot):
                dve.wait_ge(pool_hi_done, s + 1)
                nc.vector.tensor_tensor(mix_lo[:, slot, 0:4, :], ps_t[0][:, :].rearrange("p (k t) -> p k t", t=P),
                                        f32(mix_hi[:, slot, 0:4, :]), ALU.subtract).then_inc(pool_lo_done, 1)

            dve.wait_ge(consts_loaded, 32)
            nc.vector.tensor_tensor(w_pool[:, :, :], w_pool[:, :, :], pool_scale[:, :, :], ALU.mult).then_inc(wp_scaled, 1)
            rest_attention(0, 0)
            for n, k in enumerate(K_ORDER):
                dve.wait_ge(w_hi_done, n + 1)
                nc.vector.tensor_tensor(w_lo[k], w_raw[:, n, :], f32(w_hi[k]), ALU.subtract).then_inc(w_lo_done, 1)
                if n == 1:
                    rest_pool(0, 0)
            dve.wait_ge(ln_loaded, 48)
            dve.wait_ge(filled, 2)

            now, n_steps = affT[:, 0:S_SAMPLE], 0

            def topk_round(q, r):
                nonlocal now, n_steps
                size = (S_SAMPLE, S_PROMPT)[q]
                if r:
                    dve.wait_ge(topk_step, n_steps)
                eight = value[q][:, 8 * r:8 * r + 8]
                nc.vector.max(eight, now).then_inc(topk_step, 1)
                dve.wait_ge(topk_step, n_steps + 1)
                nc.vector.max_index(index[q][:, 8 * r:8 * r + 8], eight, now).then_inc(topk_step, 1)
                after = left[r % 2][:, 0:size]
                nc.vector.match_replace(after, eight, now, -1.0).then_inc(topk_step, 1)
                now = after
                n_steps += 3

            sample_rounds = iter(range(CAP_SAMPLE // 8))

            def early_topk(s, part):
                if isinstance(s, int) and s in EARLY_TOPK:
                    if part == 0 and s == N_TILES - 2:
                        dve.wait_ge(aff_copied, SAMPLE_TILES)
                    for _ in range(EARLY_TOPK[s][part]):
                        topk_round(0, next(sample_rounds))

            def step(s, slot=None):
                slot = s % 2 if slot is None else slot
                if has(s, -1) and not (isinstance(s, int) and s + 1 >= N_TILES):
                    rest_attention(s + 1, 1 - slot)
                    rest_pool(s + 1, 1 - slot)
                early_topk(s, 0)
                if has(s, 2):
                    dve.wait_ge(logits_turned, s - 1)
                    dve.wait_ge(r_exp_done, s - 2)
                    nc.vector.tensor_reduce(neg_max[:, :], ps_a[:, 0:N_EXPERTS], op=ALU.max, axis=AX.X, negate=True).then_inc(r_max_done, 1)
                if has(s, 2):
                    dve.wait_ge(r_exp_done, s - 1)
                    nc.vector.reciprocal(e_inv[:, :], e_sum[:, :]).then_inc(r_inv_done, 1)
                    dve.wait_ge(r_inv_done, s - 1)
                    dve.wait_ge(aff_turned, s - 2)
                    nc.vector.tensor_scalar(affinity[:, :], e_logits[:, :], e_inv[:, :], None, ALU.mult).then_inc(r_aff_done, 1)
                if has(s, 0):
                    if not isinstance(s, int) or s >= 2:
                        dve.wait_ge(t_done, 2 * (s - 1))
                        dve.wait_ge(acc_done, s - 1)
                        dve.wait_ge(x1_stored[slot], 16 * (s // 2) if isinstance(s, int) else 8 * (s - slot))
                    dve.wait_ge(x0_loaded[slot], 16 * (s // 2 + 1) if isinstance(s, int) else 8 * (s - slot) + 16)
                    dve.wait_ge(wo_done, s + 1)
                    nc.vector.scalar_tensor_tensor(out=x1[:, slot, :], in0=x0[:, slot, :], scalar=ALPHA, in1=ps_mix[slot][:, :],
                                                   op0=ALU.mult, op1=ALU.add).then_inc(summed, 1)
                    dve.wait_ge(summed, s + 1)
                    for h in range(2):
                        nc.vector.bn_stats(stats[:, slot, h, :], x1[:, slot, h * 512:(h + 1) * 512]).then_inc(stats_part, 1)
                    if not isinstance(s, int) or s >= 2:
                        dve.wait_ge(eps_added, s - 1)
                        dve.wait_ge(centred, s - 1)
                    dve.wait_ge(stats_part, 2 * s + 2)
                    wait_carrier(nc, carrier)
                    nc.vector.bn_aggr(moments[:, slot, :], stats[:, slot, :, :].rearrange("p h c -> p (h c)")).then_inc(stats_done, 1)
                    dve.wait_ge(rstd_done, s + 1)
                    nc.vector.tensor_scalar(x1[:, slot, :], x1[:, slot, :], moments[:, slot, 0:1], rstd[:, slot:slot + 1],
                                            ALU.subtract, ALU.mult).then_inc(centred, 1)
                    dve.wait_ge(centred, s + 1)
                    nc.vector.tensor_tensor(x1[:, slot, :], x1[:, slot, :], ln_g[:, :], ALU.mult).then_inc(scaled, 1)
                if has(s, 2):
                    dve.wait_ge(aff_turned, s - 1)
                    nc.vector.tensor_copy(affT[:, bass.ds((s - 2) * P, P)], ps_a[0:N_EXPERTS, P:2 * P]).then_inc(aff_copied, 1)
                early_topk(s, 1)

            steps(dve, step)

            assert next(sample_rounds, None) is None
            for q, (start, size, cap) in enumerate(((0, S_SAMPLE, CAP_SAMPLE), (S_SAMPLE, S_PROMPT, CAP_PROMPT))):
                if q:
                    now = affT[:, start:start + size]
                    dve.wait_ge(aff_copied, (start + size) // P)
                    for r in range(cap // 8):
                        topk_round(q, r)
                n = n_steps
                dve.wait_ge(topk_step, n)
                if q == 0:
                    nc.vector.tensor_copy(index_f[q][:, :], index[q][:, :]).then_inc(topk_step, 1)
                    n_steps = n + 1
                else:
                    nc.vector.tensor_copy(index_f[q][:, 0:cap], index[q][:, 0:cap]).then_inc(topk_step, 1)
                    nc.vector.tensor_copy(value[q][:, cap:2 * cap], value[q][:, 0:cap]).then_inc(topk_step, 1)
                    dve.wait_ge(topk_step, n + 1)
                    nc.vector.tensor_scalar(index_f[q][:, 0:cap], index_f[q][:, 0:cap], float(start), None, ALU.add).then_inc(topk_step, 1)
                    dve.wait_ge(topk_step, n + 3)
                    nc.vector.tensor_copy(index_f[q][:, cap:2 * cap], index_f[q][:, 0:cap]).then_inc(topk_step, 1)
                    n_steps = n + 4
            assert n_steps == TOPK_STEPS
            dve.wait_ge(lists_turned, 1)
            for q in range(2):
                nc.vector.tensor_copy(route["token"][q][:, :], ps_r[:, (2 * q) * N_EXPERTS:(2 * q + 1) * N_EXPERTS]).then_inc(lists_copied, 1)
                nc.vector.tensor_copy(route["gate"][q][:, :], ps_r[:, (2 * q + 1) * N_EXPERTS:(2 * q + 2) * N_EXPERTS]).then_inc(lists_copied, 1)

        @block.tensor
        def _(pe):
            def pool_product(s, slot):
                pe.wait_ge(d_loaded[slot], 16 * ((s - slot) // 2 + 1) if isinstance(s, int) else 8 * (s - slot) + 16)
                for g in range(4):
                    last = nc.tensor.matmul(ps_t[0][:, g * P:(g + 1) * P], w_pool[:, g, :], d[:, slot, g, :], start=True, stop=True)
                last.then_inc(pool_done, 1)

            def output_slices(s, slot, order):
                for n in order:
                    k = K_ORDER[n]
                    if isinstance(s, int) and s == 0:
                        pe.wait_ge(w_lo_done, n + 1)
                    for h in range(2):
                        cols = slice(h * 512, (h + 1) * 512)
                        last = three_passes(nc, ps_mix[slot][:, cols], mix_hi[:, slot, k, :], mix_lo[:, slot, k, :],
                                            w_hi[k][:, cols], w_lo[k][:, cols], n == 0, n == KD - 1)
                return last

            pe.wait_ge(wp_scaled, 1)
            pool_product(0, 0)

            def step(s, slot=None):
                slot = s % 2 if slot is None else slot
                if has(s, 0):
                    pe.wait_ge(mix_lo_done, s + 1)
                    if not isinstance(s, int) or s >= 2:
                        pe.wait_ge(summed, s - 1)
                    output_slices(s, slot, range(0, 3))
                    pe.wait_ge(pool_lo_done, s + 1)
                    output_slices(s, slot, range(3, 4))
                if has(s, 2):
                    pe.wait_ge(t_copied, 2 * (s - 1))
                    for k in range(KD):
                        last = nc.tensor.matmul(ps_r[0:N_EXPERTS, 0:P], w_router[:, k, :], x1T[:, k, :], start=k == 0, stop=k == KD - 1)
                    last.then_inc(logits_done, 1)
                if has(s, -1) and not (isinstance(s, int) and s + 1 >= N_TILES):
                    pool_product(s + 1, 1 - slot)
                if has(s, 0):
                    output_slices(s, slot, range(4, 6))
                if has(s, 2):
                    pe.wait_ge(aff_copied, s - 2)
                    pe.wait_ge(logits_copied, s - 1)
                if has(s, 0):
                    output_slices(s, slot, range(6, 7))
                if has(s, 2):
                    nc.tensor.transpose(ps_a[:, 0:N_EXPERTS], logitsT[:, :], ident[0:N_EXPERTS, 0:N_EXPERTS]).then_inc(logits_turned, 1)
                if has(s, 0):
                    output_slices(s, slot, range(7, KD)).then_inc(wo_done, 1)
                if isinstance(s, int) and s == 1:
                    pe.wait_ge(ln_loaded, 48)
                if has(s, 1):
                    pe.wait_ge(x1_done, s)
                    for h in range(2):
                        if not isinstance(s, int) or s >= 2:
                            pe.wait_ge(t_copied, 2 * (s - 1))
                        if h == 0 and not (isinstance(s, int) and s + 1 >= N_TILES):
                            pe.wait_ge(pool_lo_done, s + 2)
                        for k in range(4):
                            last = nc.tensor.transpose(ps_t[h][:, k * P:(k + 1) * P],
                                                       x1[:, 1 - slot, (4 * h + k) * P:(4 * h + k + 1) * P], ident[:, :])
                        last.then_inc(t_done, 1)
                if has(s, 2):
                    pe.wait_ge(r_aff_done, s - 1)
                    nc.tensor.transpose(ps_a[0:N_EXPERTS, P:2 * P], affinity[:, :], ident[:, :]).then_inc(aff_turned, 1)

            steps(pe, step)
            pe.wait_ge(topk_step, TOPK_STEPS)
            for q in range(2):
                for x, source in enumerate((index_f[q], value[q])):
                    c0 = (2 * q + x) * N_EXPERTS
                    last = nc.tensor.transpose(ps_r[:, c0:c0 + N_EXPERTS], source[:, :], ident[0:N_EXPERTS, 0:N_EXPERTS])
            last.then_inc(lists_turned, 1)


def phase_experts(nc, ident, dram, route, experts):
    with ExitStack() as ctx:
        m = Scope(nc, ctx)
        CS, CP = CAP_SAMPLE, CAP_PROMPT
        N = CS + CP
        FT = FFN // P
        CHUNK, HALF, N_CHUNKS = experts.CHUNK, experts.HALF, experts.N_CHUNKS
        GATE, UP, DOWN = experts.GATE, experts.UP, experts.DOWN
        raw, loaded = experts.raw, experts.loaded
        w_hi = experts.hi + [m.sb(f"w_hi{c}", [P, CHUNK], F32R) for c in range(experts.EARLY, N_CHUNKS)]
        w_lo = experts.lo + [m.sb(f"w_lo{c}", [P, CHUNK], F32R) for c in range(experts.EARLY, N_CHUNKS)]
        x_rows, x_rows_p = m.sb("x_rows_sample", [CS, D]), m.sb("x_rows_prompt", [CP, D])
        xT = m.sb("xT_hi_lo", [P, KD, 2 * N], F32R)
        g2, u2, g, u = (m.sb(x, [P, 2, N]) for x in ("gate_rest", "up_rest", "gate", "up"))
        sg, h = m.sb("silu_gate", [P, 2, N]), m.sb("h", [P, 2, N])
        hT = m.sb("hT_hi_lo", [P, FT, 2 * N], F32R)
        y_s, y_p, y_p_rest = m.sb("y_sample_rows", [CS, D]), m.sb("y_prompt_rows", [CP, D]), m.sb("y_prompt_rest", [CP, D])
        gather_at = [m.sb(f"gather_at{q}", [P, 1], U32) for q in range(2)]
        scatter_at = [m.sb(f"scatter_at{q}", [P, 1], U32) for q in range(2)]
        gate_now = [m.sb(f"gate_now{q}", [P, 1]) for q in range(2)]
        carrier, zero = m.sb("d_wait_carrier", [P, 1]), m.sb("d_zero", [P, 1])

        ps_g, ps_u = m.ps("ps_gate"), m.ps("ps_up")
        ps_x = [m.ps(f"ps_xT{b}") for b in range(2)]
        ps_ys, ps_yp = m.ps("ps_y_sample", (P, D)), m.ps("ps_y_prompt", (P, D))
        ps_turn = [ps_x[0][:, :], ps_x[1][:, :], ps_yp[:, 0:512], ps_yp[:, 512:1024]]

        hi_done, lo_done = experts.hi_done, experts.lo_done
        first_down_used = m.sem("d_first_down_used")
        gathered = [m.sem(f"d_gathered{q}") for q in range(2)]
        scattered = [m.sem(f"d_scattered{q}") for q in range(2)]
        index_copied, lists_copied, zeroed, carried = m.sem("d_index_copied"), m.sem("d_lists_copied"), m.sem("d_zeroed"), m.sem("d_carried")
        x_turned, x_hi_done, x_lo_done = m.sem("d_x_turned"), m.sem("d_x_hi_done"), m.sem("d_x_lo_done")
        g_done, u_done, g2_copied, u2_copied, g_added, u_added = (
            m.sem("d_" + x) for x in ("g_done", "u_done", "g2_copied", "u2_copied", "g_added", "u_added"))
        silu_done, h_done, h_hi_done, h_lo_done = (m.sem("d_" + x) for x in ("silu_done", "h_done", "h_hi_done", "h_lo_done"))
        ys_done, yp_done, ys_scaled, yp_rest_scaled, yp_scaled = (
            m.sem("d_" + x) for x in ("ys_done", "yp_done", "ys_scaled", "yp_rest_scaled", "yp_scaled"))

        block = ctx.enter_context(nc.Block())

        @block.sync
        def _(sp):
            for q in range(2):
                sp.wait_ge(gathered[q], 16)
            with sp.Fori(0, N_EXPERTS - 1) as e:
                for c in range(N_CHUNKS):
                    sp.wait_ge(lo_done, N_CHUNKS * e + c + 1)
                    experts.load(sp, e + 1, c)

        @block.gpsimd
        def _(pool):
            def pool_carrier():
                pool.tensor_tensor(carrier[:, :], zero[:, :], zero[:, :], ALU.add).then_inc(carried, 1)

            def copy_index(e):
                for q in range(2):
                    pool.tensor_copy(gather_at[q][:, :], route["token"][q][:, bass.ds(e, 1)]).then_inc(index_copied, 1)

            def gather(q, rows):
                n = rows.shape[0]
                pool.indirect_dma_start(rows[:, :], None, dram["x1"],
                                        bass.IndirectOffsetOnAxis(ap=gather_at[q][0:n, 0:1], axis=0)).then_inc(gathered[q], 16)

            def scatter_add(q, rows):
                n = rows.shape[0]
                pool.indirect_dma_start(dram["acc"], bass.IndirectOffsetOnAxis(ap=scatter_at[q][0:n, 0:1], axis=0),
                                        rows[:, :], None, compute_op=ALU.add).then_inc(scattered[q], 16)

            pool.memset(zero[:, :], 0.0).then_inc(zeroed, 1)
            copy_index(0)
            pool.wait_ge(zeroed, 1)
            pool.wait_ge(index_copied, 2)
            gather(0, x_rows)
            gather(1, x_rows_p)

            def step(e, last=False):
                if not last:
                    pool.wait_ge(carried, 5 * e)
                    for q in range(2):
                        pool.wait_ge(gathered[q], 16 * e + 16)
                    pool_carrier()
                    copy_index(e + 1)
                    pool.wait_ge(carried, 5 * e + 1)
                    pool.wait_ge(index_copied, 2 * e + 4)
                    pool.wait_ge(x_turned, 4 * e + 4)
                    pool_carrier()
                    gather(0, x_rows)
                    gather(1, x_rows_p)
                pool.wait_ge(carried, 5 * e + (0 if last else 2))
                pool.wait_ge(ys_scaled, e)
                pool.wait_ge(yp_scaled, e)
                for q in range(2):
                    pool.wait_ge(scattered[q], 16 * e)
                pool_carrier()
                for q in range(2):
                    pool.tensor_copy(scatter_at[q][:, :], route["token"][q][:, bass.ds(e, 1)]).then_inc(lists_copied, 1)
                    pool.tensor_copy(gate_now[q][:, :], route["gate"][q][:, bass.ds(e, 1)]).then_inc(lists_copied, 1)
                pool.wait_ge(carried, 5 * e + (1 if last else 3))
                pool.wait_ge(lists_copied, 4 * e + 4)
                pool.wait_ge(ys_scaled, e + 1)
                pool_carrier()
                scatter_add(0, y_s)
                pool.wait_ge(carried, 5 * e + (2 if last else 4))
                pool.wait_ge(yp_scaled, e + 1)
                pool_carrier()
                scatter_add(1, y_p)

            with pool.Fori(0, N_EXPERTS - 1) as e:
                step(e)
            step(N_EXPERTS - 1, last=True)
            for q in range(2):
                pool.wait_ge(scattered[q], 16 * N_EXPERTS)

        @block.scalar
        def _(act):
            def split(e, c, reuse=True):
                act.wait_ge(loaded[c], 16 * e + 16)
                if reuse:
                    if c in GATE:
                        act.wait_ge(g_done, 4 * (e - 1) + c + 2)
                    elif c in UP:
                        act.wait_ge(u_done, 4 * (e - 1) + c + 1)
                    else:
                        act.wait_ge(first_down_used if c == DOWN[0] else yp_done, e)
                act.activation(w_hi[c][:, :], raw[:, c, :], ACT.Copy).then_inc(hi_done, 1)

            def round_x(e):
                for pair in range(4):
                    act.wait_ge(x_turned, 4 * e + pair + 1)
                    act.activation(xT[:, 2 * pair:2 * pair + 2, 0:N],
                                   ps_turn[pair][:, 0:2 * N].rearrange("p (k t) -> p k t", t=N), ACT.Copy).then_inc(x_hi_done, 1)

            def round_h(e, f):
                act.wait_ge(h_done, 4 * e + f + 1)
                act.activation(hT[:, f, 0:N], h[:, f % 2, :], ACT.Copy).then_inc(h_hi_done, 1)

            round_x(0)
            split(0, experts.EARLY, reuse=False)

            def step(e, first=False, last=False):
                for f in range(FT):
                    act.wait_ge(g_done, 4 * e + f + 1)
                    act.activation(g2[:, f % 2, :], ps_g[:, N:2 * N], ACT.Copy).then_inc(g2_copied, 1)
                    if f:
                        round_h(e, f - 1)
                    if f == 0:
                        split(e, 5, reuse=not first)
                    elif f < 3 and not last:
                        split(e + 1, f - 1)
                    act.wait_ge(g_added, 4 * e + f + 1)
                    act.activation(sg[:, f % 2, :], g[:, f % 2, :], ACT.Silu).then_inc(silu_done, 1)
                    act.wait_ge(u_done, 4 * e + f + 1)
                    act.activation(u2[:, f % 2, :], ps_u[:, N:2 * N], ACT.Copy).then_inc(u2_copied, 1)
                round_h(e, FT - 1)
                if not last:
                    round_x(e + 1)
                    split(e + 1, 2)
                    split(e + 1, 3)
                act.wait_ge(lists_copied, 4 * e + 4)
                act.wait_ge(scattered[0], 16 * e)
                act.wait_ge(ys_done, e + 1)
                act.activation(y_s[:, :], ps_ys[:, :], ACT.Copy, scale=gate_now[0][:, :]).then_inc(ys_scaled, 1)
                if not last:
                    split(e + 1, 4)
                act.wait_ge(yp_done, e + 1)
                act.activation(y_p_rest[:, :], ps_yp[CP:2 * CP, :], ACT.Copy, scale=gate_now[1][CP:2 * CP, :]).then_inc(yp_rest_scaled, 1)

            step(0, first=True)
            with act.Fori(1, N_EXPERTS - 1) as e:
                step(e)
            step(N_EXPERTS - 1, last=True)

        @block.vector
        def _(dve):
            def split(e, c):
                dve.wait_ge(hi_done, N_CHUNKS * e + c + 1)
                nc.vector.tensor_tensor(w_lo[c][:, :], raw[:, c, :], f32(w_hi[c][:, :]), ALU.subtract).then_inc(lo_done, 1)

            def rest_x(e):
                for pair in range(4):
                    dve.wait_ge(x_hi_done, 4 * e + pair + 1)
                    hi = f32(xT[:, 2 * pair:2 * pair + 2, 0:N])
                    nc.vector.tensor_tensor(xT[:, 2 * pair:2 * pair + 2, N:2 * N],
                                            ps_turn[pair][:, 0:2 * N].rearrange("p (k t) -> p k t", t=N), hi,
                                            ALU.subtract).then_inc(x_lo_done, 1)

            def rest_h(e, f):
                dve.wait_ge(h_hi_done, 4 * e + f + 1)
                for cols, at in ((slice(0, CS), N + CP), (slice(CS, N), N)):
                    n = cols.stop - cols.start
                    nc.vector.tensor_tensor(hT[:, f, at:at + n], h[:, f % 2, cols], f32(hT[:, f, cols]),
                                            ALU.subtract).then_inc(h_lo_done, 1)

            rest_x(0)

            def step(e, last=False):
                for f in range(FT):
                    dve.wait_ge(g2_copied, 4 * e + f + 1)
                    nc.vector.tensor_tensor(g[:, f % 2, :], ps_g[:, 0:N], g2[:, f % 2, :], ALU.add).then_inc(g_added, 1)
                    if f:
                        rest_h(e, f - 1)
                    if f < 2:
                        split(e, 4 + f)
                    elif f == 2 and not last:
                        split(e + 1, 0)
                    dve.wait_ge(u2_copied, 4 * e + f + 1)
                    nc.vector.tensor_tensor(u[:, f % 2, :], ps_u[:, 0:N], u2[:, f % 2, :], ALU.add).then_inc(u_added, 1)
                    dve.wait_ge(silu_done, 4 * e + f + 1)
                    dve.wait_ge(u_added, 4 * e + f + 1)
                    nc.vector.tensor_tensor(h[:, f % 2, :], sg[:, f % 2, :], u[:, f % 2, :], ALU.mult).then_inc(h_done, 1)
                rest_h(e, FT - 1)
                if not last:
                    rest_x(e + 1)
                    split(e + 1, 1)
                    split(e + 1, 2)
                    split(e + 1, 3)
                dve.wait_ge(scattered[1], 16 * e)
                dve.wait_ge(yp_rest_scaled, e + 1)
                nc.vector.scalar_tensor_tensor(out=y_p[:, :], in0=ps_yp[0:CP, :], scalar=gate_now[1][0:CP, :], in1=y_p_rest[:, :],
                                               op0=ALU.mult, op1=ALU.add).then_inc(yp_scaled, 1)

            with dve.Fori(0, N_EXPERTS - 1) as e:
                step(e)
            step(N_EXPERTS - 1, last=True)

        @block.tensor
        def _(pe):
            def turn_x(e, first=False):
                for q in range(2):
                    pe.wait_ge(gathered[q], 16 * e + 16)
                if not first:
                    pe.wait_ge(yp_scaled, e - 1)
                for pair in range(4):
                    for k in range(2):
                        src = slice((2 * pair + k) * P, (2 * pair + k + 1) * P)
                        nc.tensor.transpose(ps_turn[pair][:, k * N:k * N + CS], x_rows[:, src], ident[:, :])
                        last = nc.tensor.transpose(ps_turn[pair][:, k * N + CS:(k + 1) * N], x_rows_p[:, src], ident[0:CP, 0:CP])
                    last.then_inc(x_turned, 1)

            def gate_or_up(ps, chunk, f, done):
                for k in range(KD):
                    at = slice(k * HALF + f % 2 * P, k * HALF + (f % 2 + 1) * P)
                    if k == KD - 1:
                        nc.tensor.matmul(ps[:, 0:N], w_lo[chunk][:, at], xT[:, k, 0:N], start=False, stop=False)
                        last = nc.tensor.matmul(ps[:, 0:2 * N], w_hi[chunk][:, at], xT[:, k, :], start=False, stop=True)
                    else:
                        nc.tensor.matmul(ps[:, 0:2 * N], w_hi[chunk][:, at], xT[:, k, :], start=k == 0, stop=False)
                        nc.tensor.matmul(ps[:, 0:N], w_lo[chunk][:, at], xT[:, k, 0:N], start=False, stop=False)
                last.then_inc(done, 1)

            def gate_up(e):
                pe.wait_ge(x_lo_done, 4 * e + 4)
                for f in range(FT):
                    pe.wait_ge(lo_done, N_CHUNKS * e + GATE[f // 2] + 1)
                    pe.wait_ge(g_added, 4 * e + f)
                    gate_or_up(ps_g, GATE[f // 2], f, g_done)
                    pe.wait_ge(lo_done, N_CHUNKS * e + UP[f // 2] + 1)
                    pe.wait_ge(u_added, 4 * e + f)
                    gate_or_up(ps_u, UP[f // 2], f, u_done)

            def down(e, last_expert=False):
                pe.wait_ge(ys_scaled, e)
                hi = slice(0, CS)
                for f in range(FT):
                    pe.wait_ge(h_lo_done, 8 * e + 2 * f + 2)
                    pe.wait_ge(lo_done, N_CHUNKS * e + DOWN[f // 2] + 1)
                    c = DOWN[f // 2]
                    for half in range(2):
                        cols = slice(half * 512, (half + 1) * 512)
                        wd = slice(f % 2 * D + half * 512, f % 2 * D + (half + 1) * 512)
                        last = three_passes(nc, ps_ys[:, cols], hT[:, f, hi], hT[:, f, N + CP:2 * N], w_hi[c][:, wd], w_lo[c][:, wd],
                                            f == 0, f == FT - 1)
                last.then_inc(ys_done, 1)
                if not last_expert:
                    pe.wait_ge(x_lo_done, 4 * e + 8)
                for f in range(FT):
                    for half in range(2):
                        cols = slice(half * 512, (half + 1) * 512)
                        wd = slice(f % 2 * D + half * 512, f % 2 * D + (half + 1) * 512)
                        c = DOWN[f // 2]
                        nc.tensor.matmul(ps_yp[:, cols], hT[:, f, CS:CS + 2 * CP], w_hi[c][:, wd], start=f == 0, stop=False)
                        last = nc.tensor.matmul(ps_yp[:, cols], hT[:, f, CS:CS + 2 * CP], w_lo[c][:, wd], start=False, stop=f == FT - 1)
                    if f == 1:
                        last.then_inc(first_down_used, 1)
                last.then_inc(yp_done, 1)

            turn_x(0, first=True)
            with pe.Fori(0, N_EXPERTS - 1) as e:
                gate_up(e)
                turn_x(e + 1)
                down(e)
            gate_up(N_EXPERTS - 1)
            down(N_EXPERTS - 1, last_expert=True)


def phase_norm(nc, dram):
    with ExitStack() as ctx:
        m = Scope(nc, ctx)
        SLOTS = 4
        TURNS, SAMPLE_TURNS = N_TILES // SLOTS, SAMPLE_TILES // SLOTS
        a, y = m.sb("acc_in", [P, SLOTS, D]), m.sb("y", [P, SLOTS, D])
        ln_g, ln_b = m.sb("ln2_g_all", [P, D]), m.sb("ln2_b_all", [P, D])
        stats, moments, rstd = m.sb("ln2_stats", [P, SLOTS, 2, 6]), m.sb("ln2_moments", [P, SLOTS, 2]), m.sb("ln2_rstd", [P, SLOTS])
        half_neg, eps, carrier = m.sb("e_minus_half", [P, 1]), m.sb("e_eps", [P, 1]), m.sb("e_wait_carrier", [P, 1])
        loaded, stored = [m.sem(f"e_loaded{s}") for s in range(SLOTS)], [m.sem(f"e_stored{s}") for s in range(SLOTS)]
        consts_loaded, filled, stats_part, stats_done, eps_added, rstd_done, centred, scaled, y_done = (
            m.sem("e_" + x) for x in ("consts_loaded", "filled", "stats_part", "stats_done", "eps_added", "rstd_done", "centred", "scaled", "y_done"))
        block = ctx.enter_context(nc.Block())

        @block.sync
        def _(sp):
            def load(i, b):
                sp.dma_start(a[:, b, :], dram["acc"][bass.ds((SLOTS * i + b) * P, P), :]).then_inc(loaded[b], 16)

            load(0, 0)
            load(0, 1)
            sp.dma_start(ln_g[:, :], dram["ln2_g"].partition_broadcast(P)).then_inc(consts_loaded, 16)
            sp.dma_start(ln_b[:, :], dram["ln2_b"].partition_broadcast(P)).then_inc(consts_loaded, 16)
            load(0, 2)
            load(0, 3)

            def step(i, dst, first_row, last=False):
                for b in range(SLOTS):
                    t = SLOTS * i + b
                    if not last:
                        sp.wait_ge(scaled, t + 1)
                        load(i + 1, b)
                    sp.wait_ge(y_done, t + 1)
                    sp.dma_start(dst[bass.ds(t * P - first_row, P), :], y[:, b, :]).then_inc(stored[b], 16)

            with sp.Fori(0, SAMPLE_TURNS) as i:
                step(i, dram["y_sample"], 0)
            for i in range(SAMPLE_TURNS, TURNS):
                step(i, dram["y_prompt"], S_SAMPLE, last=i == TURNS - 1)
            for b in range(SLOTS):
                sp.wait_ge(stored[b], 16 * TURNS)

        @block.gpsimd
        def _(pool):
            pool.memset(half_neg[:, :], -0.5).then_inc(filled, 1)
            pool.memset(eps[:, :], LN_EPS).then_inc(filled, 1)
            pool.wait_ge(filled, 2)
            pool.wait_ge(consts_loaded, 32)

            def reciprocal_std(t, b):
                pool.wait_ge(stats_done, t + 1)
                pool.tensor_tensor(rstd[:, b:b + 1], moments[:, b, 1:2], eps[:, :], ALU.add).then_inc(eps_added, 1)
                pool.wait_ge(eps_added, t + 1)
                pool.tensor_tensor(rstd[:, b:b + 1], rstd[:, b:b + 1], half_neg[:, :], ALU.pow).then_inc(rstd_done, 1)

            def step(i, last=False):
                for b in range(SLOTS):
                    t = SLOTS * i + b
                    if not (last and b == SLOTS - 1):
                        reciprocal_std(t + 1, (b + 1) % SLOTS)
                    pool.wait_ge(scaled, t + 1)
                    pool.tensor_tensor(y[:, b, :], y[:, b, :], ln_b[:, :], ALU.add).then_inc(y_done, 1)

            reciprocal_std(0, 0)
            with pool.Fori(0, TURNS - 1) as i:
                step(i)
            step(TURNS - 1, last=True)

        @block.vector
        def _(dve):
            def statistics(i, b):
                t = SLOTS * i + b
                dve.wait_ge(loaded[b], 16 * i + 16)
                for h in range(2):
                    nc.vector.bn_stats(stats[:, b, h, :], a[:, b, h * 512:(h + 1) * 512]).then_inc(stats_part, 1)
                dve.wait_ge(stats_part, 2 * t + 2)
                wait_carrier(nc, carrier)
                nc.vector.bn_aggr(moments[:, b, :], stats[:, b, :, :].rearrange("p h c -> p (h c)")).then_inc(stats_done, 1)

            def step(i, last=False):
                for b in range(SLOTS):
                    t = SLOTS * i + b
                    if b < SLOTS - 1:
                        statistics(i, b + 1)
                    elif not last:
                        statistics(i + 1, 0)
                    dve.wait_ge(rstd_done, t + 1)
                    nc.vector.tensor_scalar(a[:, b, :], a[:, b, :], moments[:, b, 0:1], rstd[:, b:b + 1],
                                            ALU.subtract, ALU.mult).then_inc(centred, 1)
                    dve.wait_ge(stored[b], 16 * i)
                    dve.wait_ge(centred, t + 1)
                    nc.vector.tensor_tensor(y[:, b, :], a[:, b, :], ln_g[:, :], ALU.mult).then_inc(scaled, 1)

            dve.wait_ge(consts_loaded, 32)
            statistics(0, 0)
            with dve.Fori(0, TURNS - 1) as i:
                step(i)
            step(TURNS - 1, last=True)


def constants():
    inv = (1.0 / (np.float32(10000.0) ** (np.arange(0, ROPE, 2, dtype=np.float32) / np.float32(ROPE)))).astype(np.float32)
    ang = (np.arange(S_SAMPLE, dtype=np.float32)[:, None] * inv[None, :]).astype(np.float64)
    cos, sin = np.cos(ang), np.sin(ang)
    by_tile = lambda a: np.ascontiguousarray(a.reshape(SAMPLE_TILES, P, ROPE).transpose(1, 0, 2), np.float32)
    q_table = np.concatenate([cos, cos, -sin, sin, np.ones((S_SAMPLE, NOPE))], axis=1).T * SCALE
    inv_count = np.zeros((len(POOL_WINDOWS), T), np.float32)
    for start, n in ((0, S_SAMPLE), (S_SAMPLE, S_PROMPT)):
        pos = np.arange(n)
        for g, w in enumerate(POOL_WINDOWS):
            count = np.clip(pos + w // 2 - 1, 0, n - 1) - np.clip(pos - w // 2, 0, n - 1) + 1
            inv_count[g, start:start + n] = 1.0 / count
    return {
        "rope_cos": by_tile(np.concatenate([cos, cos], axis=1)),
        "rope_sin": by_tile(np.concatenate([sin, -sin], axis=1)),
        "q_table": np.ascontiguousarray(q_table, np.float32),
        "inv_count": inv_count,
    }


INPUTS = {
    "x_sample": (S_SAMPLE, D), "x_prompt": (S_PROMPT, D), "ln_in_g": (D,), "ln_in_b": (D,),
    "w_in": (D, IN_DIM), "w_pool": (4, GROUP, GROUP), "pool_scale": (POOL_DIM,), "q_norm_g": (Q_RANK,),
    "w_uq": (Q_RANK, N_HEADS * QK), "kv_norm_g": (KV_RANK,), "w_ukv": (KV_RANK, N_HEADS * (NOPE + V_DIM)),
    "w_o": (D, D), "ln1_g": (D,), "ln1_b": (D,), "w_router": (D, N_EXPERTS),
    "w_gate": (N_EXPERTS, D, FFN), "w_up": (N_EXPERTS, D, FFN), "w_down": (N_EXPERTS, FFN, D),
    "ln2_g": (D,), "ln2_b": (D,),
}
SCRATCH = {
    "x0": (T, D), "uT": (POOL_DIM, T), "qT": (Q_RANK, T), "kvT": (KV_RANK, T), "krT": (P, T), "v": (T, 512), "dT": (POOL_DIM, T),
    "mixT": (D, T), "x1": (T, D), "acc": (T, D),
}


def build(nc, phases="ABCDE"):
    dram = {}
    for name, shape in INPUTS.items():
        dram[name] = nc.dram_tensor("in_" + name, shape, F32, kind="ExternalInput").ap()
    for name, a in constants().items():
        dram[name] = nc.dram_tensor("in_" + name, a.shape, F32, kind="ExternalInput").ap()
    for name, shape in SCRATCH.items():
        dram[name] = nc.dram_tensor("scratch_" + name, shape, F32).ap()
    dram["y_prompt"] = nc.dram_tensor("y_prompt", (S_PROMPT, D), F32, kind="ExternalOutput").ap()
    dram["y_sample"] = nc.dram_tensor("y_sample", (S_SAMPLE, D), F32, kind="ExternalOutput").ap()
    with ExitStack() as ctx:
        m = Scope(nc, ctx)
        ident = m.sb("ident", [P, P])
        ident_zero = m.sem("ident_zero")
        with nc.Block() as block:
            @block.gpsimd
            def _(pool):
                pool.memset(ident[:, :], 0.0).then_inc(ident_zero, 1)
                pool.wait_ge(ident_zero, 1)
                pool.affine_select(out=ident[:, :], in_=ident[:, :], compare_op=ALU.not_equal, fill=1.0, base=0,
                                   pattern=[[-1, P]], channel_multiplier=1).then_inc(ident_zero, 1)
        if "A" in phases:
            phase_project(nc, ident, dram)
        if "B" in phases:
            phase_attention(nc, ident, dram)
        route = {"token": [m.sb(f"route_token{q}", [P, N_EXPERTS], U32) for q in range(2)],
                 "gate": [m.sb(f"route_gate{q}", [P, N_EXPERTS]) for q in range(2)]}
        experts = ExpertWeights(m, dram)
        if "C" in phases:
            phase_mix(nc, ident, dram, route, experts)
        if "D" in phases:
            phase_experts(nc, ident, dram, route, experts)
        if "E" in phases:
            phase_norm(nc, dram)


def kernel(**inputs):
    from concourse import bacc
    from concourse.bass_utils import run_bass_kernel_spmd

    nc = bacc.Bacc("TRN2", target_bir_lowering=False, num_devices=1)
    build(nc)
    arrays = {"in_" + name: np.ascontiguousarray(inputs[name]).reshape(shape) for name, shape in INPUTS.items()}
    arrays.update({"in_" + name: a for name, a in constants().items()})
    r = run_bass_kernel_spmd(nc, [arrays], core_ids=[0])
    out = r.results[0]
    return out["y_prompt"].reshape(1, S_PROMPT, D), out["y_sample"].reshape(1, S_SAMPLE, D)
```

```python
from contextlib import ExitStack

import concourse.bass as bass
from concourse import mybir
import numpy as np

F32, F32R, U32, I32 = mybir.dt.float32, mybir.dt.float32r, mybir.dt.uint32, mybir.dt.int32
ALU, ACT, AX = mybir.AluOpType, mybir.ActivationFunctionType, mybir.AxisListType

P = 128
D = 1024
S_SAMPLE, S_PROMPT = 1024, 512
T = S_SAMPLE + S_PROMPT
N_TILES = T // P
SAMPLE_TILES = S_SAMPLE // P
POOL_WINDOWS = (2, 4, 8, 16)
POOL_DIM, GROUP = 512, 128
N_HEADS, NOPE, ROPE, V_DIM = 8, 64, 32, 64
QK = NOPE + ROPE
Q_RANK, KV_RANK = 384, 256
IN_DIM = POOL_DIM + Q_RANK + KV_RANK + ROPE
N_EXPERTS, FFN = 16, 512
CAP_SAMPLE, CAP_PROMPT = 2 * S_SAMPLE // N_EXPERTS, 2 * S_PROMPT // N_EXPERTS
LN_EPS, RMS_EPS = 1e-5, 1e-6
ALPHA = 2.0 ** 0.25
SCALE = 1.0 / float(np.sqrt(QK))
KD = D // P
QT_, KVT_ = Q_RANK // P, KV_RANK // P



class Scope:

    def __init__(self, nc, ctx):
        self.nc, self.ctx, self.sems = nc, ctx, []

    def sb(self, name, shape, dt=F32):
        return self.ctx.enter_context(self.nc.sbuf_tensor(name, shape, dt))

    def ps(self, name, shape=(P, 512)):
        return self.ctx.enter_context(self.nc.psum_tensor(name, list(shape), F32))

    def sem(self, name):
        self.sems.append(self.ctx.enter_context(self.nc.semaphore(name)))
        return self.sems[-1]

    def clear_semaphores(self):
        numbers = sorted(s.num for s in self.sems)
        with self.nc.Block() as block:
            @block.gpsimd
            def _(pool):
                start = numbers[0]
                for n, after in zip(numbers, numbers[1:] + [None]):
                    if after != n + 1:
                        pool.sem_clear(range(start, n + 1))
                        start = after


def three_passes(nc, out, a_hi, a_lo, b_hi, b_lo, first, last):
    nc.tensor.matmul(out, a_hi, b_hi, start=first, stop=False)
    nc.tensor.matmul(out, a_hi, b_lo, start=False, stop=False)
    return nc.tensor.matmul(out, a_lo, b_hi, start=False, stop=last)


def wait_carrier(nc, cell):
    nc.vector.memset(cell[:, :], 0.0)


def f32(ap):
    return ap.bitcast(F32)


def phase_project(nc, ident, dram):
    with ExitStack() as ctx:
        m = Scope(nc, ctx)
        x_in = m.sb("x_in", [P, 2, D])
        x0 = m.sb("x0", [P, 2, D])
        ln_g, ln_b = m.sb("ln_in_g_all", [P, D]), m.sb("ln_in_b_all", [P, D])
        x0T_hi = [m.sb(f"x0T_hi{s}", [P, KD, 2 * P], F32R) for s in range(2)]
        x0T_lo = [m.sb(f"x0T_lo{s}", [P, KD, 2 * P], F32R) for s in range(2)]
        RING = 5
        w_raw = m.sb("w_in_raw", [P, RING, IN_DIM])
        w_hi, w_lo = m.sb("w_in_hi", [P, KD, IN_DIM], F32R), m.sb("w_in_lo", [P, KD, IN_DIM], F32R)
        wv_hi, wv_lo = m.sb("w_v_hi", [P, KVT_, 512], F32R), m.sb("w_v_lo", [P, KVT_, 512], F32R)
        stats, moments = m.sb("ln_stats", [P, 2, 2, 6]), m.sb("ln_moments", [P, 2, 2])
        rstd = m.sb("ln_rstd", [P, 2])
        half_neg = m.sb("minus_half", [P, 2])
        eps = m.sb("eps_ln_rms_rms", [P, 3])
        carrier = m.sb("wait_carrier", [P, 1])
        squares = m.sb("squares_unused", [P, Q_RANK])
        mean_sq, rms = m.sb("lat_mean_sq", [P, 2, 2]), m.sb("lat_rms", [P, 2, 2])
        lat = m.sb("lat_scaled", [P, 2, Q_RANK + KV_RANK])
        rope_cos, rope_sin = m.sb("rope_cos", [P, SAMPLE_TILES, ROPE]), m.sb("rope_sin", [P, SAMPLE_TILES, ROPE])
        kr_cos, kr_sin = m.sb("kr_cos", [P, 2, ROPE]), m.sb("kr_sin", [P, 2, ROPE])
        k_rope = m.sb("k_rope_twice", [P, 2, P])
        q_g, kv_g = m.sb("q_norm_gain", [P, QT_]), m.sb("kv_norm_gain", [P, KVT_])
        qT, kvT = m.sb("qT", [P, QT_, 2 * P]), m.sb("kvT", [P, KVT_, 2 * P])
        kvT_hi, kvT_lo = m.sb("kvT_hi", [P, 2, KVT_, P], F32R), m.sb("kvT_lo", [P, 2, KVT_, P], F32R)
        krT = m.sb("krT", [P, 2 * P])
        uT = m.sb("uT", [P, 4, 2 * P])
        v_out = m.sb("v_out", [P, 2, 512])

        ps_tr = [m.ps(f"ps_transpose{b}") for b in range(2)]
        ps_lat = [m.ps(f"ps_lat{b}") for b in range(2)]
        ps_u = [m.ps(f"ps_u{b}") for b in range(2)]
        ps_qr, ps_kv = m.ps("ps_latT_q_rope"), m.ps("ps_latT_kv")

        x_loaded = [m.sem(f"a_x_loaded{s}") for s in range(2)]
        consts_loaded, ln_loaded = m.sem("a_consts_loaded"), m.sem("a_ln_loaded")
        w_loaded = [m.sem(f"a_w_loaded{s}") for s in range(RING)]
        w_hi_done, w_lo_done = m.sem("a_w_hi_done"), m.sem("a_w_lo_done")
        stats_part, stats_done = m.sem("a_stats_part"), m.sem("a_stats_done")
        eps_added, rstd_done = m.sem("a_eps_added"), m.sem("a_rstd_done")
        x_centred, x_scaled, x0_done = m.sem("a_x_centred"), m.sem("a_x_scaled"), m.sem("a_x0_done")
        x0_stored = [m.sem(f"a_x0_stored{s}") for s in range(2)]
        tr_done, tr_hi_done, tr_lo_done = m.sem("a_tr_done"), m.sem("a_tr_hi_done"), m.sem("a_tr_lo_done")
        lat_done, sq_done, rms_eps, rms_done = m.sem("a_lat_done"), m.sem("a_sq_done"), m.sem("a_rms_eps"), m.sem("a_rms_done")
        lat_scaled, kr_products = m.sem("a_lat_scaled"), m.sem("a_kr_products")
        u_done, u_copied, u_stored = m.sem("a_u_done"), m.sem("a_u_copied"), m.sem("a_u_stored")
        latT_done, latT_scaled = m.sem("a_latT_done"), m.sem("a_latT_scaled")
        kr_copied, kv_hi_done, kv_lo_done = m.sem("a_kr_copied"), m.sem("a_kv_hi_done"), m.sem("a_kv_lo_done")
        v_done, v_copied = m.sem("a_v_done"), m.sem("a_v_copied")
        v_stored = [m.sem(f"a_v_stored{s}") for s in range(2)]
        q_stored, kv_stored, kr_stored = m.sem("a_q_stored"), m.sem("a_kv_stored"), m.sem("a_kr_stored")
        filled = m.sem("a_filled")

        N_BLOCKS = N_TILES // 2
        PAIRS = N_BLOCKS // 2
        X0T_AFTER = (3, 6)
        SPLIT = Q_RANK

        ctx.callback(m.clear_semaphores)
        block = ctx.enter_context(nc.Block())

        @block.sync
        def _(sp):
            def load_x(rows, s):
                sp.dma_start(x_in[:, s, :], rows).then_inc(x_loaded[s], 16)

            for s in range(2):
                load_x(dram["x_sample"][s * P:(s + 1) * P, :], s)
            w_ukv_v = dram["w_ukv"].rearrange("(t p) (h c) -> t p h c", p=P, c=NOPE + V_DIM)

            def load_w(c):
                if c >= RING:
                    sp.wait_ge(w_lo_done, c - RING + 1)
                if c < KD:
                    sp.dma_start(w_raw[:, c % RING, :], dram["w_in"][c * P:(c + 1) * P, :]).then_inc(w_loaded[c % RING], 16)
                else:
                    dst = w_raw[:, c % RING, 0:512].rearrange("p (h v) -> p h v", v=V_DIM)
                    sp.dma_start(dst, w_ukv_v[c - KD][:, :, NOPE:]).then_inc(w_loaded[c % RING], 16)

            for dst, name in ((ln_g, "ln_in_g"), (ln_b, "ln_in_b")):
                sp.dma_start(dst[:, :], dram[name].partition_broadcast(P)).then_inc(ln_loaded, 16)
            for c in range(RING):
                load_w(c)
            sp.dma_start(rope_cos[:, :, :], dram["rope_cos"]).then_inc(consts_loaded, 16)
            sp.dma_start(rope_sin[:, :, :], dram["rope_sin"]).then_inc(consts_loaded, 16)
            with nc.allow_non_contiguous_dma("a gain per partition, once"):
                sp.dma_start(q_g[:, :], dram["q_norm_g"].rearrange("(t p) -> p t", p=P)).then_inc(consts_loaded, 16)
                sp.dma_start(kv_g[:, :], dram["kv_norm_g"].rearrange("(t p) -> p t", p=P)).then_inc(consts_loaded, 16)
            for c in range(RING, KD + KVT_):
                load_w(c)

            def rows_known(t):
                name, t = ("x_sample", t) if t < SAMPLE_TILES else ("x_prompt", t - SAMPLE_TILES)
                return dram[name][t * P:(t + 1) * P, :]

            def step(i, rows_of_tile, last=False):
                for b in range(2):
                    j = 2 * i + b
                    if not (last and b == 1):
                        for s in range(2):
                            sp.wait_ge(x_centred, 2 * j + s + 1)
                            load_x(rows_of_tile(2 * j + 2 + s), s)
                    for s in range(2):
                        sp.wait_ge(x0_done, 2 * j + s + 1)
                        sp.dma_start(dram["x0"][bass.ds((2 * j + s) * P, P), :], x0[:, s, :]).then_inc(x0_stored[s], 16)
                    cols = bass.ds(j * 2 * P, 2 * P)
                    sp.wait_ge(u_copied, 2 * j + 2)
                    sp.dma_start(dram["uT"].rearrange("(g p) t -> p g t", p=P)[:, :, cols], uT[:, :, :]).then_inc(u_stored, 16)
                    sp.wait_ge(latT_scaled, 4 * j + 4)
                    sp.dma_start(dram["qT"].rearrange("(g p) t -> p g t", p=P)[:, :, cols], qT[:, :, :]).then_inc(q_stored, 16)
                    sp.dma_start(dram["kvT"].rearrange("(g p) t -> p g t", p=P)[:, :, cols], kvT[:, :, :]).then_inc(kv_stored, 16)
                    sp.wait_ge(kr_copied, 2 * j + 2)
                    sp.dma_start(dram["krT"][:, cols], krT[:, :]).then_inc(kr_stored, 16)
                    for s in range(2):
                        sp.wait_ge(v_copied, 2 * j + s + 1)
                        sp.dma_start(dram["v"][bass.ds((2 * j + s) * P, P), :], v_out[:, s, :]).then_inc(v_stored[s], 16)

            with sp.Fori(0, PAIRS - 2) as i:
                step(i, lambda t: dram["x_sample"][bass.ds(t * P, P), :])
            for i in range(PAIRS - 2, PAIRS):
                step(i, rows_known, last=i == PAIRS - 1)
            for s in range(2):
                sp.wait_ge(x0_stored[s], 16 * N_BLOCKS)
                sp.wait_ge(v_stored[s], 16 * N_BLOCKS)
            for sem in (u_stored, q_stored, kv_stored, kr_stored):
                sp.wait_ge(sem, 16 * N_BLOCKS)

        @block.gpsimd
        def _(pool):
            pool.memset(half_neg[:, :], -0.5).then_inc(filled, 1)
            pool.memset(eps[:, 0:1], LN_EPS).then_inc(filled, 1)
            pool.memset(eps[:, 1:3], RMS_EPS).then_inc(filled, 1)
            pool.memset(k_rope[:, :, :], 0.0).then_inc(filled, 1)

            def reciprocal_std(j, s):
                pool.wait_ge(stats_done, 2 * j + s + 1)
                pool.tensor_tensor(rstd[:, s:s + 1], moments[:, s, 1:2], eps[:, 0:1], ALU.add).then_inc(eps_added, 1)
                pool.wait_ge(eps_added, 2 * j + s + 1)
                pool.tensor_tensor(rstd[:, s:s + 1], rstd[:, s:s + 1], half_neg[:, 0:1], ALU.pow).then_inc(rstd_done, 1)

            def add_bias(j, s):
                pool.wait_ge(x_scaled, 2 * j + s + 1)
                pool.tensor_tensor(x0[:, s, :], x0[:, s, :], ln_b[:, :], ALU.add).then_inc(x0_done, 1)

            def latent_rms(j, s):
                pool.wait_ge(sq_done, 2 * (2 * j + s + 1))
                pool.tensor_tensor(rms[:, s, :], mean_sq[:, s, :], eps[:, 1:3], ALU.add).then_inc(rms_eps, 1)
                pool.wait_ge(rms_eps, 2 * j + s + 1)
                pool.tensor_tensor(rms[:, s, :], rms[:, s, :], half_neg[:, :], ALU.pow).then_inc(rms_done, 1)

            pool.wait_ge(filled, 4)
            for s in range(2):
                reciprocal_std(0, s)
            pool.wait_ge(ln_loaded, 32)
            for s in range(2):
                add_bias(0, s)

            def step(i, last=False):
                for b in range(2):
                    j = 2 * i + b
                    more = not (last and b == 1)
                    if more:
                        reciprocal_std(j + 1, 0)
                        reciprocal_std(j + 1, 1)
                    latent_rms(j, 0)
                    if more:
                        add_bias(j + 1, 0)
                        add_bias(j + 1, 1)
                    latent_rms(j, 1)

            with pool.Fori(0, PAIRS - 1) as i:
                step(i)
            step(PAIRS - 1, last=True)

        @block.scalar
        def _(act):
            def round_x0T(j, s, slot):
                for h in range(2):
                    act.wait_ge(tr_done, 2 * (2 * j + s) + h + 1)
                    act.activation(x0T_hi[slot][:, 4 * h:4 * h + 4, s * P:(s + 1) * P],
                                   ps_tr[h][:, :].rearrange("p (k t) -> p k t", t=P), ACT.Copy).then_inc(tr_hi_done, 1)

            for c in range(KD + KVT_):
                act.wait_ge(w_loaded[c % RING], 16 * (c // RING + 1))
                if c < KD:
                    act.activation(w_hi[:, c, :], w_raw[:, c % RING, :], ACT.Copy).then_inc(w_hi_done, 1)
                else:
                    act.activation(wv_hi[:, c - KD, :], w_raw[:, c % RING, 0:512], ACT.Copy).then_inc(w_hi_done, 1)
                if c in X0T_AFTER:
                    round_x0T(0, X0T_AFTER.index(c), 0)

            def square(j, s):
                act.wait_ge(lat_done, 2 * (2 * j + s) + 1)
                act.wait_ge(sq_done, 2 * (2 * j + s))
                act.activation(squares[:, :], ps_lat[0][:, 0:Q_RANK], ACT.Square, scale=Q_RANK ** -0.5,
                               accum_out=mean_sq[:, s, 0:1]).then_inc(sq_done, 1)
                act.wait_ge(lat_done, 2 * (2 * j + s) + 2)
                act.wait_ge(sq_done, 2 * (2 * j + s) + 1)
                act.activation(squares[:, 0:KV_RANK], ps_lat[1][:, 0:KV_RANK], ACT.Square, scale=KV_RANK ** -0.5,
                               accum_out=mean_sq[:, s, 1:2]).then_inc(sq_done, 1)

            def copy_u(j, h):
                act.wait_ge(u_done, 2 * j + h + 1)
                act.wait_ge(u_stored, 16 * j)
                act.activation(uT[:, 2 * h:2 * h + 2, :], ps_u[h][:, :].rearrange("p (g t) -> p g t", g=2),
                               ACT.Copy).then_inc(u_copied, 1)

            def copy_latT(j, s):
                act.wait_ge(latT_scaled, 2 * (2 * j + s) + 2)
                act.activation(kvT_hi[:, s, :, :], kvT[:, :, s * P:(s + 1) * P], ACT.Copy).then_inc(kv_hi_done, 1)
                act.wait_ge(kr_stored, 16 * j)
                act.activation(krT[:, s * P:(s + 1) * P], ps_qr[:, Q_RANK:Q_RANK + P], ACT.Copy).then_inc(kr_copied, 1)

            def copy_v(j, s):
                act.wait_ge(v_done, 2 * j + s + 1)
                act.wait_ge(v_stored[s], 16 * j)
                act.activation(v_out[:, s, :], ps_lat[s][:, :], ACT.Copy).then_inc(v_copied, 1)

            def step(i, last=False):
                for b in range(2):
                    j = 2 * i + b
                    for s in range(2):
                        square(j, s)
                        copy_u(j, s)
                        copy_latT(j, s)
                        if not (last and b == 1):
                            round_x0T(j + 1, s, 1 - b)
                    for s in range(2):
                        copy_v(j, s)

            with act.Fori(0, PAIRS - 1) as i:
                step(i)
            step(PAIRS - 1, last=True)

        @block.vector
        def _(dve):
            def statistics(j, s):
                dve.wait_ge(x_loaded[s], 16 * (j + 1))
                if not (isinstance(j, int) and j == 0):
                    dve.wait_ge(eps_added, 2 * j + s - 1)
                    dve.wait_ge(x_centred, 2 * j + s - 1)
                for h in range(2):
                    nc.vector.bn_stats(stats[:, s, h, :], x_in[:, s, h * 512:(h + 1) * 512]).then_inc(stats_part, 1)
                dve.wait_ge(stats_part, 2 * (2 * j + s) + 2)
                wait_carrier(nc, carrier)
                nc.vector.bn_aggr(moments[:, s, :], stats[:, s, :, :].rearrange("p h c -> p (h c)")).then_inc(stats_done, 1)

            def normalise(j, s):
                dve.wait_ge(rstd_done, 2 * j + s + 1)
                if not (isinstance(j, int) and j == 0):
                    dve.wait_ge(tr_done, 2 * (2 * j + s - 1))
                    dve.wait_ge(x0_stored[s], 16 * j)
                nc.vector.tensor_scalar(x0[:, s, :], x_in[:, s, :], moments[:, s, 0:1], rstd[:, s:s + 1],
                                        ALU.subtract, ALU.mult).then_inc(x_centred, 1)
                dve.wait_ge(x_centred, 2 * j + s + 1)
                nc.vector.tensor_tensor(x0[:, s, :], x0[:, s, :], ln_g[:, :], ALU.mult).then_inc(x_scaled, 1)

            def rest_x0T(j, s, slot):
                for h in range(2):
                    dve.wait_ge(tr_hi_done, 2 * (2 * j + s) + h + 1)
                    hi = x0T_hi[slot][:, 4 * h:4 * h + 4, s * P:(s + 1) * P]
                    nc.vector.tensor_tensor(x0T_lo[slot][:, 4 * h:4 * h + 4, s * P:(s + 1) * P],
                                            ps_tr[h][:, :].rearrange("p (k t) -> p k t", t=P), f32(hi),
                                            ALU.subtract).then_inc(tr_lo_done, 1)

            def scale_latents(j, s, position):
                dve.wait_ge(rms_done, 2 * j + s + 1)
                t = 2 * j + s
                nc.vector.tensor_scalar(lat[:, s, 0:Q_RANK], ps_lat[0][:, 0:Q_RANK], rms[:, s, 0:1], None,
                                        ALU.mult).then_inc(lat_scaled, 1)
                nc.vector.tensor_scalar(lat[:, s, Q_RANK:], ps_lat[1][:, 0:KV_RANK], rms[:, s, 1:2], None,
                                        ALU.mult).then_inc(lat_scaled, 1)
                raw = ps_lat[1][:, KV_RANK:KV_RANK + ROPE]
                cos = rope_cos[:, bass.ds(position, 1), :].rearrange("p a c -> p (a c)")
                sin = rope_sin[:, bass.ds(position, 1), :].rearrange("p a c -> p (a c)")
                nc.vector.tensor_tensor(kr_cos[:, s, :], raw, cos, ALU.mult).then_inc(kr_products, 1)
                nc.vector.tensor_tensor(kr_sin[:, s, :], raw, sin, ALU.mult).then_inc(kr_products, 1)
                dve.wait_ge(kr_products, 2 * t + 2)
                half = ROPE // 2
                both = k_rope[:, s, :].rearrange("p (d c) -> p d c", d=2)
                for h in range(2):
                    a = kr_cos[:, s:s + 1, h * half:(h + 1) * half].to_broadcast([P, 2, half])
                    b = kr_sin[:, s:s + 1, (1 - h) * half:(2 - h) * half].to_broadcast([P, 2, half])
                    nc.vector.tensor_tensor(both[:, :, h * half:(h + 1) * half], a, b, ALU.add).then_inc(lat_scaled, 1)

            def scale_latT(j, s):
                t = 2 * j + s
                dve.wait_ge(latT_done, t + 1)
                dve.wait_ge(q_stored, 16 * j)
                dve.wait_ge(kv_stored, 16 * j)
                nc.vector.tensor_tensor(qT[:, :, s * P:(s + 1) * P], ps_qr[:, 0:Q_RANK].rearrange("p (k t) -> p k t", t=P),
                                        q_g[:, :].unsqueeze(2).to_broadcast([P, QT_, P]), ALU.mult).then_inc(latT_scaled, 1)
                nc.vector.tensor_tensor(kvT[:, :, s * P:(s + 1) * P], ps_kv[:, 0:KV_RANK].rearrange("p (k t) -> p k t", t=P),
                                        kv_g[:, :].unsqueeze(2).to_broadcast([P, KVT_, P]), ALU.mult).then_inc(latT_scaled, 1)
                dve.wait_ge(kv_hi_done, t + 1)
                nc.vector.tensor_tensor(kvT_lo[:, s, :, :], kvT[:, :, s * P:(s + 1) * P], f32(kvT_hi[:, s, :, :]),
                                        ALU.subtract).then_inc(kv_lo_done, 1)

            for s in range(2):
                statistics(0, s)
            dve.wait_ge(filled, 4)
            dve.wait_ge(ln_loaded, 32)
            for s in range(2):
                normalise(0, s)
            for c in range(KD + KVT_):
                dve.wait_ge(w_hi_done, c + 1)
                if c < KD:
                    nc.vector.tensor_tensor(w_lo[:, c, :], w_raw[:, c % RING, :], f32(w_hi[:, c, :]),
                                            ALU.subtract).then_inc(w_lo_done, 1)
                else:
                    nc.vector.tensor_tensor(wv_lo[:, c - KD, :], w_raw[:, c % RING, 0:512], f32(wv_hi[:, c - KD, :]),
                                            ALU.subtract).then_inc(w_lo_done, 1)
                if c in X0T_AFTER:
                    rest_x0T(0, X0T_AFTER.index(c), 0)
            dve.wait_ge(consts_loaded, 64)

            def step(i, positions, last=False):
                for b in range(2):
                    j = 2 * i + b
                    more = not (last and b == 1)
                    if more:
                        statistics(j + 1, 0)
                        statistics(j + 1, 1)
                        normalise(j + 1, 0)
                    scale_latents(j, 0, positions + 2 * b)
                    if more:
                        normalise(j + 1, 1)
                    for s in range(2):
                        if s:
                            scale_latents(j, 1, positions + 2 * b + 1)
                        scale_latT(j, s)
                        if more:
                            rest_x0T(j + 1, s, 1 - b)

            with dve.Fori(0, PAIRS - 1) as i:
                step(i, 4 * i)
            step(PAIRS - 1, 0, last=True)

        @block.tensor
        def _(pe):
            def transpose_x0(j, s):
                pe.wait_ge(x0_done, 2 * j + s + 1)
                for h in range(2):
                    t = 2 * j + s
                    if not (isinstance(t, int) and t == 0):
                        pe.wait_ge(tr_lo_done, 2 * t + h - 1)
                    for k in range(4):
                        last = nc.tensor.transpose(ps_tr[h][:, k * P:(k + 1) * P],
                                                   x0[:, s, (4 * h + k) * P:(4 * h + k + 1) * P], ident[:, :])
                    last.then_inc(tr_done, 1)

            def latents(j, s, slot):
                t = 2 * j + s
                pe.wait_ge(tr_lo_done, 4 * j + 2 * s + 2)
                pe.wait_ge(lat_scaled, 4 * t)
                pe.wait_ge(kr_products, 2 * t)
                for h, (c0, c1) in enumerate(((POOL_DIM, POOL_DIM + SPLIT), (POOL_DIM + SPLIT, IN_DIM))):
                    if s == 0 and not (isinstance(j, int) and j == 0):
                        pe.wait_ge(v_copied, 2 * j - 1 + h)
                    for k in range(KD):
                        if isinstance(t, int) and t == 0 and h == 0:
                            pe.wait_ge(w_lo_done, k + 1)
                        a_hi, a_lo = (x[slot][:, k, s * P:(s + 1) * P] for x in (x0T_hi, x0T_lo))
                        last = three_passes(nc, ps_lat[h][:, 0:c1 - c0], a_hi, a_lo,
                                            w_hi[:, k, c0:c1], w_lo[:, k, c0:c1], k == 0, k == KD - 1)
                    last.then_inc(lat_done, 1)

            def pool_inputs(j, h, slot):
                pe.wait_ge(u_copied, 2 * j)
                for g in range(2):
                    c0 = (2 * h + g) * P
                    for k in range(KD):
                        last = three_passes(nc, ps_u[h][:, g * 2 * P:(g + 1) * 2 * P],
                                            w_hi[:, k, c0:c0 + P], w_lo[:, k, c0:c0 + P],
                                            x0T_hi[slot][:, k, :], x0T_lo[slot][:, k, :], k == 0, k == KD - 1)
                last.then_inc(u_done, 1)

            def transpose_latents(j, s):
                t = 2 * j + s
                pe.wait_ge(lat_scaled, 4 * t + 4)
                if not (isinstance(t, int) and t == 0):
                    pe.wait_ge(kr_copied, t)
                    pe.wait_ge(latT_scaled, 2 * t)
                for k in range(QT_):
                    nc.tensor.transpose(ps_qr[:, k * P:(k + 1) * P], lat[:, s, k * P:(k + 1) * P], ident[:, :])
                nc.tensor.transpose(ps_qr[:, Q_RANK:Q_RANK + P], k_rope[:, s, :], ident[:, :])
                for k in range(KVT_):
                    last = nc.tensor.transpose(ps_kv[:, k * P:(k + 1) * P],
                                               lat[:, s, Q_RANK + k * P:Q_RANK + (k + 1) * P], ident[:, :])
                last.then_inc(latT_done, 1)

            def values(j, s):
                if isinstance(j, int) or s == 0:
                    pe.wait_ge(w_lo_done, KD + KVT_)
                pe.wait_ge(kv_lo_done, 2 * j + s + 1)
                for k in range(KVT_):
                    last = three_passes(nc, ps_lat[s][:, :], kvT_hi[:, s, k, :], kvT_lo[:, s, k, :],
                                        wv_hi[:, k, :], wv_lo[:, k, :], k == 0, k == KVT_ - 1)
                last.then_inc(v_done, 1)

            for s in range(2):
                transpose_x0(0, s)
            latents(0, 0, 0)

            def step(i, last=False):
                for b in range(2):
                    j = 2 * i + b
                    more = not (last and b == 1)
                    pe.wait_ge(tr_lo_done, 4 * j + 4)
                    pool_inputs(j, 0, b)
                    transpose_latents(j, 0)
                    if more:
                        transpose_x0(j + 1, 0)
                    latents(j, 1, b)
                    pool_inputs(j, 1, b)
                    transpose_latents(j, 1)
                    if more:
                        transpose_x0(j + 1, 1)
                    for s in range(2):
                        values(j, s)
                    if more:
                        latents(j + 1, 0, 1 - b)

            with pe.Fori(0, PAIRS - 1) as i:
                step(i)
            step(PAIRS - 1, last=True)


def phase_attention(nc, ident, dram):
    with ExitStack() as ctx:
        m = Scope(nc, ctx)
        BLK = 512
        PAIRS, BLOCKS, UNITS = N_HEADS // 2, 6, 12
        steps = [(b, [t]) if b % 3 < 2 else (b, [2 * t, 2 * t + 1])
                 for b in range(BLOCKS) for t in range(4 if b % 3 < 2 else 2)]
        STEPS, HALVES = len(steps), 2 * len(steps)
        first_step = [[b for b, _ in steps].index(b) for b in range(BLOCKS)]
        unit_of = [2 * b + tiles[0] // 2 for b, tiles in steps]
        last_step = [max(n for n in range(STEPS) if unit_of[n] == u) for u in range(UNITS)]

        V_STEP = 2

        def is_prompt(n):
            return steps[n][0] % 3 == 2

        SPLIT = (0, 1, 2, 6, 7, 8)

        def output_parts(n):
            return [(u, part) for u in range(UNITS) for part in range(2 if u in SPLIT else 1) if last_step[u] + 2 + part == n]

        def finished_at(n):
            return [u for u in range(UNITS) if last_step[u] + (4 if u in SPLIT else 3) == n]

        def half_place(n, h):
            k, x = (0, h) if is_prompt(n) else (4 * h, steps[n][1][0] % 2)
            return slice(None), slice(k, k + 4), slice(x * P, (x + 1) * P)

        qn_hi, qn_lo = m.sb("qn_hi", [P, QT_, T], F32R), m.sb("qn_lo", [P, QT_, T], F32R)
        kvn_hi, kvn_lo = m.sb("kvn_hi", [P, KVT_, T], F32R), m.sb("kvn_lo", [P, KVT_, T], F32R)
        k_hi, k_lo = m.sb("k_hi", [P, 2, T], F32R), m.sb("k_lo", [P, 2, T], F32R)
        q_hi, q_lo = m.sb("q_hi", [P, 2, BLK], F32R), m.sb("q_lo", [P, 2, BLK], F32R)
        q_table, q_work, q_moved = m.sb("q_table", [P, S_SAMPLE]), m.sb("q_work", [P, BLK]), m.sb("q_moved", [ROPE, BLK])
        v_parts = m.sb("v_hi_lo", [P, N_TILES, 2, 2, V_DIM], F32R)
        v_raw = m.sb("v_raw", [P, N_TILES, 2, V_DIM])
        probs = m.sb("probs", [P, 2, S_SAMPLE])
        pT_hi = [m.sb(f"pT_hi{s}", [P, 8, 2 * P], F32R) for s in range(2)]
        pT_lo = [m.sb(f"pT_lo{s}", [P, 8, 2 * P], F32R) for s in range(2)]
        neg_max = m.sb("neg_max", [P, 2, 2])
        row_sum, inv_sum = m.sb("row_sum", [P, 4]), m.sb("inv_sum", [P, 4])
        wq_raw, wq_wide = m.sb("wq_raw", [P, QT_, 2, QK]), m.sb("wq_wide", [P, QT_, 2, P])
        wq_hi, wq_lo = m.sb("wq_hi", [P, QT_, 2, P], F32R), m.sb("wq_lo", [P, QT_, 2, P], F32R)
        wk_raw = m.sb("wk_raw", [P, KVT_, 2, NOPE])
        wk_hi, wk_lo = m.sb("wk_hi", [P, KVT_, P], F32R), m.sb("wk_lo", [P, KVT_, P], F32R)
        o_low, o_sum = m.sb("o_low", [V_DIM, 2 * P]), m.sb("o_sum", [V_DIM, 2 * P])
        o_out = m.sb("o_out", [V_DIM, 2, BLK])
        PAD = max(POOL_WINDOWS) // 2
        W_MAX = S_SAMPLE + 2 * PAD
        u_in, sum_a, sum_b = m.sb("u_in", [P, W_MAX]), m.sb("window_a", [P, W_MAX]), m.sb("window_b", [P, W_MAX])
        inv_count = m.sb("inv_count", [P, S_SAMPLE])

        ps_s = [m.ps(f"ps_scores{s}", (P, 1024)) for s in range(2)]
        ps_t = [m.ps(f"ps_probsT{s}") for s in range(2)]
        ps_k = [ps_s[0][:, 0:BLK], ps_s[0][:, BLK:2 * BLK], ps_s[1][:, 0:BLK]]
        ps_q, ps_o = m.ps("ps_q"), m.ps("ps_o")

        RING = 6
        lat_loaded = [m.sem(f"b_lat_loaded{s}") for s in range(RING)]
        lat_hi_done, lat_lo_done = m.sem("b_lat_hi_done"), m.sem("b_lat_lo_done")
        table_loaded = m.sem("b_table_loaded")
        wq_loaded, wk_loaded, v_loaded = m.sem("b_wq_loaded"), m.sem("b_wk_loaded"), m.sem("b_v_loaded")
        wq_widened, w_hi_done, w_lo_done = m.sem("b_wq_widened"), m.sem("b_w_hi_done"), m.sem("b_w_lo_done")
        v_hi_done, v_lo_done = m.sem("b_v_hi_done"), m.sem("b_v_lo_done")
        k_done, k_hi_done, k_lo_done = m.sem("b_k_done"), m.sem("b_k_hi_done"), m.sem("b_k_lo_done")
        q_done, q_rotated, q_shifted = m.sem("b_q_done"), m.sem("b_q_rotated"), m.sem("b_q_shifted")
        q_added, q_hi_done, q_lo_done = m.sem("b_q_added"), m.sem("b_q_hi_done"), m.sem("b_q_lo_done")
        s_done, max_done, exp_done = m.sem("b_s_done"), m.sem("b_max_done"), m.sem("b_exp_done")
        t_done, t_hi_done, t_lo_done = m.sem("b_t_done"), m.sem("b_t_hi_done"), m.sem("b_t_lo_done")
        o_done, inv_done, o_low_copied, o_added, o_scaled = (
            m.sem("b_" + x) for x in ("o_done", "inv_done", "o_low_copied", "o_added", "o_scaled"))
        o_stored = [m.sem(f"b_o_stored{s}") for s in range(2)]
        u_loaded, count_loaded = m.sem("b_u_loaded"), m.sem("b_count_loaded")
        window_step, d_stored = m.sem("b_window_step"), m.sem("b_d_stored")

        PIECE = T // 2
        piece_raw = m.sb("piece_raw", [P, RING - 2, PIECE])
        pieces = [("kvT", kvn_hi, kvn_lo, k, c) for k in range(KVT_) for c in range(2)] \
            + [("krT", k_hi, k_lo, None, c) for c in range(2)] \
            + [("qT", qn_hi, qn_lo, k, c) for c in range(2) for k in range(QT_)]
        FIRST_QUERY_PIECES = 2 * KVT_ + 2 + QT_

        def raw_piece(n, rows=P):
            slot = n % RING
            return probs[0:rows, slot, 0:PIECE] if slot < 2 else piece_raw[0:rows, slot - 2, :]

        def piece_views(n, part):
            _, hi, lo, k, c = pieces[n]
            buf = hi if part == "hi" else lo
            cols = slice(c * PIECE, (c + 1) * PIECE)
            if k is not None:
                return [(buf[:, k, cols], raw_piece(n), f32(hi[:, k, cols]))]
            return [(buf[0:2 * ROPE, h, cols], raw_piece(n, 2 * ROPE), f32(hi[0:2 * ROPE, h, cols])) for h in range(2)]

        splits_before = [sum(2 if pieces[x][3] is None else 1 for x in range(n)) for n in range(len(pieces) + 1)]

        def next_block(i, n, last):
            b = steps[n][0] + 1
            return (i, b) if b < BLOCKS else None if last else (i + 1, 0)

        block = ctx.enter_context(nc.Block())

        @block.sync
        def _(sp):
            w_q = dram["w_uq"].rearrange("(t p) (h c) -> p t (h c)", p=P, c=QK)
            w_k = dram["w_ukv"].rearrange("(t p) (h c) -> t p h c", p=P, c=NOPE + V_DIM)
            v_rows = dram["v"].rearrange("(t p) c -> p t c", p=P)

            def load_v(v_column):
                sp.dma_start(v_raw[:, :, :, :].rearrange("p t h v -> p t (h v)"), v_rows[:, :, bass.ds(v_column, 2 * V_DIM)]).then_inc(v_loaded, 16)

            def load_weights(q_column, head):
                sp.dma_start(wq_raw[:, :, :, :].rearrange("p t h c -> p t (h c)"),
                             w_q[:, :, bass.ds(q_column, 2 * QK)]).then_inc(wq_loaded, 16)
                for k in range(KVT_):
                    sp.dma_start(wk_raw[:, k, :, :], w_k[k][:, bass.ds(head, 2), 0:NOPE]).then_inc(wk_loaded, 16)

            load_weights(0, 0)
            for n, (name, _, _, k, c) in enumerate(pieces):
                if n >= RING:
                    sp.wait_ge(lat_lo_done, splits_before[n - RING + 1])
                cols = slice(c * PIECE, (c + 1) * PIECE)
                rows, n_rows = (slice(k * P, (k + 1) * P), P) if k is not None else (slice(0, 2 * ROPE), 2 * ROPE)
                sp.dma_start(raw_piece(n, n_rows), dram[name][rows, cols]).then_inc(lat_loaded[n % RING], 16)
                if n == FIRST_QUERY_PIECES - 1:
                    sp.dma_start(q_table[:, :], dram["q_table"]).then_inc(table_loaded, 16)
                    load_v(0)

            def step(i, last=False):
                if not last:
                    at = [sp.snap((i + 1) * 2 * size) for size in (QK, 1, V_DIM)]
                    sp.wait_ge(v_lo_done, i + 1)
                    sp.wait_ge(w_lo_done, 2 * i + 2)
                    load_weights(*at[0:2])
                    load_v(at[2])
                for b in range(BLOCKS):
                    head, blk = b // 3, b % 3
                    first = POOL_DIM + (2 * i + head) * V_DIM
                    rows = bass.ds(first if last else sp.snap(first), V_DIM)
                    sp.wait_ge(o_scaled, UNITS * i + 2 * b + 2)
                    sp.dma_start(dram["mixT"][rows, blk * BLK:(blk + 1) * BLK], o_out[:, b % 2, :]).then_inc(o_stored[b % 2], 16)

            with sp.Fori(0, PAIRS - 1) as i:
                step(i)
            step(PAIRS - 1, last=True)
            for s in range(2):
                sp.wait_ge(o_stored[s], 16 * 3 * PAIRS)

        @block.gpsimd
        def _(pool):
            pool.memset(u_in[:, :], 0.0).then_inc(window_step, 1)
            steps, loads = 1, 0
            pool.wait_ge(table_loaded, 16)
            for start, n in ((0, S_SAMPLE), (S_SAMPLE, S_PROMPT)):
                width = n + 2 * PAD
                if start:
                    pool.wait_ge(window_step, steps)
                    pool.memset(u_in[:, PAD + n:width], 0.0).then_inc(window_step, 1)
                    steps += 1
                for g, window in enumerate(POOL_WINDOWS):
                    pool.wait_ge(window_step, steps)
                    pool.wait_ge(d_stored, 16 * loads)
                    pool.dma_start(u_in[:, PAD:PAD + n], dram["uT"][g * GROUP:(g + 1) * GROUP, start:start + n]).then_inc(u_loaded, 16)
                    pool.dma_start(inv_count[:, 0:n], dram["inv_count"][g, start:start + n].partition_broadcast(P)).then_inc(count_loaded, 16)
                    loads += 1
                    pool.wait_ge(u_loaded, 16 * loads)
                    pool.wait_ge(count_loaded, 16 * loads)
                    src, dst, other = u_in, sum_a, sum_b
                    pool.tensor_tensor(dst[:, 1:width], u_in[:, 0:width - 1], u_in[:, 1:width], ALU.add).then_inc(window_step, 1)
                    steps += 1
                    reach, size = 1, 2
                    while size < window:
                        src, dst, other = dst, other, dst
                        half = size // 2
                        lo, hi = reach + half, width - (reach - 1) - half
                        pool.wait_ge(window_step, steps)
                        pool.tensor_tensor(dst[:, lo:hi], src[:, lo - half:hi - half], src[:, lo + half:hi + half], ALU.add).then_inc(window_step, 1)
                        steps += 1
                        reach, size = lo, 2 * size
                    body = slice(PAD, PAD + n)
                    pool.wait_ge(window_step, steps)
                    pool.tensor_tensor(dst[:, body], dst[:, body], inv_count[:, 0:n], ALU.mult).then_inc(window_step, 1)
                    pool.wait_ge(window_step, steps + 1)
                    pool.tensor_tensor(dst[:, body], dst[:, body], u_in[:, body], ALU.subtract).then_inc(window_step, 1)
                    steps += 2
                    pool.wait_ge(window_step, steps)
                    pool.dma_start(dram["dT"][g * GROUP:(g + 1) * GROUP, start:start + n], dst[:, body]).then_inc(d_stored, 16)
            pool.wait_ge(d_stored, 16 * loads)

        @block.scalar
        def _(act):
            def round_weights(i):
                act.wait_ge(wk_loaded, 32 * (i + 1))
                act.wait_ge(k_done, 3 * i)
                act.activation(wk_hi[:, :, :], wk_raw[:, :, :, :].rearrange("p t h c -> p t (h c)"), ACT.Copy).then_inc(w_hi_done, 1)
                act.wait_ge(wq_widened, 4 * (i + 1))
                act.wait_ge(q_done, BLOCKS * i)
                act.activation(wq_hi[:, :, :, :], wq_wide[:, :, :, :], ACT.Copy).then_inc(w_hi_done, 1)

            round_weights(0)

            def round_pieces(first, after):
                for n in range(first, after):
                    act.wait_ge(lat_loaded[n % RING], 16 * (n // RING + 1))
                    for out, src, _ in piece_views(n, "hi"):
                        act.activation(out, src, ACT.Copy).then_inc(lat_hi_done, 1)

            def shift_rope(i, b):
                act.wait_ge(q_rotated, BLOCKS * i + b + 1)
                act.wait_ge(q_added, BLOCKS * i + b)
                act.activation(q_moved[:, :], q_work[ROPE:2 * ROPE, :], ACT.Copy).then_inc(q_shifted, 1)

            def round_q(i, b):
                act.wait_ge(q_added, BLOCKS * i + b + 1)
                if b != 0 or not isinstance(i, int) or i > 0:
                    act.wait_ge(s_done, STEPS * i + (first_step[b - 1] if b else first_step[-1] - STEPS))
                act.activation(q_hi[:, b % 2, :], q_work[:, :], ACT.Copy).then_inc(q_hi_done, 1)

            def round_probsT(i, n):
                unit = unit_of[n]
                for h in range(2):
                    act.wait_ge(o_done, UNITS * i + max(unit - 1, 0))
                    act.wait_ge(t_done, HALVES * i + 2 * n + h + 1)
                    act.activation(pT_hi[unit % 2][half_place(n, h)], ps_t[h][:, :].rearrange("p (k t) -> p k t", t=P),
                                   ACT.Copy).then_inc(t_hi_done, 1)

            def exponent(i, n):
                tiles = steps[n][1]
                act.wait_ge(t_done, HALVES * i + 2 * max(n - 1, 0))
                act.wait_ge(max_done, STEPS * i + n + 1)
                width = 2 * BLK // len(tiles)
                for x, t in enumerate(tiles):
                    last = act.activation(probs[:, n % 2, x * width:(x + 1) * width], ps_s[n % 2][:, x * width:(x + 1) * width],
                                          ACT.Exp, bias=neg_max[:, n % 2, x:x + 1], accum_out=row_sum[:, t:t + 1])
                last.then_inc(exp_done, 1)

            def copy_low(i, unit):
                act.wait_ge(o_done, UNITS * i + unit + 1)
                act.wait_ge(o_added, UNITS * i + unit)
                act.activation(o_low[:, :], ps_o[V_DIM:P, 0:2 * P], ACT.Copy).then_inc(o_low_copied, 1)

            def round_keys(i, blocks=range(3)):
                for blk in blocks:
                    act.wait_ge(k_done, 3 * i + blk + 1)
                    for head in range(2):
                        act.activation(k_hi[NOPE:P, head, blk * BLK:(blk + 1) * BLK],
                                       ps_k[blk][head * NOPE:(head + 1) * NOPE, :], ACT.Copy).then_inc(k_hi_done, 1)

            def round_v(i):
                act.wait_ge(v_loaded, 16 * (i + 1))
                act.wait_ge(o_done, UNITS * i)
                act.activation(v_parts[:, :, :, 0, :], v_raw[:, :, :, :], ACT.Copy).then_inc(v_hi_done, 1)

            def step(i, last=False):
                for n in range(STEPS):
                    for unit in finished_at(n):
                        copy_low(i, unit)
                    if n:
                        round_probsT(i, n - 1)
                    ahead = next_block(i, n, last)
                    in_block = n - first_step[steps[n][0]]
                    if ahead and in_block == 1 and is_prompt(n):
                        round_q(*ahead)
                    exponent(i, n)
                    if ahead and in_block == 0:
                        shift_rope(*ahead)
                    if ahead and in_block == 1 and not is_prompt(n):
                        round_q(*ahead)
                    if n == V_STEP:
                        round_v(i)
                    if n == first_step[4] + 1 and not last:
                        round_weights(i + 1)
                copy_low(i, UNITS - 3)
                round_probsT(i, STEPS - 1)
                if not last:
                    round_keys(i + 1, (0, 1))
                copy_low(i, UNITS - 2)
                if not last:
                    round_keys(i + 1, (2,))
                copy_low(i, UNITS - 1)

            round_pieces(0, FIRST_QUERY_PIECES)
            round_keys(0)
            shift_rope(0, 0)
            round_q(0, 0)
            round_pieces(FIRST_QUERY_PIECES, len(pieces))
            with act.Fori(0, PAIRS - 1) as i:
                step(i)
            step(PAIRS - 1, last=True)

        @block.vector
        def _(dve):
            def widen_weights(i):
                dve.wait_ge(wq_loaded, 16 * (i + 1))
                dve.wait_ge(w_lo_done, 2 * i)
                half = ROPE // 2
                for dst, src, size in ((0, NOPE, ROPE), (ROPE, NOPE + half, half), (ROPE + half, NOPE, half), (2 * ROPE, 0, NOPE)):
                    nc.vector.tensor_copy(wq_wide[:, :, :, dst:dst + size], wq_raw[:, :, :, src:src + size]).then_inc(wq_widened, 1)

            def rest_weights(i):
                dve.wait_ge(w_hi_done, 2 * i + 1)
                nc.vector.tensor_tensor(wk_lo[:, :, :], wk_raw[:, :, :, :].rearrange("p t h c -> p t (h c)"),
                                        f32(wk_hi[:, :, :]), ALU.subtract).then_inc(w_lo_done, 1)
                dve.wait_ge(w_hi_done, 2 * i + 2)
                nc.vector.tensor_tensor(wq_lo[:, :, :, :], wq_wide[:, :, :, :], f32(wq_hi[:, :, :, :]),
                                        ALU.subtract).then_inc(w_lo_done, 1)

            widen_weights(0)
            rest_weights(0)

            def rest_pieces(first, after):
                for n in range(first, after):
                    for x, (out, src, hi) in enumerate(piece_views(n, "lo")):
                        dve.wait_ge(lat_hi_done, splits_before[n] + x + 1)
                        nc.vector.tensor_tensor(out, src, hi, ALU.subtract).then_inc(lat_lo_done, 1)

            def rotate(i, b):
                blk = b % 3
                dve.wait_ge(q_done, BLOCKS * i + b + 1)
                dve.wait_ge(q_lo_done, BLOCKS * i + b)
                position = 0 if blk == 2 else blk * BLK
                nc.vector.tensor_tensor(q_work[:, :], ps_q[:, :], q_table[:, position:position + BLK], ALU.mult).then_inc(q_rotated, 1)

            def add_rope(i, b):
                dve.wait_ge(q_shifted, BLOCKS * i + b + 1)
                nc.vector.tensor_tensor(q_work[0:ROPE, :], q_work[0:ROPE, :], q_moved[:, :], ALU.add).then_inc(q_added, 1)

            def rest_q(i, b):
                dve.wait_ge(q_hi_done, BLOCKS * i + b + 1)
                nc.vector.tensor_tensor(q_lo[:, b % 2, :], q_work[:, :], f32(q_hi[:, b % 2, :]), ALU.subtract).then_inc(q_lo_done, 1)

            def maximum(i, n):
                count = len(steps[n][1])
                dve.wait_ge(exp_done, STEPS * i + max(n - 1, 0))
                dve.wait_ge(s_done, STEPS * i + n + 1)
                nc.vector.tensor_reduce(neg_max[:, n % 2, 0:count], ps_s[n % 2][:, :].rearrange("p (x c) -> p x c", x=count),
                                        op=ALU.max, axis=AX.X, negate=True).then_inc(max_done, 1)

            def rest_probsT(i, n):
                unit, tiles = unit_of[n], slice(steps[n][1][0], steps[n][1][-1] + 1)
                dve.wait_ge(exp_done, STEPS * i + n + 1)
                nc.vector.reciprocal(inv_sum[:, tiles], row_sum[:, tiles]).then_inc(inv_done, 1)
                for h in range(2):
                    dve.wait_ge(t_hi_done, HALVES * i + 2 * n + h + 1)
                    at = half_place(n, h)
                    nc.vector.tensor_tensor(pT_lo[unit % 2][at], ps_t[h][:, :].rearrange("p (k t) -> p k t", t=P),
                                            f32(pT_hi[unit % 2][at]), ALU.subtract).then_inc(t_lo_done, 1)

            def divide(i, unit):
                b = unit // 2
                dve.wait_ge(o_low_copied, UNITS * i + unit + 1)
                nc.vector.tensor_tensor(o_sum[:, :], ps_o[0:V_DIM, 0:2 * P], o_low[:, :], ALU.add).then_inc(o_added, 1)
                dve.wait_ge(o_stored[b % 2], 16 * (3 * i + b // 2))
                dve.wait_ge(o_added, UNITS * i + unit + 1)
                nc.vector.tensor_tensor(o_out[:, b % 2, (unit % 2) * 2 * P:(unit % 2 + 1) * 2 * P], o_sum[:, :],
                                        ps_o[0:V_DIM, 2 * P:4 * P], ALU.mult).then_inc(o_scaled, 1)

            def rest_keys(i, blocks=range(3)):
                for blk in blocks:
                    for head in range(2):
                        dve.wait_ge(k_hi_done, 6 * i + 2 * blk + 2)
                        keep = (slice(NOPE, P), head, slice(blk * BLK, (blk + 1) * BLK))
                        nc.vector.tensor_tensor(k_lo[keep], ps_k[blk][head * NOPE:(head + 1) * NOPE, :], f32(k_hi[keep]),
                                                ALU.subtract).then_inc(k_lo_done, 1)

            def rest_v(i):
                dve.wait_ge(v_hi_done, i + 1)
                nc.vector.tensor_tensor(v_parts[:, :, :, 1, :], v_raw[:, :, :, :], f32(v_parts[:, :, :, 0, :]),
                                        ALU.subtract).then_inc(v_lo_done, 1)

            rest_pieces(0, FIRST_QUERY_PIECES)
            rest_keys(0)
            dve.wait_ge(table_loaded, 16)
            rotate(0, 0)
            add_rope(0, 0)
            rest_q(0, 0)
            rest_pieces(FIRST_QUERY_PIECES, len(pieces))

            def step(i, last=False):
                for n in range(STEPS):
                    ahead = next_block(i, n, last)
                    in_block = n - first_step[steps[n][0]]
                    for unit in finished_at(n):
                        divide(i, unit)
                    if ahead and in_block == 1:
                        add_rope(*ahead)
                    maximum(i, n)
                    if n:
                        rest_probsT(i, n - 1)
                    if ahead and in_block == 0:
                        rotate(*ahead)
                    if ahead and n < STEPS - 1 and in_block == (1 if is_prompt(n) else 2):
                        rest_q(*ahead)
                    if n == V_STEP:
                        rest_v(i)
                    if n == first_step[4] and not last:
                        widen_weights(i + 1)
                    if n == first_step[4] + 2 and not last:
                        rest_weights(i + 1)
                divide(i, UNITS - 3)
                rest_probsT(i, STEPS - 1)
                if not last:
                    rest_q(i + 1, 0)
                    rest_keys(i + 1, (0, 1))
                divide(i, UNITS - 2)
                if not last:
                    rest_keys(i + 1, (2,))
                divide(i, UNITS - 1)

            with dve.Fori(0, PAIRS - 1) as i:
                step(i)
            step(PAIRS - 1, last=True)

        @block.tensor
        def _(pe):
            def key_block(i, blk):
                if blk == 0:
                    pe.wait_ge(w_lo_done, 2 * i + 2)
                for k in range(KVT_):
                    cols = slice(blk * BLK, (blk + 1) * BLK)
                    last = three_passes(nc, ps_k[blk], wk_hi[:, k, :], wk_lo[:, k, :], kvn_hi[:, k, cols], kvn_lo[:, k, cols],
                                        k == 0, k == KVT_ - 1)
                last.then_inc(k_done, 1)

            def query_block(i, b):
                head, blk = b // 3, b % 3
                if b == 0:
                    pe.wait_ge(w_lo_done, 2 * i + 2)
                if b or not isinstance(i, int) or i:
                    pe.wait_ge(q_rotated, BLOCKS * i + b)
                for k in range(QT_):
                    cols = slice(blk * BLK, (blk + 1) * BLK)
                    last = three_passes(nc, ps_q[:, :], wq_hi[:, k, head, :], wq_lo[:, k, head, :],
                                        qn_hi[:, k, cols], qn_lo[:, k, cols], k == 0, k == QT_ - 1)
                last.then_inc(q_done, 1)

            def scores(i, n):
                b, tiles = steps[n]
                if n == 0:
                    pe.wait_ge(k_lo_done, 6 * i + 6)
                pe.wait_ge(q_lo_done, BLOCKS * i + b + 1)
                pe.wait_ge(exp_done, STEPS * i + max(n - 1, 0))
                for x in range(2):
                    t, key = (tiles[x], S_SAMPLE) if is_prompt(n) else (tiles[0], x * BLK)
                    rows, cols = slice(t * P, (t + 1) * P), slice(key, key + BLK)
                    last = three_passes(nc, ps_s[n % 2][:, x * BLK:(x + 1) * BLK], q_hi[:, b % 2, rows], q_lo[:, b % 2, rows],
                                        k_hi[:, b // 3, cols], k_lo[:, b // 3, cols], True, True)
                last.then_inc(s_done, 1)

            def transpose_probs(i, n):
                for h in range(2):
                    pe.wait_ge(exp_done, STEPS * i + n + 1)
                    pe.wait_ge(t_lo_done, HALVES * i + max(2 * n + h - 1, 0))
                    for k in range(4):
                        last = nc.tensor.transpose(ps_t[h][:, k * P:(k + 1) * P],
                                                   probs[:, n % 2, (4 * h + k) * P:(4 * h + k + 1) * P], ident[:, :])
                    last.then_inc(t_done, 1)

            def outputs(i, unit, part=0):
                head = unit // 6
                start, nk = (S_SAMPLE, S_PROMPT // P) if is_prompt(last_step[unit]) else (0, S_SAMPLE // P)
                if unit == 0:
                    pe.wait_ge(v_lo_done, i + 1)
                pe.wait_ge(t_lo_done, HALVES * i + 2 * last_step[unit] + 2)
                pe.wait_ge(o_scaled, UNITS * i + unit)
                parts = 2 if unit in SPLIT else 1
                for k in range(part * nk // parts, (part + 1) * nk // parts):
                    both = v_parts[:, start // P + k, head, :, :].rearrange("p a v -> p (a v)")
                    nc.tensor.matmul(ps_o[:, 0:2 * P], both, pT_hi[unit % 2][:, k, :], start=k == 0, stop=False)
                    nc.tensor.matmul(ps_o[:, 0:2 * P], both, pT_lo[unit % 2][:, k, :], start=False, stop=k == nk - 1)
                if part < parts - 1:
                    return
                pe.wait_ge(inv_done, STEPS * i + last_step[unit] + 1)
                for x in range(2):
                    at = unit % 2 * 2 + x
                    last = nc.tensor.matmul(ps_o[0:V_DIM, (2 + x) * P:(3 + x) * P], inv_sum[:, at:at + 1].to_broadcast([P, V_DIM]),
                                            ident[:, :], start=True, stop=True)
                last.then_inc(o_done, 1)

            pe.wait_ge(lat_lo_done, splits_before[2 * KVT_])
            for blk in range(3):
                key_block(0, blk)
            pe.wait_ge(lat_lo_done, splits_before[FIRST_QUERY_PIECES])
            query_block(0, 0)

            def step(i, last=False):
                for n in range(STEPS):
                    ahead = next_block(i, n, last)
                    scores(i, n)
                    if n:
                        transpose_probs(i, n - 1)
                    else:
                        pe.wait_ge(lat_lo_done, splits_before[-1])
                    if ahead and n == first_step[steps[n][0]]:
                        query_block(*ahead)
                    for unit, part in output_parts(n):
                        outputs(i, unit, part)
                transpose_probs(i, STEPS - 1)
                if not last:
                    key_block(i + 1, 0)
                    key_block(i + 1, 1)
                outputs(i, UNITS - 2)
                if not last:
                    key_block(i + 1, 2)
                outputs(i, UNITS - 1)

            with pe.Fori(0, PAIRS - 1) as i:
                step(i)
            step(PAIRS - 1, last=True)


class ExpertWeights:
    CHUNK, HALF, N_CHUNKS = 2048, FFN // 2, 6
    EARLY = 4
    GATE, UP, DOWN = (0, 2), (1, 3), (4, 5)

    def __init__(self, m, dram):
        self.dram = dram
        self.raw = m.sb("w_raw", [P, self.N_CHUNKS, self.CHUNK])
        self.hi = [m.sb(f"w_hi{c}", [P, self.CHUNK], F32R) for c in range(self.EARLY)]
        self.lo = [m.sb(f"w_lo{c}", [P, self.CHUNK], F32R) for c in range(self.EARLY)]
        self.loaded = [m.sem(f"expert_loaded{c}") for c in range(self.N_CHUNKS)]
        self.hi_done, self.lo_done = m.sem("expert_hi_done"), m.sem("expert_lo_done")

    def load(self, sp, e, c):
        if c in self.DOWN:
            rows = slice((c - 4) * 2 * P, (c - 3) * 2 * P)
            src = self.dram["w_down"][bass.ds(e, 1), rows, :].rearrange("e (k p) d -> p (e k) d", p=P)
            dst = self.raw[:, c, :].rearrange("p (k d) -> p k d", d=D)
        else:
            w = self.dram["w_gate" if c in self.GATE else "w_up"]
            cols = slice(c // 2 * self.HALF, (c // 2 + 1) * self.HALF)
            src = w[bass.ds(e, 1), :, cols].rearrange("e (k p) f -> p (e k) f", p=P)
            dst = self.raw[:, c, :].rearrange("p (k f) -> p k f", f=self.HALF)
        sp.dma_start(dst, src).then_inc(self.loaded[c], 16)


def phase_mix(nc, ident, dram, route, experts):
    with ExitStack() as ctx:
        m = Scope(nc, ctx)
        w_raw = experts.raw[:, :, :].rearrange("p c (h d) -> p (c h) d", d=D)
        w_hi = [experts.hi[k // 2][:, k % 2 * D:(k % 2 + 1) * D] for k in range(KD)]
        w_lo = [experts.lo[k // 2][:, k % 2 * D:(k % 2 + 1) * D] for k in range(KD)]
        w_pool, pool_scale = m.sb("w_pool", [P, 4, P]), m.sb("pool_scale_all", [P, 4, P])
        d = m.sb("d", [P, 2, 4, P])
        mix_raw = m.sb("mix_raw", [P, 2, 4, P])
        mix_hi, mix_lo = m.sb("mix_hi", [P, 2, KD, P], F32R), m.sb("mix_lo", [P, 2, KD, P], F32R)
        x0, x1, acc = m.sb("x0_again", [P, 2, D]), m.sb("x1", [P, 2, D]), m.sb("acc_out", [P, 2, D])
        ln_g, ln_b = m.sb("ln1_g_all", [P, D]), m.sb("ln1_b_all", [P, D])
        stats, moments, rstd = m.sb("ln1_stats", [P, 2, 2, 6]), m.sb("ln1_moments", [P, 2, 2]), m.sb("ln1_rstd", [P, 2])
        half_neg, eps, carrier = m.sb("c_minus_half", [P, 1]), m.sb("c_eps", [P, 1]), m.sb("c_wait_carrier", [P, 1])
        x1T = m.sb("x1T", [P, KD, P])
        w_router = m.sb("w_router", [P, KD, N_EXPERTS])
        logitsT, neg_max, e_logits = m.sb("logitsT", [N_EXPERTS, P]), m.sb("router_neg_max", [P, 1]), m.sb("e_logits", [P, N_EXPERTS])
        e_sum, e_inv = m.sb("e_sum", [P, 1]), m.sb("e_inv", [P, 1])
        SAMPLE_ROWS, PROMPT_ROWS, ROWS = slice(0, N_EXPERTS), slice(32, 32 + N_EXPERTS), 32 + N_EXPERTS
        affinity = m.sb("affinity", [P, ROWS])
        affT = m.sb("affT_sample", [N_EXPERTS, S_SAMPLE])
        left = [m.sb(f"topk_left{s}", [ROWS, S_SAMPLE]) for s in range(2)]
        value, index, index_f = m.sb("topk_value", [ROWS, P]), m.sb("topk_index", [ROWS, P], U32), m.sb("topk_index_f", [ROWS, P])

        ps_mix = [m.ps(f"ps_mix{s}", (P, D)) for s in range(2)]
        ps_t = [m.ps(f"ps_x1T{s}") for s in range(2)]
        ps_r, ps_a = m.ps("ps_router"), m.ps("ps_affinity")

        consts_loaded, ln_loaded, filled = m.sem("c_consts_loaded"), m.sem("c_ln_loaded"), m.sem("c_filled")
        wp_scaled = m.sem("c_wp_scaled")
        d_loaded = [m.sem(f"c_d_loaded{s}") for s in range(2)]
        pool_done = m.sem("c_pool_done")
        w_loaded = [m.sem(f"c_w_loaded{k}") for k in range(KD)]
        w_hi_done, w_lo_done = m.sem("c_w_hi_done"), m.sem("c_w_lo_done")
        mix_loaded = [m.sem(f"c_mix_loaded{s}") for s in range(2)]
        mix_hi_done, mix_lo_done = m.sem("c_mix_hi_done"), m.sem("c_mix_lo_done")
        pool_hi_done, pool_lo_done = m.sem("c_pool_hi_done"), m.sem("c_pool_lo_done")
        x0_loaded = [m.sem(f"c_x0_loaded{s}") for s in range(2)]
        wo_done, summed, stats_part, stats_done = m.sem("c_wo_done"), m.sem("c_summed"), m.sem("c_stats_part"), m.sem("c_stats_done")
        eps_added, rstd_done, centred, scaled, x1_done = (m.sem("c_" + x) for x in ("eps_added", "rstd_done", "centred", "scaled", "x1_done"))
        acc_done = m.sem("c_acc_done")
        x1_stored, acc_stored = [m.sem(f"c_x1_stored{s}") for s in range(2)], [m.sem(f"c_acc_stored{s}") for s in range(2)]
        t_done, t_copied, logits_done, logits_copied, logits_turned = (m.sem("c_" + x) for x in ("t_done", "t_copied", "logits_done", "logits_copied", "logits_turned"))
        r_max_done, r_exp_done, r_inv_done, r_aff_done, aff_turned, aff_copied = (
            m.sem("c_" + x) for x in ("r_max_done", "r_exp_done", "r_inv_done", "r_aff_done", "aff_turned", "aff_copied"))
        topk_step, lists_turned, lists_copied = m.sem("c_topk_step"), m.sem("c_lists_turned"), m.sem("c_lists_copied")

        K_ORDER = (4, 5, 6, 7, 0, 1, 2, 3)
        ROUNDS, FIRST_COLUMN = CAP_SAMPLE // 8, CAP_SAMPLE - CAP_PROMPT
        EARLY_TOPK = {N_TILES - 2: (1, 2), N_TILES - 1: (1, 2), N_TILES: (0, 2), N_TILES + 1: (1, 0)}
        JOIN = sum(a + b for a, b in EARLY_TOPK.values())
        ALONE = range(FIRST_COLUMN // 8, JOIN)
        TOPK_STEPS = 3 * (ROUNDS + len(ALONE)) - 1 + 5
        block = ctx.enter_context(nc.Block())

        def steps(eng, step):
            for s in range(2):
                step(s)
            with eng.Fori(1, N_TILES // 2 - 1) as i:
                for b in range(2):
                    step(2 * i + b, b)
            for s in range(N_TILES - 2, N_TILES + 2):
                step(s)

        def has(s, lag):
            return not isinstance(s, int) or lag <= s < N_TILES + lag

        def rows_of(t):
            return PROMPT_ROWS if isinstance(t, int) and t >= SAMPLE_TILES else SAMPLE_ROWS

        @block.sync
        def _(sp):
            def load_mix(s, slot):
                cols = bass.ds(s * P, P)
                by_slice = lambda name: dram[name].rearrange("(k p) t -> p k t", p=P)
                sp.dma_start(d[:, slot, :, :], by_slice("dT")[:, :, cols]).then_inc(d_loaded[slot], 16)
                sp.dma_start(mix_raw[:, slot, :, :], by_slice("mixT")[:, 4:8, cols]).then_inc(mix_loaded[slot], 16)

            def load_x0(s, slot):
                sp.dma_start(x0[:, slot, :], dram["x0"][bass.ds(s * P, P), :]).then_inc(x0_loaded[slot], 16)

            sp.dma_start(w_pool[:, :, :], dram["w_pool"].rearrange("g c d -> c g d")).then_inc(consts_loaded, 16)
            sp.dma_start(pool_scale[:, :, :].rearrange("p g d -> p (g d)"),
                         dram["pool_scale"].partition_broadcast(P)).then_inc(consts_loaded, 16)
            load_mix(0, 0)
            for n, k in enumerate(K_ORDER):
                sp.dma_start(w_raw[:, n, :], dram["w_o"][k * P:(k + 1) * P, :]).then_inc(w_loaded[n], 16)
                if n == 3:
                    load_x0(0, 0)
                    load_mix(1, 1)
            sp.dma_start(ln_g[:, :], dram["ln1_g"].partition_broadcast(P)).then_inc(ln_loaded, 16)
            sp.dma_start(ln_b[:, :], dram["ln1_b"].partition_broadcast(P)).then_inc(ln_loaded, 16)
            sp.dma_start(w_router[:, :, :], dram["w_router"].rearrange("(k p) e -> p k e", p=P)).then_inc(ln_loaded, 16)
            load_x0(1, 1)

            def step(s, slot=None):
                slot = s % 2 if slot is None else slot
                if not isinstance(s, int) or s + 2 < N_TILES:
                    sp.wait_ge(mix_lo_done, s + 1)
                    sp.wait_ge(pool_done, s + 1)
                    load_mix(s + 2, slot)
                if not isinstance(s, int) or 0 < s < N_TILES - 1:
                    sp.wait_ge(summed, s)
                    load_x0(s + 1, 1 - slot)
                if isinstance(s, int) and s == N_TILES - 1:
                    sp.wait_ge(w_lo_done, KD)
                    for c in range(experts.N_CHUNKS):
                        experts.load(sp, 0, c)
                if has(s, 1):
                    t = s - 1
                    sp.wait_ge(x1_done, s)
                    sp.dma_start(dram["x1"][bass.ds(t * P, P), :], x1[:, 1 - slot, :]).then_inc(x1_stored[1 - slot], 16)
                    sp.wait_ge(acc_done, s)
                    sp.dma_start(dram["acc"][bass.ds(t * P, P), :], acc[:, 1 - slot, :]).then_inc(acc_stored[1 - slot], 16)

            steps(sp, step)
            for s in range(2):
                sp.wait_ge(x1_stored[s], 16 * N_TILES // 2)
                sp.wait_ge(acc_stored[s], 16 * N_TILES // 2)

        @block.gpsimd
        def _(pool):
            pool.memset(half_neg[:, :], -0.5).then_inc(filled, 1)
            pool.memset(eps[:, :], LN_EPS).then_inc(filled, 1)
            pool.memset(affinity[:, :], 0.0).then_inc(filled, 1)
            pool.memset(left[(JOIN - 1) % 2][:, :], -1.0).then_inc(filled, 1)
            pool.memset(value[:, :], 0.0).then_inc(filled, 1)
            pool.memset(index_f[:, :], 0.0).then_inc(filled, 1)
            pool.wait_ge(filled, 6)
            pool.wait_ge(ln_loaded, 48)

            def step(s, slot=None):
                slot = s % 2 if slot is None else slot
                if not has(s, 0):
                    return
                pool.wait_ge(stats_done, s + 1)
                pool.tensor_tensor(rstd[:, slot:slot + 1], moments[:, slot, 1:2], eps[:, :], ALU.add).then_inc(eps_added, 1)
                pool.wait_ge(eps_added, s + 1)
                pool.tensor_tensor(rstd[:, slot:slot + 1], rstd[:, slot:slot + 1], half_neg[:, :], ALU.pow).then_inc(rstd_done, 1)
                pool.wait_ge(scaled, s + 1)
                pool.tensor_tensor(x1[:, slot, :], x1[:, slot, :], ln_b[:, :], ALU.add).then_inc(x1_done, 1)

            steps(pool, step)
            for c in range(experts.EARLY):
                pool.wait_ge(experts.hi_done, c + 1)
                pool.tensor_tensor(experts.lo[c][:, :], experts.raw[:, c, :], f32(experts.hi[c][:, :]), ALU.subtract).then_inc(experts.lo_done, 1)

        @block.scalar
        def _(act):
            def round_attention(s, slot):
                act.wait_ge(mix_loaded[slot], 16 * ((s - slot) // 2 + 1) if isinstance(s, int) else 8 * (s - slot) + 16)
                if not isinstance(s, int) or s >= 2:
                    act.wait_ge(wo_done, s - 1)
                act.activation(mix_hi[:, slot, 4:8, :], mix_raw[:, slot, :, :], ACT.Copy).then_inc(mix_hi_done, 1)

            def round_pool(s, slot):
                act.wait_ge(pool_done, s + 1)
                act.activation(mix_hi[:, slot, 0:4, :], ps_t[0][:, :].rearrange("p (k t) -> p k t", t=P), ACT.Copy).then_inc(pool_hi_done, 1)

            round_attention(0, 0)
            for n, k in enumerate(K_ORDER):
                act.wait_ge(w_loaded[n], 16)
                act.activation(w_hi[k], w_raw[:, n, :], ACT.Copy).then_inc(w_hi_done, 1)
                if n == 1:
                    round_pool(0, 0)

            def step(s, slot=None):
                slot = s % 2 if slot is None else slot
                if has(s, 2):
                    act.wait_ge(logits_done, s - 1)
                    act.activation(logitsT[:, :], ps_r[0:N_EXPERTS, 0:P], ACT.Copy).then_inc(logits_copied, 1)
                if has(s, -1) and not (isinstance(s, int) and s + 1 >= N_TILES):
                    round_attention(s + 1, 1 - slot)
                    round_pool(s + 1, 1 - slot)
                if has(s, 1):
                    if not isinstance(s, int) or s >= 3:
                        act.wait_ge(acc_stored[1 - slot], 16 * ((s - 1) // 2) if isinstance(s, int) else 8 * (s - 1 - (1 - slot)))
                    act.wait_ge(x1_done, s)
                    act.activation(acc[:, 1 - slot, :], x1[:, 1 - slot, :], ACT.Copy, scale=ALPHA).then_inc(acc_done, 1)
                if has(s, 2):
                    act.wait_ge(r_max_done, s - 1)
                    act.activation(e_logits[:, :], ps_a[:, 0:N_EXPERTS], ACT.Exp, bias=neg_max[:, :],
                                   accum_out=e_sum[:, :]).then_inc(r_exp_done, 1)
                if has(s, 1):
                    for h in range(2):
                        if has(s, 2):
                            act.wait_ge(logits_done, s - 1)
                        act.wait_ge(t_done, 2 * (s - 1) + h + 1)
                        act.activation(x1T[:, 4 * h:4 * h + 4, :], ps_t[h][:, :].rearrange("p (k t) -> p k t", t=P),
                                       ACT.Copy).then_inc(t_copied, 1)

            steps(act, step)
            act.wait_ge(wo_done, N_TILES)
            for c in range(experts.EARLY):
                act.wait_ge(experts.loaded[c], 16)
                act.activation(experts.hi[c][:, :], experts.raw[:, c, :], ACT.Copy).then_inc(experts.hi_done, 1)

        @block.vector
        def _(dve):
            def rest_attention(s, slot):
                dve.wait_ge(mix_hi_done, s + 1)
                nc.vector.tensor_tensor(mix_lo[:, slot, 4:8, :], mix_raw[:, slot, :, :], f32(mix_hi[:, slot, 4:8, :]),
                                        ALU.subtract).then_inc(mix_lo_done, 1)

            def rest_pool(s, slot):
                dve.wait_ge(pool_hi_done, s + 1)
                nc.vector.tensor_tensor(mix_lo[:, slot, 0:4, :], ps_t[0][:, :].rearrange("p (k t) -> p k t", t=P),
                                        f32(mix_hi[:, slot, 0:4, :]), ALU.subtract).then_inc(pool_lo_done, 1)

            dve.wait_ge(consts_loaded, 32)
            nc.vector.tensor_tensor(w_pool[:, :, :], w_pool[:, :, :], pool_scale[:, :, :], ALU.mult).then_inc(wp_scaled, 1)
            rest_attention(0, 0)
            for n, k in enumerate(K_ORDER):
                dve.wait_ge(w_hi_done, n + 1)
                nc.vector.tensor_tensor(w_lo[k], w_raw[:, n, :], f32(w_hi[k]), ALU.subtract).then_inc(w_lo_done, 1)
                if n == 1:
                    rest_pool(0, 0)
            dve.wait_ge(ln_loaded, 48)
            dve.wait_ge(filled, 6)

            now, buffer, n_steps = affT, 0, 0

            def topk_round(r, rows, size, first=False, replace=(None, None)):
                nonlocal now, buffer, n_steps
                if not first:
                    dve.wait_ge(topk_step, n_steps - 1)
                eight = value[rows, 8 * r:8 * r + 8]
                nc.vector.max(eight, now[rows, 0:size]).then_inc(topk_step, 1)
                dve.wait_ge(topk_step, n_steps + 1)
                after = left[buffer]
                replaced, width = replace
                if replaced is not None:
                    nc.vector.match_replace(after[replaced, 0:width], value[replaced, 8 * r:8 * r + 8],
                                            now[replaced, 0:width], -1.0).then_inc(topk_step, 1)
                    n_steps += 1
                nc.vector.max_index(index[rows, 8 * r:8 * r + 8], eight, now[rows, 0:size]).then_inc(topk_step, 1)
                now, buffer = after, 1 - buffer
                n_steps += 2

            sample_rounds = iter(range(JOIN))

            def early_topk(s, part):
                if isinstance(s, int) and s in EARLY_TOPK:
                    if part == 0 and s == N_TILES - 2:
                        dve.wait_ge(aff_copied, SAMPLE_TILES)
                    for _ in range(EARLY_TOPK[s][part]):
                        r = next(sample_rounds)
                        topk_round(r, SAMPLE_ROWS, S_SAMPLE, first=r == 0, replace=(SAMPLE_ROWS, S_SAMPLE))

            def step(s, slot=None):
                slot = s % 2 if slot is None else slot
                if has(s, -1) and not (isinstance(s, int) and s + 1 >= N_TILES):
                    rest_attention(s + 1, 1 - slot)
                    rest_pool(s + 1, 1 - slot)
                early_topk(s, 0)
                if has(s, 2):
                    dve.wait_ge(logits_turned, s - 1)
                    dve.wait_ge(r_exp_done, s - 2)
                    nc.vector.tensor_reduce(neg_max[:, :], ps_a[:, 0:N_EXPERTS], op=ALU.max, axis=AX.X, negate=True).then_inc(r_max_done, 1)
                if has(s, 2):
                    dve.wait_ge(r_exp_done, s - 1)
                    nc.vector.reciprocal(e_inv[:, :], e_sum[:, :]).then_inc(r_inv_done, 1)
                    dve.wait_ge(r_inv_done, s - 1)
                    dve.wait_ge(aff_turned, s - 2)
                    nc.vector.tensor_scalar(affinity[:, rows_of(s - 2)], e_logits[:, :], e_inv[:, :], None, ALU.mult).then_inc(r_aff_done, 1)
                if has(s, 0):
                    if not isinstance(s, int) or s >= 2:
                        dve.wait_ge(t_done, 2 * (s - 1))
                        dve.wait_ge(acc_done, s - 1)
                        dve.wait_ge(x1_stored[slot], 16 * (s // 2) if isinstance(s, int) else 8 * (s - slot))
                    dve.wait_ge(x0_loaded[slot], 16 * (s // 2 + 1) if isinstance(s, int) else 8 * (s - slot) + 16)
                    dve.wait_ge(wo_done, s + 1)
                    nc.vector.scalar_tensor_tensor(out=x1[:, slot, :], in0=x0[:, slot, :], scalar=ALPHA, in1=ps_mix[slot][:, :],
                                                   op0=ALU.mult, op1=ALU.add).then_inc(summed, 1)
                    dve.wait_ge(summed, s + 1)
                    for h in range(2):
                        nc.vector.bn_stats(stats[:, slot, h, :], x1[:, slot, h * 512:(h + 1) * 512]).then_inc(stats_part, 1)
                    if not isinstance(s, int) or s >= 2:
                        dve.wait_ge(eps_added, s - 1)
                        dve.wait_ge(centred, s - 1)
                    dve.wait_ge(stats_part, 2 * s + 2)
                    wait_carrier(nc, carrier)
                    nc.vector.bn_aggr(moments[:, slot, :], stats[:, slot, :, :].rearrange("p h c -> p (h c)")).then_inc(stats_done, 1)
                    dve.wait_ge(rstd_done, s + 1)
                    nc.vector.tensor_scalar(x1[:, slot, :], x1[:, slot, :], moments[:, slot, 0:1], rstd[:, slot:slot + 1],
                                            ALU.subtract, ALU.mult).then_inc(centred, 1)
                    dve.wait_ge(centred, s + 1)
                    nc.vector.tensor_tensor(x1[:, slot, :], x1[:, slot, :], ln_g[:, :], ALU.mult).then_inc(scaled, 1)
                if has(s, 2):
                    dve.wait_ge(aff_turned, s - 1)
                    if rows_of(s - 2) == SAMPLE_ROWS:
                        to = affT[:, bass.ds((s - 2) * P, P)]
                    else:
                        at = (s - 2 - SAMPLE_TILES) * P
                        to = left[(JOIN - 1) % 2][PROMPT_ROWS, at:at + P]
                    nc.vector.tensor_copy(to, ps_a[rows_of(s - 2), P:2 * P]).then_inc(aff_copied, 1)
                early_topk(s, 1)

            steps(dve, step)

            assert next(sample_rounds, None) is None
            both = slice(0, ROWS)
            dve.wait_ge(aff_copied, N_TILES)
            for r in range(JOIN, ROUNDS - 1):
                topk_round(r, both, S_SAMPLE, replace=(both, S_SAMPLE))
            topk_round(ROUNDS - 1, both, S_SAMPLE, replace=(PROMPT_ROWS, S_PROMPT))
            for r in ALONE:
                topk_round(r, PROMPT_ROWS, S_PROMPT, replace=(None, None) if r == ALONE[-1] else (PROMPT_ROWS, S_PROMPT))
            n, found, again = n_steps, slice(FIRST_COLUMN, CAP_SAMPLE), slice(0, CAP_PROMPT)
            dve.wait_ge(topk_step, n)
            nc.vector.tensor_copy(index_f[PROMPT_ROWS, found], index[PROMPT_ROWS, found]).then_inc(topk_step, 1)
            nc.vector.tensor_copy(index_f[SAMPLE_ROWS, :], index[SAMPLE_ROWS, :]).then_inc(topk_step, 1)
            nc.vector.tensor_copy(value[PROMPT_ROWS, again], value[PROMPT_ROWS, found]).then_inc(topk_step, 1)
            dve.wait_ge(topk_step, n + 1)
            nc.vector.tensor_scalar(index_f[PROMPT_ROWS, found], index_f[PROMPT_ROWS, found], float(S_SAMPLE), None, ALU.add).then_inc(topk_step, 1)
            dve.wait_ge(topk_step, n + 4)
            nc.vector.tensor_copy(index_f[PROMPT_ROWS, again], index_f[PROMPT_ROWS, found]).then_inc(topk_step, 1)
            assert n + 5 == TOPK_STEPS
            dve.wait_ge(lists_turned, 1)
            for q, rows in enumerate((SAMPLE_ROWS, PROMPT_ROWS)):
                nc.vector.tensor_copy(route["token"][q][:, :], ps_r[:, rows]).then_inc(lists_copied, 1)
                nc.vector.tensor_copy(route["gate"][q][:, :], ps_r[:, ROWS + rows.start:ROWS + rows.stop]).then_inc(lists_copied, 1)

        @block.tensor
        def _(pe):
            def pool_product(s, slot):
                pe.wait_ge(d_loaded[slot], 16 * ((s - slot) // 2 + 1) if isinstance(s, int) else 8 * (s - slot) + 16)
                for g in range(4):
                    last = nc.tensor.matmul(ps_t[0][:, g * P:(g + 1) * P], w_pool[:, g, :], d[:, slot, g, :], start=True, stop=True)
                last.then_inc(pool_done, 1)

            def output_slices(s, slot, order):
                for n in order:
                    k = K_ORDER[n]
                    if isinstance(s, int) and s == 0:
                        pe.wait_ge(w_lo_done, n + 1)
                    for h in range(2):
                        cols = slice(h * 512, (h + 1) * 512)
                        last = three_passes(nc, ps_mix[slot][:, cols], mix_hi[:, slot, k, :], mix_lo[:, slot, k, :],
                                            w_hi[k][:, cols], w_lo[k][:, cols], n == 0, n == KD - 1)
                return last

            pe.wait_ge(wp_scaled, 1)
            pool_product(0, 0)

            def step(s, slot=None):
                slot = s % 2 if slot is None else slot
                if has(s, 0):
                    pe.wait_ge(mix_lo_done, s + 1)
                    if not isinstance(s, int) or s >= 2:
                        pe.wait_ge(summed, s - 1)
                    output_slices(s, slot, range(0, 3))
                    pe.wait_ge(pool_lo_done, s + 1)
                    output_slices(s, slot, range(3, 4))
                if has(s, 2):
                    pe.wait_ge(t_copied, 2 * (s - 1))
                    for k in range(KD):
                        last = nc.tensor.matmul(ps_r[0:N_EXPERTS, 0:P], w_router[:, k, :], x1T[:, k, :], start=k == 0, stop=k == KD - 1)
                    last.then_inc(logits_done, 1)
                if has(s, -1) and not (isinstance(s, int) and s + 1 >= N_TILES):
                    pool_product(s + 1, 1 - slot)
                if has(s, 0):
                    output_slices(s, slot, range(4, 6))
                if has(s, 2):
                    pe.wait_ge(aff_copied, s - 2)
                    pe.wait_ge(logits_copied, s - 1)
                if has(s, 0):
                    output_slices(s, slot, range(6, 7))
                if has(s, 2):
                    nc.tensor.transpose(ps_a[:, 0:N_EXPERTS], logitsT[:, :], ident[0:N_EXPERTS, 0:N_EXPERTS]).then_inc(logits_turned, 1)
                if has(s, 0):
                    output_slices(s, slot, range(7, KD)).then_inc(wo_done, 1)
                if isinstance(s, int) and s == 1:
                    pe.wait_ge(ln_loaded, 48)
                if has(s, 1):
                    pe.wait_ge(x1_done, s)
                    for h in range(2):
                        if not isinstance(s, int) or s >= 2:
                            pe.wait_ge(t_copied, 2 * (s - 1))
                        if h == 0 and not (isinstance(s, int) and s + 1 >= N_TILES):
                            pe.wait_ge(pool_lo_done, s + 2)
                        for k in range(4):
                            last = nc.tensor.transpose(ps_t[h][:, k * P:(k + 1) * P],
                                                       x1[:, 1 - slot, (4 * h + k) * P:(4 * h + k + 1) * P], ident[:, :])
                        last.then_inc(t_done, 1)
                if has(s, 2):
                    pe.wait_ge(r_aff_done, s - 1)
                    rows = slice(0, rows_of(s - 2).stop)
                    nc.tensor.transpose(ps_a[rows, P:2 * P], affinity[:, rows], ident[:, :]).then_inc(aff_turned, 1)

            steps(pe, step)
            pe.wait_ge(topk_step, TOPK_STEPS)
            for x, source in enumerate((index_f, value)):
                last = nc.tensor.transpose(ps_r[:, x * ROWS:(x + 1) * ROWS], source[:, :], ident[0:ROWS, 0:ROWS])
            last.then_inc(lists_turned, 1)


class OutputNorm:
    SLOTS = 4
    TURNS, SAMPLE_TURNS = N_TILES // SLOTS, SAMPLE_TILES // SLOTS

    def __init__(self, nc, m, dram, experts):
        self.nc, self.dram = nc, dram
        rows = experts.raw[:, :, :].rearrange("p c (h d) -> p (c h) d", d=D)
        self.a, self.y = [rows[:, b, :] for b in range(self.SLOTS)], [rows[:, self.SLOTS + b, :] for b in range(self.SLOTS)]
        self.ln_g, self.ln_b = rows[:, 2 * self.SLOTS, :], rows[:, 2 * self.SLOTS + 1, :]
        self.stats, self.moments = m.sb("ln2_stats", [P, self.SLOTS, 2, 6]), m.sb("ln2_moments", [P, self.SLOTS, 2])
        self.rstd, self.minus_mean, self.bias = (m.sb("ln2_" + x, [P, self.SLOTS]) for x in ("rstd", "minus_mean", "bias"))
        self.half_neg, self.eps, self.carrier = m.sb("e_minus_half", [P, 1]), m.sb("e_eps", [P, 1]), m.sb("e_wait_carrier", [P, 1])
        self.loaded, self.stored = [m.sem(f"e_loaded{b}") for b in range(self.SLOTS)], [m.sem(f"e_stored{b}") for b in range(self.SLOTS)]
        (self.g_loaded, self.b_loaded, self.filled, self.stats_part, self.stats_done, self.eps_added, self.rstd_done, self.mean_negated,
         self.bias_done, self.centred, self.scaled, self.y_done) = (m.sem("e_" + x) for x in (
             "g_loaded", "b_loaded", "filled", "stats_part", "stats_done", "eps_added", "rstd_done", "mean_negated",
             "bias_done", "centred", "scaled", "y_done"))

    def load(self, sp, i, b):
        sp.dma_start(self.a[b], self.dram["acc"][bass.ds((self.SLOTS * i + b) * P, P), :]).then_inc(self.loaded[b], 16)

    def load_constants(self, sp):
        sp.dma_start(self.ln_g, self.dram["ln2_g"].partition_broadcast(P)).then_inc(self.g_loaded, 16)
        sp.dma_start(self.ln_b, self.dram["ln2_b"].partition_broadcast(P)).then_inc(self.b_loaded, 16)

    def load_and_store(self, sp):
        def step(i, dst, first_row, last=False):
            for b in range(self.SLOTS):
                t = self.SLOTS * i + b
                if not last:
                    sp.wait_ge(self.centred, t + 1)
                    self.load(sp, i + 1, b)
                sp.wait_ge(self.y_done, t + 1)
                sp.dma_start(dst[bass.ds(t * P - first_row, P), :], self.y[b]).then_inc(self.stored[b], 16)

        with sp.Fori(0, self.SAMPLE_TURNS) as i:
            step(i, self.dram["y_sample"], 0)
        for i in range(self.SAMPLE_TURNS, self.TURNS):
            step(i, self.dram["y_prompt"], S_SAMPLE, last=i == self.TURNS - 1)
        for b in range(self.SLOTS):
            sp.wait_ge(self.stored[b], 16 * self.TURNS)

    def fill(self, pool):
        pool.memset(self.half_neg[:, :], -0.5).then_inc(self.filled, 1)
        pool.memset(self.eps[:, :], LN_EPS).then_inc(self.filled, 1)

    def deviations_and_sum(self, pool):
        def reciprocal_std(t, b):
            pool.wait_ge(self.stats_done, t + 1)
            pool.tensor_tensor(self.rstd[:, b:b + 1], self.moments[:, b, 1:2], self.eps[:, :], ALU.add).then_inc(self.eps_added, 1)
            pool.wait_ge(self.eps_added, t + 1)
            pool.tensor_tensor(self.rstd[:, b:b + 1], self.rstd[:, b:b + 1], self.half_neg[:, :], ALU.pow).then_inc(self.rstd_done, 1)

        def step(i, last=False):
            for b in range(self.SLOTS):
                t = self.SLOTS * i + b
                if not (last and b == self.SLOTS - 1):
                    reciprocal_std(t + 1, (b + 1) % self.SLOTS)
                pool.wait_ge(self.scaled, t + 1)
                pool.tensor_tensor(self.y[b], self.y[b], self.ln_b, ALU.add).then_inc(self.y_done, 1)

        pool.wait_ge(self.filled, 2)
        reciprocal_std(0, 0)
        pool.wait_ge(self.b_loaded, 16)
        with pool.Fori(0, self.TURNS - 1) as i:
            step(i)
        step(self.TURNS - 1, last=True)

    def centre(self, act):
        with act.Fori(0, self.TURNS) as i:
            for b in range(self.SLOTS):
                t = self.SLOTS * i + b
                at = slice(b, b + 1)
                act.wait_ge(self.stats_done, t + 1)
                act.activation(self.minus_mean[:, at], self.moments[:, b, 0:1], ACT.Copy, scale=-1.0).then_inc(self.mean_negated, 1)
                act.wait_ge(self.mean_negated, t + 1)
                act.wait_ge(self.rstd_done, t + 1)
                act.activation(self.bias[:, at], self.minus_mean[:, at], ACT.Copy, scale=self.rstd[:, at]).then_inc(self.bias_done, 1)
                act.wait_ge(self.bias_done, t + 1)
                act.wait_ge(self.stored[b], 16 * i)
                act.activation(self.y[b], self.a[b], ACT.Identity, bias=self.bias[:, at], scale=self.rstd[:, at]).then_inc(self.centred, 1)

    def statistics_and_product(self, dve):
        nc = self.nc

        def statistics(i, b):
            t = self.SLOTS * i + b
            dve.wait_ge(self.loaded[b], 16 * i + 16)
            for h in range(2):
                nc.vector.bn_stats(self.stats[:, b, h, :], self.a[b][:, h * 512:(h + 1) * 512]).then_inc(self.stats_part, 1)
            dve.wait_ge(self.stats_part, 2 * t + 2)
            wait_carrier(nc, self.carrier)
            nc.vector.bn_aggr(self.moments[:, b, :], self.stats[:, b, :, :].rearrange("p h c -> p (h c)")).then_inc(self.stats_done, 1)

        def step(i, last=False):
            for b in range(self.SLOTS):
                t = self.SLOTS * i + b
                if b < self.SLOTS - 1:
                    statistics(i, b + 1)
                elif not last:
                    statistics(i + 1, 0)
                dve.wait_ge(self.centred, t + 1)
                nc.vector.tensor_tensor(self.y[b], self.y[b], self.ln_g, ALU.mult).then_inc(self.scaled, 1)

        statistics(0, 0)
        dve.wait_ge(self.g_loaded, 16)
        with dve.Fori(0, self.TURNS - 1) as i:
            step(i)
        step(self.TURNS - 1, last=True)


def phase_experts(nc, ident, dram, route, experts):
    with ExitStack() as ctx:
        m = Scope(nc, ctx)
        CS, CP = CAP_SAMPLE, CAP_PROMPT
        N = CS + CP
        FT = FFN // P
        CHUNK, HALF, N_CHUNKS = experts.CHUNK, experts.HALF, experts.N_CHUNKS
        GATE, UP, DOWN = experts.GATE, experts.UP, experts.DOWN
        raw, loaded = experts.raw, experts.loaded
        w_hi = experts.hi + [m.sb(f"w_hi{c}", [P, CHUNK], F32R) for c in range(experts.EARLY, N_CHUNKS)]
        w_lo = experts.lo + [m.sb(f"w_lo{c}", [P, CHUNK], F32R) for c in range(experts.EARLY, N_CHUNKS)]
        x_rows, x_rows_p = m.sb("x_rows_sample", [CS, D]), m.sb("x_rows_prompt", [CP, D])
        xT = m.sb("xT_hi_lo", [P, KD, 2 * N], F32R)
        g2, u2, g, u = (m.sb(x, [P, 2, N]) for x in ("gate_rest", "up_rest", "gate", "up"))
        sg, h = m.sb("silu_gate", [P, 2, N]), m.sb("h", [P, 2, N])
        hT = m.sb("hT_hi_lo", [P, FT, 2 * N], F32R)
        y_s, y_p, y_p_rest = m.sb("y_sample_rows", [CS, D]), m.sb("y_prompt_rows", [CP, D]), m.sb("y_prompt_rest", [CP, D])
        gather_at = [m.sb(f"gather_at{q}", [P, 1], U32) for q in range(2)]
        scatter_at = [m.sb(f"scatter_at{q}", [P, 1], U32) for q in range(2)]
        gate_now = [m.sb(f"gate_now{q}", [P, 1]) for q in range(2)]
        carrier, zero = m.sb("d_wait_carrier", [P, 1]), m.sb("d_zero", [P, 1])

        ps_g, ps_u = m.ps("ps_gate"), m.ps("ps_up")
        ps_x = [m.ps(f"ps_xT{b}") for b in range(2)]
        ps_ys, ps_yp = m.ps("ps_y_sample", (P, D)), m.ps("ps_y_prompt", (P, D))
        ps_turn = [ps_x[0][:, :], ps_x[1][:, :], ps_yp[:, 0:512], ps_yp[:, 512:1024]]

        hi_done, lo_done = experts.hi_done, experts.lo_done
        first_down_used = m.sem("d_first_down_used")
        gathered = [m.sem(f"d_gathered{q}") for q in range(2)]
        scattered = [m.sem(f"d_scattered{q}") for q in range(2)]
        index_copied, lists_copied, zeroed, carried = m.sem("d_index_copied"), m.sem("d_lists_copied"), m.sem("d_zeroed"), m.sem("d_carried")
        x_turned, x_hi_done, x_lo_done = m.sem("d_x_turned"), m.sem("d_x_hi_done"), m.sem("d_x_lo_done")
        g_done, u_done, g2_copied, u2_copied, g_added, u_added = (
            m.sem("d_" + x) for x in ("g_done", "u_done", "g2_copied", "u2_copied", "g_added", "u_added"))
        silu_done, h_done, h_hi_done, h_lo_done = (m.sem("d_" + x) for x in ("silu_done", "h_done", "h_hi_done", "h_lo_done"))
        ys_done, yp_done, ys_scaled, yp_rest_scaled, yp_scaled = (
            m.sem("d_" + x) for x in ("ys_done", "yp_done", "ys_scaled", "yp_rest_scaled", "yp_scaled"))

        norm = OutputNorm(nc, m, dram, experts)
        block = ctx.enter_context(nc.Block())

        @block.sync
        def _(sp):
            for q in range(2):
                sp.wait_ge(gathered[q], 16)
            with sp.Fori(0, N_EXPERTS - 1) as e:
                for c in range(N_CHUNKS):
                    sp.wait_ge(lo_done, N_CHUNKS * e + c + 1)
                    experts.load(sp, e + 1, c)
            sp.wait_ge(lo_done, N_CHUNKS * N_EXPERTS)
            norm.load_constants(sp)
            sp.wait_ge(scattered[0], 16 * N_EXPERTS)
            for b in range(norm.SLOTS):
                norm.load(sp, 0, b)
            sp.wait_ge(scattered[1], 16 * N_EXPERTS)
            norm.load_and_store(sp)

        @block.gpsimd
        def _(pool):
            def pool_carrier():
                pool.tensor_tensor(carrier[:, :], zero[:, :], zero[:, :], ALU.add).then_inc(carried, 1)

            def copy_index(e):
                for q in range(2):
                    pool.tensor_copy(gather_at[q][:, :], route["token"][q][:, bass.ds(e, 1)]).then_inc(index_copied, 1)

            def gather(q, rows):
                n = rows.shape[0]
                pool.indirect_dma_start(rows[:, :], None, dram["x1"],
                                        bass.IndirectOffsetOnAxis(ap=gather_at[q][0:n, 0:1], axis=0)).then_inc(gathered[q], 16)

            def scatter_add(q, rows):
                n = rows.shape[0]
                pool.indirect_dma_start(dram["acc"], bass.IndirectOffsetOnAxis(ap=scatter_at[q][0:n, 0:1], axis=0),
                                        rows[:, :], None, compute_op=ALU.add).then_inc(scattered[q], 16)

            pool.memset(zero[:, :], 0.0).then_inc(zeroed, 1)
            copy_index(0)
            pool.wait_ge(zeroed, 1)
            pool.wait_ge(index_copied, 2)
            gather(0, x_rows)
            gather(1, x_rows_p)
            norm.fill(pool)

            def step(e, last=False):
                if not last:
                    pool.wait_ge(carried, 5 * e)
                    for q in range(2):
                        pool.wait_ge(gathered[q], 16 * e + 16)
                    pool_carrier()
                    copy_index(e + 1)
                    pool.wait_ge(carried, 5 * e + 1)
                    pool.wait_ge(index_copied, 2 * e + 4)
                    pool.wait_ge(x_turned, 4 * e + 4)
                    pool_carrier()
                    gather(0, x_rows)
                    gather(1, x_rows_p)
                pool.wait_ge(carried, 5 * e + (0 if last else 2))
                pool.wait_ge(ys_scaled, e)
                pool.wait_ge(yp_scaled, e)
                for q in range(2):
                    pool.wait_ge(scattered[q], 16 * e)
                pool_carrier()
                for q in range(2):
                    pool.tensor_copy(scatter_at[q][:, :], route["token"][q][:, bass.ds(e, 1)]).then_inc(lists_copied, 1)
                    pool.tensor_copy(gate_now[q][:, :], route["gate"][q][:, bass.ds(e, 1)]).then_inc(lists_copied, 1)
                pool.wait_ge(carried, 5 * e + (1 if last else 3))
                pool.wait_ge(lists_copied, 4 * e + 4)
                pool.wait_ge(ys_scaled, e + 1)
                pool_carrier()
                scatter_add(0, y_s)
                pool.wait_ge(carried, 5 * e + (2 if last else 4))
                pool.wait_ge(yp_scaled, e + 1)
                pool_carrier()
                scatter_add(1, y_p)

            with pool.Fori(0, N_EXPERTS - 1) as e:
                step(e)
            step(N_EXPERTS - 1, last=True)
            norm.deviations_and_sum(pool)

        @block.scalar
        def _(act):
            def split(e, c, reuse=True):
                act.wait_ge(loaded[c], 16 * e + 16)
                if reuse:
                    if c in GATE:
                        act.wait_ge(g_done, 4 * (e - 1) + c + 2)
                    elif c in UP:
                        act.wait_ge(u_done, 4 * (e - 1) + c + 1)
                    else:
                        act.wait_ge(first_down_used if c == DOWN[0] else yp_done, e)
                act.activation(w_hi[c][:, :], raw[:, c, :], ACT.Copy).then_inc(hi_done, 1)

            def round_x(e):
                for pair in range(4):
                    act.wait_ge(x_turned, 4 * e + pair + 1)
                    act.activation(xT[:, 2 * pair:2 * pair + 2, 0:N],
                                   ps_turn[pair][:, 0:2 * N].rearrange("p (k t) -> p k t", t=N), ACT.Copy).then_inc(x_hi_done, 1)

            def round_h(e, f):
                act.wait_ge(h_done, 4 * e + f + 1)
                act.activation(hT[:, f, 0:N], h[:, f % 2, :], ACT.Copy).then_inc(h_hi_done, 1)

            round_x(0)
            split(0, experts.EARLY, reuse=False)

            def step(e, first=False, last=False):
                for f in range(FT):
                    act.wait_ge(g_done, 4 * e + f + 1)
                    act.activation(g2[:, f % 2, :], ps_g[:, N:2 * N], ACT.Copy).then_inc(g2_copied, 1)
                    if f:
                        round_h(e, f - 1)
                    if f == 0:
                        split(e, 5, reuse=not first)
                    elif f < 3 and not last:
                        split(e + 1, f - 1)
                    act.wait_ge(g_added, 4 * e + f + 1)
                    act.activation(sg[:, f % 2, :], g[:, f % 2, :], ACT.Silu).then_inc(silu_done, 1)
                    act.wait_ge(u_done, 4 * e + f + 1)
                    act.activation(u2[:, f % 2, :], ps_u[:, N:2 * N], ACT.Copy).then_inc(u2_copied, 1)
                round_h(e, FT - 1)
                if not last:
                    round_x(e + 1)
                    split(e + 1, 2)
                    split(e + 1, 3)
                act.wait_ge(lists_copied, 4 * e + 4)
                act.wait_ge(scattered[0], 16 * e)
                act.wait_ge(ys_done, e + 1)
                act.activation(y_s[:, :], ps_ys[:, :], ACT.Copy, scale=gate_now[0][:, :]).then_inc(ys_scaled, 1)
                if not last:
                    split(e + 1, 4)
                act.wait_ge(yp_done, e + 1)
                act.activation(y_p_rest[:, :], ps_yp[CP:2 * CP, :], ACT.Copy, scale=gate_now[1][CP:2 * CP, :]).then_inc(yp_rest_scaled, 1)

            step(0, first=True)
            with act.Fori(1, N_EXPERTS - 1) as e:
                step(e)
            step(N_EXPERTS - 1, last=True)
            norm.centre(act)

        @block.vector
        def _(dve):
            def split(e, c):
                dve.wait_ge(hi_done, N_CHUNKS * e + c + 1)
                nc.vector.tensor_tensor(w_lo[c][:, :], raw[:, c, :], f32(w_hi[c][:, :]), ALU.subtract).then_inc(lo_done, 1)

            def rest_x(e):
                for pair in range(4):
                    dve.wait_ge(x_hi_done, 4 * e + pair + 1)
                    hi = f32(xT[:, 2 * pair:2 * pair + 2, 0:N])
                    nc.vector.tensor_tensor(xT[:, 2 * pair:2 * pair + 2, N:2 * N],
                                            ps_turn[pair][:, 0:2 * N].rearrange("p (k t) -> p k t", t=N), hi,
                                            ALU.subtract).then_inc(x_lo_done, 1)

            def rest_h(e, f):
                dve.wait_ge(h_hi_done, 4 * e + f + 1)
                for cols, at in ((slice(0, CS), N + CP), (slice(CS, N), N)):
                    n = cols.stop - cols.start
                    nc.vector.tensor_tensor(hT[:, f, at:at + n], h[:, f % 2, cols], f32(hT[:, f, cols]),
                                            ALU.subtract).then_inc(h_lo_done, 1)

            rest_x(0)

            def step(e, last=False):
                for f in range(FT):
                    dve.wait_ge(g2_copied, 4 * e + f + 1)
                    nc.vector.tensor_tensor(g[:, f % 2, :], ps_g[:, 0:N], g2[:, f % 2, :], ALU.add).then_inc(g_added, 1)
                    if f:
                        rest_h(e, f - 1)
                    if f < 2:
                        split(e, 4 + f)
                    elif f == 2 and not last:
                        split(e + 1, 0)
                    dve.wait_ge(u2_copied, 4 * e + f + 1)
                    nc.vector.tensor_tensor(u[:, f % 2, :], ps_u[:, 0:N], u2[:, f % 2, :], ALU.add).then_inc(u_added, 1)
                    dve.wait_ge(silu_done, 4 * e + f + 1)
                    dve.wait_ge(u_added, 4 * e + f + 1)
                    nc.vector.tensor_tensor(h[:, f % 2, :], sg[:, f % 2, :], u[:, f % 2, :], ALU.mult).then_inc(h_done, 1)
                rest_h(e, FT - 1)
                if not last:
                    rest_x(e + 1)
                    split(e + 1, 1)
                    split(e + 1, 2)
                    split(e + 1, 3)
                dve.wait_ge(scattered[1], 16 * e)
                dve.wait_ge(yp_rest_scaled, e + 1)
                nc.vector.scalar_tensor_tensor(out=y_p[:, :], in0=ps_yp[0:CP, :], scalar=gate_now[1][0:CP, :], in1=y_p_rest[:, :],
                                               op0=ALU.mult, op1=ALU.add).then_inc(yp_scaled, 1)

            with dve.Fori(0, N_EXPERTS - 1) as e:
                step(e)
            step(N_EXPERTS - 1, last=True)
            norm.statistics_and_product(dve)

        @block.tensor
        def _(pe):
            def turn_x(e, first=False):
                for q in range(2):
                    pe.wait_ge(gathered[q], 16 * e + 16)
                if not first:
                    pe.wait_ge(yp_scaled, e - 1)
                for pair in range(4):
                    for k in range(2):
                        src = slice((2 * pair + k) * P, (2 * pair + k + 1) * P)
                        nc.tensor.transpose(ps_turn[pair][:, k * N:k * N + CS], x_rows[:, src], ident[:, :])
                        last = nc.tensor.transpose(ps_turn[pair][:, k * N + CS:(k + 1) * N], x_rows_p[:, src], ident[0:CP, 0:CP])
                    last.then_inc(x_turned, 1)

            def gate_or_up(ps, chunk, f, done):
                for k in range(KD):
                    at = slice(k * HALF + f % 2 * P, k * HALF + (f % 2 + 1) * P)
                    if k == KD - 1:
                        nc.tensor.matmul(ps[:, 0:N], w_lo[chunk][:, at], xT[:, k, 0:N], start=False, stop=False)
                        last = nc.tensor.matmul(ps[:, 0:2 * N], w_hi[chunk][:, at], xT[:, k, :], start=False, stop=True)
                    else:
                        nc.tensor.matmul(ps[:, 0:2 * N], w_hi[chunk][:, at], xT[:, k, :], start=k == 0, stop=False)
                        nc.tensor.matmul(ps[:, 0:N], w_lo[chunk][:, at], xT[:, k, 0:N], start=False, stop=False)
                last.then_inc(done, 1)

            def gate_up(e):
                pe.wait_ge(x_lo_done, 4 * e + 4)
                for f in range(FT):
                    pe.wait_ge(lo_done, N_CHUNKS * e + GATE[f // 2] + 1)
                    pe.wait_ge(g_added, 4 * e + f)
                    gate_or_up(ps_g, GATE[f // 2], f, g_done)
                    pe.wait_ge(lo_done, N_CHUNKS * e + UP[f // 2] + 1)
                    pe.wait_ge(u_added, 4 * e + f)
                    gate_or_up(ps_u, UP[f // 2], f, u_done)

            def down(e, last_expert=False):
                pe.wait_ge(ys_scaled, e)
                hi = slice(0, CS)
                for f in range(FT):
                    pe.wait_ge(h_lo_done, 8 * e + 2 * f + 2)
                    pe.wait_ge(lo_done, N_CHUNKS * e + DOWN[f // 2] + 1)
                    c = DOWN[f // 2]
                    for half in range(2):
                        cols = slice(half * 512, (half + 1) * 512)
                        wd = slice(f % 2 * D + half * 512, f % 2 * D + (half + 1) * 512)
                        last = three_passes(nc, ps_ys[:, cols], hT[:, f, hi], hT[:, f, N + CP:2 * N], w_hi[c][:, wd], w_lo[c][:, wd],
                                            f == 0, f == FT - 1)
                last.then_inc(ys_done, 1)
                if not last_expert:
                    pe.wait_ge(x_lo_done, 4 * e + 8)
                for f in range(FT):
                    for half in range(2):
                        cols = slice(half * 512, (half + 1) * 512)
                        wd = slice(f % 2 * D + half * 512, f % 2 * D + (half + 1) * 512)
                        c = DOWN[f // 2]
                        nc.tensor.matmul(ps_yp[:, cols], hT[:, f, CS:CS + 2 * CP], w_hi[c][:, wd], start=f == 0, stop=False)
                        last = nc.tensor.matmul(ps_yp[:, cols], hT[:, f, CS:CS + 2 * CP], w_lo[c][:, wd], start=False, stop=f == FT - 1)
                    if f == 1:
                        last.then_inc(first_down_used, 1)
                last.then_inc(yp_done, 1)

            turn_x(0, first=True)
            with pe.Fori(0, N_EXPERTS - 1) as e:
                gate_up(e)
                turn_x(e + 1)
                down(e)
            gate_up(N_EXPERTS - 1)
            down(N_EXPERTS - 1, last_expert=True)


def constants():
    inv = (1.0 / (np.float32(10000.0) ** (np.arange(0, ROPE, 2, dtype=np.float32) / np.float32(ROPE)))).astype(np.float32)
    ang = (np.arange(S_SAMPLE, dtype=np.float32)[:, None] * inv[None, :]).astype(np.float64)
    cos, sin = np.cos(ang), np.sin(ang)
    by_tile = lambda a: np.ascontiguousarray(a.reshape(SAMPLE_TILES, P, ROPE).transpose(1, 0, 2), np.float32)
    q_table = np.concatenate([cos, cos, -sin, sin, np.ones((S_SAMPLE, NOPE))], axis=1).T * SCALE
    inv_count = np.zeros((len(POOL_WINDOWS), T), np.float32)
    for start, n in ((0, S_SAMPLE), (S_SAMPLE, S_PROMPT)):
        pos = np.arange(n)
        for g, w in enumerate(POOL_WINDOWS):
            count = np.clip(pos + w // 2 - 1, 0, n - 1) - np.clip(pos - w // 2, 0, n - 1) + 1
            inv_count[g, start:start + n] = 1.0 / count
    return {
        "rope_cos": by_tile(np.concatenate([cos, cos], axis=1)),
        "rope_sin": by_tile(np.concatenate([sin, -sin], axis=1)),
        "q_table": np.ascontiguousarray(q_table, np.float32),
        "inv_count": inv_count,
    }


INPUTS = {
    "x_sample": (S_SAMPLE, D), "x_prompt": (S_PROMPT, D), "ln_in_g": (D,), "ln_in_b": (D,),
    "w_in": (D, IN_DIM), "w_pool": (4, GROUP, GROUP), "pool_scale": (POOL_DIM,), "q_norm_g": (Q_RANK,),
    "w_uq": (Q_RANK, N_HEADS * QK), "kv_norm_g": (KV_RANK,), "w_ukv": (KV_RANK, N_HEADS * (NOPE + V_DIM)),
    "w_o": (D, D), "ln1_g": (D,), "ln1_b": (D,), "w_router": (D, N_EXPERTS),
    "w_gate": (N_EXPERTS, D, FFN), "w_up": (N_EXPERTS, D, FFN), "w_down": (N_EXPERTS, FFN, D),
    "ln2_g": (D,), "ln2_b": (D,),
}
SCRATCH = {
    "x0": (T, D), "uT": (POOL_DIM, T), "qT": (Q_RANK, T), "kvT": (KV_RANK, T), "krT": (P, T), "v": (T, 512), "dT": (POOL_DIM, T),
    "mixT": (D, T), "x1": (T, D), "acc": (T, D),
}


def build(nc, phases="ABCD"):
    dram = {}
    for name, shape in INPUTS.items():
        dram[name] = nc.dram_tensor("in_" + name, shape, F32, kind="ExternalInput").ap()
    for name, a in constants().items():
        dram[name] = nc.dram_tensor("in_" + name, a.shape, F32, kind="ExternalInput").ap()
    for name, shape in SCRATCH.items():
        dram[name] = nc.dram_tensor("scratch_" + name, shape, F32).ap()
    dram["y_prompt"] = nc.dram_tensor("y_prompt", (S_PROMPT, D), F32, kind="ExternalOutput").ap()
    dram["y_sample"] = nc.dram_tensor("y_sample", (S_SAMPLE, D), F32, kind="ExternalOutput").ap()
    with ExitStack() as ctx:
        m = Scope(nc, ctx)
        ident = m.sb("ident", [P, P])
        ident_zero = m.sem("ident_zero")
        with nc.Block() as block:
            @block.gpsimd
            def _(pool):
                pool.memset(ident[:, :], 0.0).then_inc(ident_zero, 1)
                pool.wait_ge(ident_zero, 1)
                pool.affine_select(out=ident[:, :], in_=ident[:, :], compare_op=ALU.not_equal, fill=1.0, base=0,
                                   pattern=[[-1, P]], channel_multiplier=1).then_inc(ident_zero, 1)
        if "A" in phases:
            phase_project(nc, ident, dram)
        if "B" in phases:
            phase_attention(nc, ident, dram)
        route = {"token": [m.sb(f"route_token{q}", [P, N_EXPERTS], U32) for q in range(2)],
                 "gate": [m.sb(f"route_gate{q}", [P, N_EXPERTS]) for q in range(2)]}
        experts = ExpertWeights(m, dram)
        if "C" in phases:
            phase_mix(nc, ident, dram, route, experts)
        if "D" in phases:
            phase_experts(nc, ident, dram, route, experts)


def kernel(**inputs):
    from concourse import bacc
    from concourse.bass_utils import run_bass_kernel_spmd

    nc = bacc.Bacc("TRN2", target_bir_lowering=False, num_devices=1)
    build(nc)
    arrays = {"in_" + name: np.ascontiguousarray(inputs[name]).reshape(shape) for name, shape in INPUTS.items()}
    arrays.update({"in_" + name: a for name, a in constants().items()})
    r = run_bass_kernel_spmd(nc, [arrays], core_ids=[0])
    out = r.results[0]
    return out["y_prompt"].reshape(1, S_PROMPT, D), out["y_sample"].reshape(1, S_SAMPLE, D)
```
